# Optimizing a Trainium2 kernel written in Bass

```python
import math
import jax, jax.numpy as jnp
from jax import lax
import numpy as np

D_MODEL = 1024
BATCH = 1
SEQ = 1024
DEPTH = 2

CTX_LEN = 256
GRID_W = 64
N_GROUPS = 4
N_HEADS_GROUP = 4
HEAD_DIM = D_MODEL // (N_GROUPS * N_HEADS_GROUP)
GROUP_WIDTH = N_HEADS_GROUP * HEAD_DIM
MIX_WIDTH = N_GROUPS * GROUP_WIDTH
ROPE_DIM = HEAD_DIM // 2
DIFF_QK_DIM = HEAD_DIM // 2
MLA_Q_LORA = D_MODEL // 4
MLA_KV_LORA = D_MODEL // 8
MLA_NOPE = HEAD_DIM
MLA_ROPE = ROPE_DIM
MLA_V = HEAD_DIM
MLSTM_CHUNK = 64
MLSTM_CONV = 3
NA_WIN_ROWS = 8
NA_WIN_COLS = 16
FFN_HIDDEN = 2816
FFN_CONV = 3
ROPE_BASE = 10000.0
NORM_EPS = 1e-6
ATTN_BLOCK = 128
IN_LAYOUT = (
    ('diff_q', N_HEADS_GROUP * 2 * DIFF_QK_DIM),
    ('diff_k', N_HEADS_GROUP * 2 * DIFF_QK_DIM),
    ('diff_v', N_HEADS_GROUP * HEAD_DIM),
    ('mla_cq', MLA_Q_LORA),
    ('mla_ckv', MLA_KV_LORA),
    ('mla_kr', MLA_ROPE),
    ('ml_q', GROUP_WIDTH),
    ('ml_k', GROUP_WIDTH),
    ('ml_v', GROUP_WIDTH),
    ('ml_o', GROUP_WIDTH),
    ('ml_i', 2 * N_HEADS_GROUP),
    ('ml_f', 2 * N_HEADS_GROUP),
    ('na_q', GROUP_WIDTH),
    ('na_k', GROUP_WIDTH),
    ('na_v', GROUP_WIDTH),
)
IN_WIDTH = sum(n for _, n in IN_LAYOUT)

kernel_name = 'hybrid_headgroup_diffusion_trunk'

def rmsnorm(x, g):
    xf = x.astype(jnp.float32)
    y = xf * lax.rsqrt(jnp.mean(xf * xf, axis=-1, keepdims=True) + NORM_EPS)
    return (y * g.astype(jnp.float32)).astype(x.dtype)

def split_cols(p):
    out, off = {}, 0
    for name, n in IN_LAYOUT:
        out[name] = p[..., off:off + n]
        off += n
    return out

def dwconv(x, w):
    k = w.shape[0]
    return lax.conv_general_dilated(x, w[:, None, :].astype(x.dtype), (1,), [(k // 2, k // 2)],
                                    dimension_numbers=('NWC', 'WIO', 'NWC'),
                                    feature_group_count=x.shape[-1])

def rope_tables(t_len):
    nf = ROPE_DIM // 4
    t = jnp.arange(t_len, dtype=jnp.int32)
    row = (t // GRID_W).astype(jnp.float32)
    col = (t % GRID_W).astype(jnp.float32)
    inv = ROPE_BASE ** (-jnp.arange(nf, dtype=jnp.float32) / nf)
    ar, ac = row[:, None] * inv, col[:, None] * inv
    return jnp.cos(ar), jnp.sin(ar), jnp.cos(ac), jnp.sin(ac)

def apply_axial_rope(t, rope):
    cr, sr, cc, sc = rope
    shp = (1, t.shape[1]) + (1,) * (t.ndim - 3) + (cr.shape[-1],)

    def rot(u, cos, sin):
        cos = cos.reshape(shp).astype(u.dtype)
        sin = sin.reshape(shp).astype(u.dtype)
        u1, u2 = jnp.split(u, 2, axis=-1)
        return jnp.concatenate([u1 * cos - u2 * sin, u1 * sin + u2 * cos], axis=-1)

    tr, tc = jnp.split(t, 2, axis=-1)
    return jnp.concatenate([rot(tr, cr, sr), rot(tc, cc, sc)], axis=-1)

def block_attention(q, k, v, map_w, scale):
    b, s_len, g, m, dk = q.shape
    blk = min(ATTN_BLOCK, s_len)
    qb = jnp.moveaxis(q.reshape(b, s_len // blk, blk, g, m, dk), 1, 0)
    w = map_w.astype(jnp.float32)

    def one(qi):
        s = jnp.einsum('bqgmd,bkgmd->bgmqk', qi, k, preferred_element_type=jnp.float32) * scale
        p = jnp.einsum('bgmqk,m->bgqk', jax.nn.softmax(s, axis=-1), w)
        return jnp.einsum('bgqk,bkgd->bqgd', p.astype(v.dtype), v)

    o = lax.map(one, qb)
    return jnp.moveaxis(o, 0, 1).reshape(b, s_len, g, v.shape[-1])

def diff_attention_mixer(cols, cols_c, g_q, g_k, lam_vec, g_out, lam_init, rope, need_ctx):
    H, dk = N_HEADS_GROUP, DIFF_QK_DIM

    def qk(t, g):
        return rmsnorm(t.reshape(t.shape[0], t.shape[1], H, 2, dk), g)

    def vals(t):
        return t.reshape(t.shape[0], t.shape[1], H, HEAD_DIM)

    q = apply_axial_rope(qk(cols['diff_q'], g_q), rope)
    k = apply_axial_rope(qk(cols['diff_k'], g_k), rope)
    kc, vc = qk(cols_c['diff_k'], g_k), vals(cols_c['diff_v'])
    lv = lam_vec.astype(jnp.float32)
    lam = jnp.exp(jnp.dot(lv[0], lv[1])) - jnp.exp(jnp.dot(lv[2], lv[3])) + lam_init
    map_w = jnp.stack([jnp.ones_like(lam), -lam])
    scale = dk ** -0.5

    def finish(o):
        o = rmsnorm(o, g_out) * (1.0 - lam_init)
        return o.reshape(o.shape[0], o.shape[1], H * HEAD_DIM)

    y = finish(block_attention(q, jnp.concatenate([k, kc], 1),
                               jnp.concatenate([vals(cols['diff_v']), vc], 1), map_w, scale))
    yc = finish(block_attention(qk(cols_c['diff_q'], g_q), kc, vc, map_w, scale)) if need_ctx else None
    return y, yc

def mla_mixer(cols, cols_c, g_cq, g_ckv, w_uq, w_ukv, g_q, g_k, rope, need_ctx):
    H = N_HEADS_GROUP

    def queries(c):
        q = rmsnorm(c['mla_cq'], g_cq) @ w_uq
        return rmsnorm(q.reshape(q.shape[0], q.shape[1], H, MLA_NOPE + MLA_ROPE), g_q)

    def keys_values(c):
        kv = rmsnorm(c['mla_ckv'], g_ckv) @ w_ukv
        kv = kv.reshape(kv.shape[0], kv.shape[1], H, MLA_NOPE + MLA_V)
        k_nope, v = kv[..., :MLA_NOPE], kv[..., MLA_NOPE:]
        k_rope = jnp.broadcast_to(c['mla_kr'][:, :, None, :], k_nope.shape[:3] + (MLA_ROPE,))
        return rmsnorm(jnp.concatenate([k_nope, k_rope], -1), g_k), v

    def rope_part(t):
        return jnp.concatenate([t[..., :MLA_NOPE], apply_axial_rope(t[..., MLA_NOPE:], rope)], -1)

    q = rope_part(queries(cols))
    k, v = keys_values(cols)
    k = rope_part(k)
    kc, vc = keys_values(cols_c)
    w1 = jnp.ones((1,), jnp.float32)
    scale = (MLA_NOPE + MLA_ROPE) ** -0.5
    o = block_attention(q[:, :, :, None], jnp.concatenate([k, kc], 1)[:, :, :, None],
                        jnp.concatenate([v, vc], 1), w1, scale)
    y = o.reshape(o.shape[0], o.shape[1], H * MLA_V)
    yc = None
    if need_ctx:
        oc = block_attention(queries(cols_c)[:, :, :, None], kc[:, :, :, None], vc, w1, scale)
        yc = oc.reshape(oc.shape[0], oc.shape[1], H * MLA_V)
    return y, yc

def mlstm_chunkwise(q, k, v, ig, lf, state0, want_out):
    b_, t_len, H, d = q.shape
    L = min(MLSTM_CHUNK, t_len)
    N = t_len // L

    def chunks(t):
        return jnp.moveaxis(t.reshape((b_, N, L) + t.shape[2:]), 3, 1)

    qc, kc, vc, igc, lfc = (chunks(t) for t in (q, k, v, ig, lf))
    b = jnp.cumsum(lfc, axis=-1)
    g = b[..., -1]
    a = g[..., None] - b + igc
    m_loc = jnp.max(a, axis=-1)
    w = jnp.exp(a - m_loc[..., None])
    c_loc = jnp.einsum('bhnl,bhnld,bhnle->bhnde', w, vc, kc)
    n_loc = jnp.einsum('bhnl,bhnle->bhne', w, kc)

    def step(carry, inp):
        c_s, n_s, m_s = carry
        g_j, ml_j, cl_j, nl_j = inp
        m_new = jnp.maximum(g_j + m_s, ml_j)
        a_old = jnp.exp(g_j + m_s - m_new)
        a_loc = jnp.exp(ml_j - m_new)
        c_new = a_old[..., None, None] * c_s + a_loc[..., None, None] * cl_j
        n_new = a_old[..., None] * n_s + a_loc[..., None] * nl_j
        return (c_new, n_new, m_new), (c_s, n_s, m_s)

    xs = tuple(jnp.moveaxis(t, 2, 0) for t in (g, m_loc, c_loc, n_loc))
    final, prev = lax.scan(step, state0, xs)
    if not want_out:
        return None, final
    c_prev, n_prev, m_prev = (jnp.moveaxis(t, 0, 2) for t in prev)
    tri = jnp.tril(jnp.ones((L, L), dtype=bool))
    dlog = jnp.where(tri, b[..., :, None] - b[..., None, :] + igc[..., None, :], -jnp.inf)
    inter = b + m_prev[..., None]
    m_t = jnp.maximum(jnp.max(dlog, axis=-1), inter)
    s = jnp.einsum('bhnld,bhnsd->bhnls', qc, kc) * jnp.exp(dlog - m_t[..., None])
    e = jnp.exp(inter - m_t)
    num = jnp.einsum('bhnls,bhnsd->bhnld', s, vc) + e[..., None] * jnp.einsum('bhnde,bhnle->bhnld', c_prev, qc)
    den = jnp.sum(s, axis=-1) + e * jnp.einsum('bhne,bhnle->bhnl', n_prev, qc)
    h = num / jnp.maximum(jnp.abs(den), jnp.exp(-m_t))[..., None]
    return jnp.moveaxis(h, 1, 3).reshape(b_, t_len, H, d), final

def mlstm_mixer(cols, cols_c, w_conv, b_i, b_f, g_out, need_ctx):
    H, d = N_HEADS_GROUP, HEAD_DIM
    f32 = jnp.float32

    def prep(c):
        bb, t_len = c['ml_q'].shape[:2]
        qk = jax.nn.silu(dwconv(jnp.concatenate([c['ml_q'], c['ml_k']], -1), w_conv))
        q, k = jnp.split(qk, 2, axis=-1)
        q = q.reshape(bb, t_len, H, d).astype(f32)
        k = k.reshape(bb, t_len, H, d).astype(f32) * (d ** -0.5)
        v = c['ml_v'].reshape(bb, t_len, H, d).astype(f32)
        ig = c['ml_i'].reshape(bb, t_len, 2, H).astype(f32) + b_i.astype(f32)
        lf = jax.nn.log_sigmoid(c['ml_f'].reshape(bb, t_len, 2, H).astype(f32) + b_f.astype(f32))
        return q, k, v, ig, lf

    lat, ctxp = prep(cols), prep(cols_c)
    bb = lat[0].shape[0]
    zero_state = (jnp.zeros((bb, H, d, d), f32), jnp.zeros((bb, H, d), f32), jnp.zeros((bb, H), f32))
    h_lat, h_ctx = [], []
    for direction in range(2):
        def order(t):
            return t[:, ::-1] if direction == 1 else t

        def seq(p):
            q, k, v, ig, lf = p
            return order(q), order(k), order(v), order(ig[:, :, direction]), order(lf[:, :, direction])

        hc, state_c = mlstm_chunkwise(*seq(ctxp), zero_state, need_ctx)
        hl, _ = mlstm_chunkwise(*seq(lat), state_c, True)
        h_lat.append(order(hl))
        if need_ctx:
            h_ctx.append(order(hc))

    def finish(h, c):
        o = jax.nn.sigmoid(c['ml_o'].astype(f32)).reshape(h.shape)
        y = (rmsnorm(h, g_out) * o).astype(c['ml_o'].dtype)
        return y.reshape(h.shape[0], h.shape[1], H * d)

    y = finish(h_lat[0] + h_lat[1], cols)
    yc = finish(h_ctx[0] + h_ctx[1], cols_c) if need_ctx else None
    return y, yc

def neighbourhood_mixer(cols, cols_c, g_q, g_k, rpb, need_ctx):
    H, d = N_HEADS_GROUP, HEAD_DIM

    def heads(t):
        return t.reshape(t.shape[0], t.shape[1], H, d)

    q = rmsnorm(heads(cols['na_q']), g_q)
    k = rmsnorm(heads(cols['na_k']), g_k)
    v = heads(cols['na_v'])
    kc = rmsnorm(heads(cols_c['na_k']), g_k)
    vc = heads(cols_c['na_v'])
    bb, s_len = q.shape[:2]
    W = GRID_W
    R = s_len // W
    wr = min(NA_WIN_ROWS, R)
    scale = d ** -0.5
    qg = q.reshape(bb, R, W, H, d)
    r = jnp.arange(R)
    ridx = jnp.clip(r - wr // 2, 0, R - wr)[:, None] + jnp.arange(wr)[None, :]
    kw = k.reshape(bb, R, W, H, d)[:, ridx]
    vw = v.reshape(bb, R, W, H, d)[:, ridx]
    cidx = jnp.arange(W)
    cs = jnp.clip(cidx - NA_WIN_COLS // 2, 0, W - NA_WIN_COLS)
    col_ok = (cidx[None, :] >= cs[:, None]) & (cidx[None, :] < cs[:, None] + NA_WIN_COLS)
    roff = ridx - r[:, None] + (NA_WIN_ROWS - 1)
    coff = jnp.clip(cidx[None, :] - cidx[:, None], 1 - NA_WIN_COLS, NA_WIN_COLS - 1) + (NA_WIN_COLS - 1)
    bias = rpb[:, roff[:, None, :, None], coff[None, :, None, :]]
    s_win = jnp.einsum('brqhd,brjkhd->bhrqjk', qg, kw, preferred_element_type=jnp.float32) * scale
    s_win = jnp.where(col_ok[:, None, :], s_win + bias[None].astype(jnp.float32), -jnp.inf)
    s_ctx = jnp.einsum('brqhd,bchd->bhrqc', qg, kc, preferred_element_type=jnp.float32) * scale
    p = jax.nn.softmax(jnp.concatenate([s_win.reshape(bb, H, R, W, wr * W), s_ctx], -1), axis=-1)
    p_win = p[..., :wr * W].reshape(bb, H, R, W, wr, W).astype(v.dtype)
    p_ctx = p[..., wr * W:].astype(v.dtype)
    o = jnp.einsum('bhrqjk,brjkhd->brqhd', p_win, vw) + jnp.einsum('bhrqc,bchd->brqhd', p_ctx, vc)
    y = o.reshape(bb, s_len, H * d)
    yc = None
    if need_ctx:
        qc = rmsnorm(heads(cols_c['na_q']), g_q)
        oc = block_attention(qc[:, :, :, None], kc[:, :, :, None], vc, jnp.ones((1,), jnp.float32), scale)
        yc = oc.reshape(oc.shape[0], oc.shape[1], H * d)
    return y, yc

def conv_ffn(h, w_up, w_conv, w_down):
    u = dwconv(h @ w_up, w_conv)
    a, g = jnp.split(u, 2, axis=-1)
    return (jax.nn.silu(g) * a) @ w_down

def setup_inputs(seed: int = 0) -> dict:
    key = jax.random.key(seed)
    ks = iter(jax.random.split(key, 40))
    L, D, H = DEPTH, D_MODEL, N_HEADS_GROUP

    def nrm(shape, s):
        return s * jax.random.normal(next(ks), shape, jnp.float32)

    def gain(shape):
        return 1.0 + nrm(shape, 0.1)

    return {
        'x': nrm((BATCH, SEQ, D), 1.0),
        'c': nrm((BATCH, D), 1.0),
        'ctx': nrm((BATCH, CTX_LEN, D), 1.0),
        'c_ctx': nrm((D,), 1.0),
        'w_mod': nrm((L, D, 6 * D), 0.5 * D ** -0.5),
        'b_mod': nrm((L, 6 * D), 0.02),
        'g_norm1': gain((L, D)),
        'g_norm2': gain((L, D)),
        'w_in': nrm((L, D, IN_WIDTH), D ** -0.5),
        'w_out': nrm((L, MIX_WIDTH, D), MIX_WIDTH ** -0.5),
        'diff_g_q': gain((L, DIFF_QK_DIM)),
        'diff_g_k': gain((L, DIFF_QK_DIM)),
        'diff_lam': nrm((L, 4, DIFF_QK_DIM), 0.1),
        'diff_g_out': gain((L, HEAD_DIM)),
        'mla_g_cq': gain((L, MLA_Q_LORA)),
        'mla_g_ckv': gain((L, MLA_KV_LORA)),
        'mla_w_uq': nrm((L, MLA_Q_LORA, H * (MLA_NOPE + MLA_ROPE)), MLA_Q_LORA ** -0.5),
        'mla_w_ukv': nrm((L, MLA_KV_LORA, H * (MLA_NOPE + MLA_V)), MLA_KV_LORA ** -0.5),
        'mla_g_q': gain((L, MLA_NOPE + MLA_ROPE)),
        'mla_g_k': gain((L, MLA_NOPE + MLA_ROPE)),
        'mlstm_w_conv': nrm((L, MLSTM_CONV, 2 * GROUP_WIDTH), MLSTM_CONV ** -0.5),
        'mlstm_b_i': nrm((L, 2, H), 0.1),
        'mlstm_b_f': jnp.linspace(3.0, 6.0, H, dtype=jnp.float32) + nrm((L, 2, H), 0.1),
        'mlstm_g_out': gain((L, HEAD_DIM)),
        'na_g_q': gain((L, HEAD_DIM)),
        'na_g_k': gain((L, HEAD_DIM)),
        'na_rpb': nrm((L, H, 2 * NA_WIN_ROWS - 1, 2 * NA_WIN_COLS - 1), 0.1),
        'ffn_w_up': nrm((L, D, 2 * FFN_HIDDEN), D ** -0.5),
        'ffn_w_conv': nrm((L, FFN_CONV, 2 * FFN_HIDDEN), FFN_CONV ** -0.5),
        'ffn_w_down': nrm((L, FFN_HIDDEN, D), FFN_HIDDEN ** -0.5),
    }

def reference(x, c, ctx, c_ctx, w_mod, b_mod, g_norm1, g_norm2, w_in, w_out,
              diff_g_q, diff_g_k, diff_lam, diff_g_out,
              mla_g_cq, mla_g_ckv, mla_w_uq, mla_w_ukv, mla_g_q, mla_g_k,
              mlstm_w_conv, mlstm_b_i, mlstm_b_f, mlstm_g_out,
              na_g_q, na_g_k, na_rpb, ffn_w_up, ffn_w_conv, ffn_w_down):
    rope = rope_tables(x.shape[1])
    xc = ctx
    for l in range(DEPTH):
        need_ctx = l < DEPTH - 1
        lam_init = 0.8 - 0.6 * math.exp(-0.3 * l)
        mod = jax.nn.silu(c) @ w_mod[l] + b_mod[l]
        mod_c = jax.nn.silu(c_ctx) @ w_mod[l] + b_mod[l]
        sh1, sc1, gt1, sh2, sc2, gt2 = jnp.split(mod[:, None, :], 6, axis=-1)
        csh1, csc1, cgt1, csh2, csc2, cgt2 = jnp.split(mod_c, 6, axis=-1)
        h = rmsnorm(x, g_norm1[l]) * (1.0 + sc1) + sh1
        hc = rmsnorm(xc, g_norm1[l]) * (1.0 + csc1) + csh1
        cols = split_cols(h @ w_in[l])
        cols_c = split_cols(hc @ w_in[l])
        y_diff, cy_diff = diff_attention_mixer(cols, cols_c, diff_g_q[l], diff_g_k[l], diff_lam[l],
                                               diff_g_out[l], lam_init, rope, need_ctx)
        y_mla, cy_mla = mla_mixer(cols, cols_c, mla_g_cq[l], mla_g_ckv[l], mla_w_uq[l], mla_w_ukv[l],
                                  mla_g_q[l], mla_g_k[l], rope, need_ctx)
        y_ml, cy_ml = mlstm_mixer(cols, cols_c, mlstm_w_conv[l], mlstm_b_i[l], mlstm_b_f[l],
                                  mlstm_g_out[l], need_ctx)
        y_na, cy_na = neighbourhood_mixer(cols, cols_c, na_g_q[l], na_g_k[l], na_rpb[l], need_ctx)
        x = x + gt1 * (jnp.concatenate([y_diff, y_mla, y_ml, y_na], axis=-1) @ w_out[l])
        h2 = rmsnorm(x, g_norm2[l]) * (1.0 + sc2) + sh2
        x = x + gt2 * conv_ffn(h2, ffn_w_up[l], ffn_w_conv[l], ffn_w_down[l])
        if need_ctx:
            xc = xc + cgt1 * (jnp.concatenate([cy_diff, cy_mla, cy_ml, cy_na], axis=-1) @ w_out[l])
            hc2 = rmsnorm(xc, g_norm2[l]) * (1.0 + csc2) + csh2
            xc = xc + cgt2 * conv_ffn(hc2, ffn_w_up[l], ffn_w_conv[l], ffn_w_down[l])
    return x


_drawn_inputs = setup_inputs


def setup_inputs(seed=0):
    import zlib

    import numpy as np

    out = dict(_drawn_inputs(seed))
    spreads = {}
    factors = {'g_norm1': 2.998,
     'diff_g_q': 8.0,
     'diff_g_k': 8.0,
     'diff_lam': 4.415,
     'diff_g_out': 3.271,
     'mla_g_cq': 8.0,
     'mla_g_ckv': 8.0,
     'mla_w_uq': 3.03,
     'mla_g_q': 8.0,
     'mla_g_k': 8.0,
     'mlstm_b_i': 43.766,
     'mlstm_g_out': 3.949,
     'na_g_q': 8.0,
     'na_g_k': 8.0,
     'na_rpb': 8.0}
    for name, (base, spread) in spreads.items():
        noise = np.random.default_rng([zlib.crc32(name.encode()), seed]).standard_normal(out[name].shape)
        drawn = base * np.exp(spread * noise) if base else spread * noise
        out[name] = __import__('jax').numpy.asarray(drawn.astype(out[name].dtype))
    for name, factor in factors.items():
        out[name] = (out[name] * factor).astype(out[name].dtype)
    return out
```

```python
import math
from contextlib import ExitStack

import numpy as np
import concourse.bass as bass
from concourse import mybir

F32 = mybir.dt.float32
ALU = mybir.AluOpType
ACT = mybir.ActivationFunctionType
AX = mybir.AxisListType.X

P = 128
D = 1024
DC = D // P
DEPTH = 2
SEQ = 1024
CTX = 256
T = SEQ + CTX
NT = T // P
LT = SEQ // P
H = 4
HD = 64
GW = H * HD
GRID_W = 64
DQK = 32
ROPE = 32
MQ = 256
MKV = 128
MD = 96
HID = 2816
HC = HID // P
WIN_R = 8
WIN_C = 16
NROW = SEQ // GRID_W
EPS = 1e-6
NEG = -1e30
BANK = 512

OFF = {}
_o = 0
for _n, _w in (("diff", 768), ("mla", 416), ("mlqk", 512), ("mlvo", 512), ("mlg", 16), ("na", 768)):
    OFF[_n] = _o
    _o += _w
IN_WIDTH = _o
BLOCKS = [(0, 512, 0), (512, 512, 0), (1024, 256, 1)]

V_BMOD, V_G1, V_G2, V_MCONV, V_GCQ, V_GCKV, V_N = 0, 48, 56, 64, 76, 78, 79
V_FCONV = V_N
V_TOTAL = V_N + 3 * 2 * HC
ROWS = {}
_o = 0
for _n, _w in (("diff_g_q", 32), ("diff_g_k", 32), ("diff_lam", 128), ("diff_g_out", 64), ("mla_g_q", 96),
               ("mla_g_k", 96), ("mlstm_g_out", 64), ("mlstm_b_i", 8), ("mlstm_b_f", 8), ("na_g_q", 64),
               ("na_g_k", 64)):
    ROWS[_n] = (_o, _w)
    _o += _w
ROWS_N = _o

C_ID, C_REV, C_CUM, C_CUMR, C_E127, C_MASK0, C_MASK1, C_COS, C_SIN, C_COL, C_ROW = (
    0, 128, 256, 384, 512, 640, 768, 896, 896 + 256, 896 + 512, 896 + 512 + 64)
C_N = C_ROW + 8 * 10
NSLOT = 18


def window_start(j):
    return min(max(j - 2, 0), LT - 5)


def shape_constants():
    c = np.zeros((P, C_N), np.float32)
    i = np.arange(P)
    c[:, C_ID:C_ID + P] = np.eye(P)
    c[:, C_REV:C_REV + P] = np.eye(P)[::-1]
    c[:, C_CUM:C_CUM + P] = i[:, None] <= i[None, :]
    c[:, C_CUMR:C_CUMR + P] = i[:, None] >= i[None, :]
    c[P - 1, C_E127:C_E127 + P] = 1.0
    c[:, C_MASK0:C_MASK0 + P] = np.where(i[:, None] <= i[None, :], 0.0, NEG)
    c[:, C_MASK1:C_MASK1 + P] = np.where(i[:, None] >= i[None, :], 0.0, NEG)
    nf = ROPE // 4
    t = np.arange(SEQ)
    inv = (10000.0 ** (-np.arange(nf, dtype=np.float32) / nf)).astype(np.float32)
    ar = (t // GRID_W).astype(np.float32)[:, None] * inv
    ac = (t % GRID_W).astype(np.float32)[:, None] * inv
    cos = np.concatenate([np.cos(ar), np.cos(ar), np.cos(ac), np.cos(ac)], 1)
    sin = np.concatenate([-np.sin(ar), np.sin(ar), -np.sin(ac), np.sin(ac)], 1)
    c[:, C_COS:C_COS + 256] = cos.reshape(LT, P, 32).transpose(1, 0, 2).reshape(P, 256)
    c[:, C_SIN:C_SIN + 256] = sin.reshape(LT, P, 32).transpose(1, 0, 2).reshape(P, 256)
    q = i % GRID_W
    cs = np.clip(q - WIN_C // 2, 0, GRID_W - WIN_C)
    k = np.arange(GRID_W)
    c[:, C_COL:C_COL + 64] = np.where((k[None] >= cs[:, None]) & (k[None] < cs[:, None] + WIN_C), 0.0, NEG)
    for j in range(LT):
        row = 2 * j + i // GRID_W
        rs = np.clip(row - WIN_R // 2, 0, NROW - WIN_R)
        kr = 2 * window_start(j) + np.arange(10)
        ok = (kr[None] >= rs[:, None]) & (kr[None] < rs[:, None] + WIN_R)
        c[:, C_ROW + 10 * j:C_ROW + 10 * j + 10] = np.where(ok, 0.0, NEG)
    return c


class Chain:

    def __init__(self, eng, sem):
        self.eng, self.sem, self.n = eng, sem, 0

    def then(self, ins):
        self.n += 1
        ins.then_inc(self.sem, 1)
        return self.n

    def wait(self, n=None):
        self.eng.wait_ge(self.sem, self.n if n is None else n)


def build(nc, a, out):
    ctx = ExitStack()
    with ctx:
        _build(nc, a, out, ctx)


def _build(nc, a, out, ctx):
    def sb(name, shape, stack=ctx):
        return stack.enter_context(nc.sbuf_tensor(name, shape, F32))

    in_use = []

    def sem(name):
        in_use.append(nc.alloc_semaphore(name=name))
        return in_use[-1]

    def clear_semaphores():
        nc.clear_and_free_semaphores(in_use)
        in_use.clear()
        nc.all_engine_barrier()

    cst = sb("cst", [P, C_N])
    ones = sb("ones", [P, P])
    vec = sb("vec", [P, DEPTH, V_TOTAL])
    rows = sb("rows", [P, DEPTH, ROWS_N])
    mod = sb("mod", [P, 48, 2])
    scl = sb("scl", [P, 2, DC, 2])
    cc = sb("cc", [P, DC, 2])
    neglam = sb("neglam", [P, 2])
    half = sb("half", [P, 16])
    ps = ctx.enter_context(nc.psum_tensor("ps", [P, 8 * BANK], F32))
    rpb_pad = nc.dram_tensor("rpb_pad", [DEPTH, H, NSLOT + 1, 127], F32).ap()

    ident = cst[:, C_ID:C_ID + P]
    xT = sb("xT", [P, DC, T])

    def bank(b, n=BANK, w=0):
        return ps[:, b * BANK + w:b * BANK + w + n]

    def entry():
        st = ExitStack()
        with st:
            xin = sb("xin", [P, NT, D], st)
            vrows = sb("vrows", [P, 2, 3, P], st)
            craw = sb("craw", [P, DC, 2], st)
            padz = sb("padz", [P, H, 127], st)
            s_x = [sem(f"x_loaded{i}") for i in range(2)]
            s_c = sem("constants_loaded")
            s_c2 = sem("rows_loaded")
            s_r = sem("rpb_loaded")
            s_rd = sem("rpb_written")
            s_ones = sem("ones_set")
            s_zero = sem("pad_zeroed")
            s_turn = sem("x_turned")
            s_kept = sem("x_kept")
            s_vt = sem("vectors_turned")
            s_vk = sem("vectors_kept")
            s_silu = sem("cond_ready")
            s_rows = sem("rows_scaled")
            s_lam = sem("lam_sums")
            with nc.Block() as block:
                @block.sync
                def _(sp):
                    sp.dma_start(cst[:, :], a["consts"]).then_inc(s_c, 16)
                    sp.dma_start(xin[:, 0:4, :], a["x"][0].rearrange("(t p) d -> p t d", p=P)[:, 0:4, :]).then_inc(s_x[0], 16)
                    sp.dma_start(xin[:, 4:8, :], a["x"][0].rearrange("(t p) d -> p t d", p=P)[:, 4:8, :]).then_inc(s_x[1], 16)
                    sp.dma_start(xin[:, 8:10, :], a["ctx"][0].rearrange("(t p) d -> p t d", p=P)).then_inc(s_x[1], 16)
                    sp.wait_ge(s_zero, 1)
                    for l in range(DEPTH):
                        sp.dma_start(padz[64 * l + 2:64 * l + 2 + 2 * WIN_R - 1, :, 48:79],
                                     a["na_rpb"][l].rearrange("h s w -> s h w")).then_inc(s_r, 16)
                    sp.wait_ge(s_r, 16 * DEPTH)
                    for l in range(DEPTH):
                        sp.dma_start(rpb_pad[l].rearrange("h s w -> s h w"),
                                     padz[64 * l:64 * l + NSLOT + 1, :, :]).then_inc(s_rd, 16)
                    sp.wait_ge(s_rd, 16 * DEPTH)

                @block.gpsimd
                def _(pool):
                    nc.gpsimd.memset(padz[:, :, :], 0.0).then_inc(s_zero, 1)
                    nc.gpsimd.memset(half[:, :], -0.5)
                    nc.gpsimd.memset(ones[:, :], 1.0).then_inc(s_ones, 1)

                @block.scalar
                def _(act):
                    n = 0
                    for l in range(DEPTH):
                        parts = [(a["b_mod"][l].rearrange("(r p) -> r p", p=P), 0, 48, 0),
                                 (a["g_norm1"][l].rearrange("(r p) -> r p", p=P), V_G1, 8, 0),
                                 (a["g_norm2"][l].rearrange("(r p) -> r p", p=P), V_G2, 8, 0),
                                 (a["mlstm_w_conv"][l].rearrange("k (r p) -> (k r) p", p=P), V_MCONV, 12, 0),
                                 (a["mla_g_cq"][l].rearrange("(r p) -> r p", p=P), V_GCQ, 2, 0),
                                 (a["mla_g_ckv"][l].rearrange("(r p) -> r p", p=P), V_GCKV, 1, 0),
                                 (a["ffn_w_conv"][l].rearrange("k (r p) -> (k r) p", p=P)[0:66], 0, 66, 1),
                                 (a["ffn_w_conv"][l].rearrange("k (r p) -> (k r) p", p=P)[66:132], 0, 66, 2)]
                        for src, r0, nr, j in parts:
                            act.dma_start(vrows[r0:r0 + nr, l, j, :], src).then_inc(s_c, 16)
                            n += 1
                        for name, (o, w) in ROWS.items():
                            src = a[name][l]
                            if len(src.shape) == 2:
                                src = src.rearrange("a b -> (a b)")
                            act.dma_start(rows[:, l, o:o + w], src.partition_broadcast(P)).then_inc(s_c2, 16)
                    act.dma_start(craw[:, :, 0], a["c"][0].rearrange("(c p) -> p c", p=P),
                                  allow_slow_non_contiguous=True).then_inc(s_c2, 16)
                    act.dma_start(craw[:, :, 1], a["c_ctx"].rearrange("(c p) -> p c", p=P),
                                  allow_slow_non_contiguous=True).then_inc(s_c2, 16)
                    act.wait_ge(s_c2, 16 * (DEPTH * len(ROWS) + 2))
                    nc.scalar.activation(cc[:, :, :], craw[:, :, :], ACT.Silu).then_inc(s_silu, 1)
                    act.wait_ge(s_silu, 1)

                @block.tensor
                def _(pe):
                    pe.wait_ge(s_c, 16 * (1 + 8 * DEPTH))
                    for l in range(DEPTH):
                        if l >= 1:
                            pe.wait_ge(s_vk, 3 * l)
                        for j, (nr, b) in enumerate(((V_N, 0), (66, 1), (66, 2))):
                            mm = nc.tensor.transpose(bank(b, nr), vrows[0:nr, l, j, :], ident[0:nr, 0:nr])
                        mm.then_inc(s_vt, 1)
                    n = 0
                    for t in range(NT):
                        if t == 0:
                            pe.wait_ge(s_x[0], 16)
                        if t == 4:
                            pe.wait_ge(s_x[1], 32)
                        for g in range(2):
                            if n >= 4:
                                pe.wait_ge(s_kept, n - 3)
                            for c in range(4):
                                mm = nc.tensor.transpose(bank(4 + n % 4, P, c * P), xin[:, t, (4 * g + c) * P:(4 * g + c + 1) * P], ident)
                            mm.then_inc(s_turn, 1)
                            n += 1

                @block.vector
                def _(dve):
                    for l in range(DEPTH):
                        dve.wait_ge(s_vt, l + 1)
                        for j, (nr, o) in enumerate(((V_N, 0), (66, V_N), (66, V_N + 66))):
                            nc.vector.tensor_copy(vec[:, l, o:o + nr], bank(j, nr)).then_inc(s_vk, 1)
                    n = 0
                    for t in range(NT):
                        for g in range(2):
                            dve.wait_ge(s_turn, n + 1)
                            nc.vector.tensor_copy(xT[:, 4 * g:4 * g + 4, t * P:(t + 1) * P],
                                                  bank(4 + n % 4).rearrange("p (c t) -> p c t", c=4)).then_inc(s_kept, 1)
                            n += 1
                    dve.wait_ge(s_c2, 16 * (DEPTH * len(ROWS) + 2))
                    for l in range(DEPTH):
                        lam0 = 0.8 - 0.6 * math.exp(-0.3 * l)
                        for name, f in (("diff_g_q", DQK ** -0.5), ("diff_g_out", 1.0 - lam0),
                                        ("mla_g_q", MD ** -0.5), ("na_g_q", HD ** -0.5)):
                            o, w = ROWS[name]
                            nc.vector.tensor_scalar(rows[:, l, o:o + w], rows[:, l, o:o + w], f, None, ALU.mult).then_inc(s_rows, 1)
                    dve.wait_ge(s_rows, 8)
            return

    entry()
    clear_semaphores()
    hT = sb("hT", [P, DC, T])

    def modulation(l):
        st = ExitStack()
        with st:
            wm = [sb(f"wm{i}_{l}", [P, DC, 512], st) for i in range(2)]
            lv = sb(f"lv{l}", [P, 2, 32], st)
            ls = sb(f"ls{l}", [P, 2], st)
            w_in = [sem(f"mod_w{i}_{l}") for i in range(2)]
            w_used = sem(f"mod_w_used{l}")
            done = sem(f"mod_kept{l}")
            lam = sem(f"lam{l}")
            lame = sem(f"lame{l}")
            w = a["w_mod"][l].rearrange("(c p) n -> p c n", p=P)
            with nc.Block() as block:
                @block.sync
                def _(sp):
                    for i in range(2):
                        sp.dma_start(wm[i][:, :, :], w[:, :, i * 512:(i + 1) * 512]).then_inc(w_in[i], 16)
                    with sp.Fori(0, 5) as n:
                        for i in range(2):
                            sp.wait_ge(w_used, n * 2 + (i + 1))
                            sp.dma_start(wm[i][:, :, :], w[:, :, bass.ds(n * 1024 + (1024 + 512 * i), 512)]).then_inc(w_in[i], 16)

                @block.tensor
                def _(pe):
                    with pe.Fori(0, 6) as n:
                        for i in range(2):
                            pe.wait_ge(w_in[i], n * 16 + 16)
                            pe.wait_ge(done, n * 2 + (i + 1))
                            for f in range(4):
                                for c in range(DC):
                                    mm = nc.tensor.matmul(bank(i, 2, 2 * f), wm[i][:, c, f * P:(f + 1) * P], cc[:, c, :],
                                                          start=(c == 0), stop=(c == DC - 1))
                            mm.then_inc(w_used, 1)

                @block.vector
                def _(dve):
                    dve.sem_inc(done, 2)
                    with dve.Fori(0, 6) as n:
                        for i in range(2):
                            dve.wait_ge(w_used, n * 2 + (i + 1))
                            b = vec[:, l, bass.ds(n * 8 + 4 * i, 4)].unsqueeze(2).broadcast_to([P, 4, 2])
                            nc.vector.tensor_tensor(mod[:, bass.ds(n * 8 + 4 * i, 4), :],
                                                    bank(i, 8).rearrange("p (f s) -> p f s", s=2), b, ALU.add).then_inc(done, 1)
                    dve.wait_ge(done, 14)
                    for k, (sc, g) in enumerate(((8, V_G1), (32, V_G2))):
                        gb = vec[:, l, g:g + DC].unsqueeze(2).broadcast_to([P, DC, 2])
                        nc.vector.scalar_tensor_tensor(out=scl[:, k, :, :], in0=mod[:, sc:sc + DC, :], scalar=1.0, in1=gb,
                                                       op0=ALU.add, op1=ALU.mult).then_inc(done, 1)
                    o, _w = ROWS["diff_lam"]
                    v = rows[:, l, o:o + 128].rearrange("p (a b d) -> p a b d", a=2, b=2)
                    nc.vector.tensor_tensor(lv[:, :, :], v[:, :, 0, :], v[:, :, 1, :], ALU.mult).then_inc(lam, 1)
                    dve.wait_ge(lam, 1)
                    nc.vector.tensor_reduce(ls[:, :], lv[:, :, :], AX, ALU.add).then_inc(lam, 1)
                    dve.wait_ge(lame, 1)
                    nc.vector.scalar_tensor_tensor(out=neglam[:, 0:1], in0=ls[:, 1:2], scalar=-(0.8 - 0.6 * math.exp(-0.3 * l)),
                                                   in1=ls[:, 0:1], op0=ALU.add, op1=ALU.subtract).then_inc(lam, 1)
                    dve.wait_ge(lam, 3)

                @block.scalar
                def _(act):
                    act.wait_ge(lam, 2)
                    nc.scalar.activation(ls[:, :], ls[:, :], ACT.Exp).then_inc(lame, 1)

    def norm(l, k, blocks):
        st = ExitStack()
        with st:
            sq = [sb(f"sq{i}_{l}{k}", [P, DC, 512], st) for i in range(2)]
            rs = [sb(f"rs{i}_{l}{k}", [P, 512], st) for i in range(2)]
            squared = sem(f"squared{l}{k}")
            summed = sem(f"summed{l}{k}")
            mean = sem(f"mean{l}{k}")
            root = sem(f"root{l}{k}")
            inv = sem(f"inv{l}{k}")
            normed = sem(f"normed{l}{k}")
            ready = sem(f"h_ready{l}{k}")
            sh = 24 * k
            with nc.Block() as block:
                @block.tensor
                def _(pe):
                    for i, (t0, n, s) in enumerate(blocks):
                        for c in range(DC):
                            pe.wait_ge(squared, DC * i + c + 1)
                            mm = nc.tensor.matmul(bank(i, n), ones[:, :], sq[i % 2][:, c, 0:n], start=(c == 0), stop=(c == DC - 1))
                        mm.then_inc(summed, 1)

                @block.scalar
                def _(act):
                    def squares(i):
                        t0, n, s = blocks[i]
                        if i >= 2:
                            act.wait_ge(summed, i - 1)
                        for c in range(DC):
                            nc.scalar.activation(sq[i % 2][:, c, 0:n], xT[:, c, t0:t0 + n], ACT.Square).then_inc(squared, 1)
                    squares(0)
                    for i, (t0, n, s) in enumerate(blocks):
                        if i + 1 < len(blocks):
                            squares(i + 1)
                        act.wait_ge(mean, i + 1)
                        nc.scalar.activation(rs[i % 2][:, 0:n], rs[i % 2][:, 0:n], ACT.Sqrt).then_inc(root, 1)
                        for c in range(DC):
                            act.wait_ge(normed, DC * i + c + 1)
                            nc.scalar.activation(hT[:, c, t0:t0 + n], hT[:, c, t0:t0 + n], ACT.Identity,
                                                 bias=mod[:, sh + c, s:s + 1], scale=scl[:, k, c, s:s + 1]).then_inc(ready, 1)

                @block.vector
                def _(dve):
                    for i, (t0, n, s) in enumerate(blocks):
                        dve.wait_ge(summed, i + 1)
                        if i >= 2:
                            dve.wait_ge(normed, DC * (i - 1))
                        nc.vector.tensor_scalar(rs[i % 2][:, 0:n], bank(i, n), 1.0 / D, EPS, ALU.mult, ALU.add).then_inc(mean, 1)
                        dve.wait_ge(root, i + 1)
                        nc.vector.reciprocal(rs[i % 2][:, 0:n], rs[i % 2][:, 0:n]).then_inc(inv, 1)
                        dve.wait_ge(inv, i + 1)
                        for c in range(DC):
                            nc.vector.tensor_tensor(hT[:, c, t0:t0 + n], xT[:, c, t0:t0 + n], rs[i % 2][:, 0:n],
                                                    ALU.mult).then_inc(normed, 1)

    def add_product(tag, l, w, kc, src, gate, blocks):
        st = ExitStack()
        with st:
            wb = [sb(f"wb{i}_{tag}", [P, kc, P], st) for i in range(2)]
            loaded = [sem(f"w_loaded{i}_{tag}") for i in range(2)]
            multiplied = sem(f"multiplied_{tag}")
            added = sem(f"added_{tag}")
            nb = len(blocks)
            wv = w.rearrange("(k p) n -> p k n", p=P)
            with nc.Block() as block:
                @block.sync
                def _(sp):
                    for i in range(2):
                        sp.dma_start(wb[i][:, :, :], wv[:, :, i * P:(i + 1) * P]).then_inc(loaded[i], 16)
                    with sp.Fori(0, DC // 2 - 1) as n:
                        for i in range(2):
                            sp.wait_ge(multiplied, n * (2 * nb) + nb * (i + 1))
                            sp.dma_start(wb[i][:, :, :], wv[:, :, bass.ds(n * (2 * P) + (2 + i) * P, P)]).then_inc(loaded[i], 16)

                @block.tensor
                def _(pe):
                    with pe.Fori(0, DC // 2) as n:
                        for i in range(2):
                            pe.wait_ge(loaded[i], n * 16 + 16)
                            for j, (t0, m, s) in enumerate(blocks):
                                pe.wait_ge(added, n * (2 * nb) + (nb * i + j + 1))
                                for k in range(kc):
                                    mm = nc.tensor.matmul(bank(3 * i + j, m), wb[i][:, k, :], src[:, k, t0:t0 + m],
                                                          start=(k == 0), stop=(k == kc - 1))
                                mm.then_inc(multiplied, 1)

                @block.vector
                def _(dve):
                    dve.sem_inc(added, 2 * nb)
                    with dve.Fori(0, DC // 2) as n:
                        for i in range(2):
                            for j, (t0, m, s) in enumerate(blocks):
                                dve.wait_ge(multiplied, n * (2 * nb) + (nb * i + j + 1))
                                x = xT[:, bass.ds(n * 2 + i, 1), t0:t0 + m]
                                nc.vector.scalar_tensor_tensor(out=x, in0=bank(3 * i + j, m).unsqueeze(1),
                                                               scalar=mod[:, bass.ds(n * 2 + (gate + i), 1), s],
                                                               in1=x, op0=ALU.mult, op1=ALU.add).then_inc(added, 1)

    def ffn(l, blocks):
        per = HC // 2
        st = ExitStack()
        with st:
            act_buf = sb(f"acts{l}", [P, per, T], st)
            for g in range(2):
                ffn_up(l, g, per, act_buf, blocks)
                add_product(f"down{l}{g}", l, a["ffn_w_down"][l][g * per * P:(g + 1) * per * P, :], per, act_buf, 40, blocks)

    def ffn_up(l, g, per, act_buf, blocks):
        st = ExitStack()
        ctx_too = len(blocks) == 3
        width = T + 4
        span = (T + 2) if ctx_too else SEQ
        with st:
            tag = f"{l}{g}"
            wu = [sb(f"wu{i}_{tag}", [P, DC, P], st) for i in range(2)]
            u = [sb(f"u{i}_{tag}", [P, width], st) for i in range(2)]
            cv = [sb(f"cv{i}_{tag}", [P, width], st) for i in range(2)]
            loaded = [sem(f"up_loaded{i}_{tag}") for i in range(2)]
            multiplied = [sem(f"up_mult{i}_{tag}") for i in range(2)]
            copied = [sem(f"up_copied{i}_{tag}") for i in range(2)]
            zeroed = sem(f"up_zeroed_{tag}")
            tap0 = [sem(f"tap0_{i}_{tag}") for i in range(2)]
            tap1 = [sem(f"tap1_{i}_{tag}") for i in range(2)]
            conv = [sem(f"conv{i}_{tag}") for i in range(2)]
            silu = sem(f"silu_{tag}")
            gated = sem(f"gated_{tag}")
            wv = a["ffn_w_up"][l].rearrange("(c p) n -> p c n", p=P)
            nb = len(blocks)
            with nc.Block() as block:
                @block.sync
                def _(sp):
                    for i in range(2):
                        c0 = i * HID + g * per * P
                        sp.dma_start(wu[i][:, :, :], wv[:, :, c0:c0 + P]).then_inc(loaded[i], 16)
                    with sp.Fori(0, per - 1) as n:
                        for i in range(2):
                            sp.wait_ge(multiplied[i], n + 1)
                            sp.dma_start(wu[i][:, :, :], wv[:, :, bass.ds(n * P + (i * HID + (g * per + 1) * P), P)]).then_inc(loaded[i], 16)

                @block.tensor
                def _(pe):
                    with pe.Fori(0, per) as n:
                        for i in range(2):
                            pe.wait_ge(loaded[i], n * 16 + 16)
                            pe.wait_ge(copied[i], n * 2 + 1)
                            for j, (t0, m, s) in enumerate(blocks):
                                for c in range(DC):
                                    mm = nc.tensor.matmul(bank(3 * i + j, m), wu[i][:, c, :], hT[:, c, t0:t0 + m],
                                                          start=(c == 0), stop=(c == DC - 1))
                            mm.then_inc(multiplied[i], 1)

                @block.scalar
                def _(act):
                    def leave_banks(i, n):
                        act.wait_ge(multiplied[i], n + 1)
                        act.wait_ge(conv[i], n + 1)
                        nc.scalar.activation(u[i][:, 1:1 + SEQ], bank(3 * i, SEQ), ACT.Copy).then_inc(copied[i], 1)
                        src = bank(3 * i + 2, CTX) if ctx_too else bank(3 * i + 1, 1, 511)
                        dst = u[i][:, SEQ + 3:SEQ + 3 + CTX] if ctx_too else cv[i][:, width - 1:width]
                        nc.scalar.activation(dst, src, ACT.Copy).then_inc(copied[i], 1)
                    act.wait_ge(zeroed, 2)
                    for i in range(2):
                        act.sem_inc(copied[i], 1)
                    with act.Fori(0, per) as n:
                        leave_banks(0, n)
                        leave_banks(1, n)
                        act.wait_ge(conv[1], n + 2)
                        nc.scalar.activation(cv[1][:, 0:span], cv[1][:, 0:span], ACT.Silu).then_inc(silu, 1)

                @block.gpsimd
                def _(pool):
                    nc.gpsimd.memset(u[0][:, :], 0.0).then_inc(zeroed, 1)
                    nc.gpsimd.memset(u[1][:, :], 0.0).then_inc(zeroed, 1)

                @block.vector
                def _(dve):
                    for i in range(2):
                        dve.sem_inc(conv[i], 1)
                    dve.sem_inc(gated, 1)
                    with dve.Fori(0, per) as n:
                        for i in range(2):
                            def w(k):
                                return vec[:, l, bass.ds(n + (V_FCONV + k * 2 * HC + i * HC + g * per), 1)]
                            dve.wait_ge(copied[i], n * 2 + 3)
                            if i == 0:
                                dve.wait_ge(gated, n * nb + 1)
                            nc.vector.tensor_scalar(cv[i][:, 0:span], u[i][:, 0:span], w(0), None, ALU.mult).then_inc(tap0[i], 1)
                            dve.wait_ge(tap0[i], n + 1)
                            nc.vector.scalar_tensor_tensor(out=cv[i][:, 0:span], in0=u[i][:, 1:1 + span], scalar=w(1),
                                                           in1=cv[i][:, 0:span], op0=ALU.mult, op1=ALU.add).then_inc(tap1[i], 1)
                            dve.wait_ge(tap1[i], n + 1)
                            nc.vector.scalar_tensor_tensor(out=cv[i][:, 0:span], in0=u[i][:, 2:2 + span], scalar=w(2),
                                                           in1=cv[i][:, 0:span], op0=ALU.mult, op1=ALU.add).then_inc(conv[i], 1)
                        dve.wait_ge(silu, n + 1)
                        for t0, m, s in blocks:
                            o = t0 + 2 * s
                            nc.vector.tensor_tensor(act_buf[:, bass.ds(n, 1), t0:t0 + m], cv[0][:, o:o + m].unsqueeze(1),
                                                    cv[1][:, o:o + m].unsqueeze(1), ALU.mult).then_inc(gated, 1)

    def leave():
        st = ExitStack()
        with st:
            xo = [sb(f"xo{i}", [P, D], st) for i in range(4)]
            turned = sem("out_turned")
            kept = sem("out_kept")
            stored = [sem(f"out_stored{i}") for i in range(4)]
            with nc.Block() as block:
                @block.tensor
                def _(pe):
                    n = 0
                    for t in range(LT):
                        for g in range(2):
                            if n >= 8:
                                pe.wait_ge(kept, n - 7)
                            for c in range(4):
                                mm = nc.tensor.transpose(bank(n % 8, P, c * P), xT[:, 4 * g + c, t * P:(t + 1) * P], ident)
                            mm.then_inc(turned, 1)
                            n += 1

                @block.vector
                def _(dve):
                    for n in range(2 * LT):
                        dve.wait_ge(turned, n + 1)
                        if n >= 8 and n % 2 == 0:
                            dve.wait_ge(stored[(n // 2) % 4], 16 * (n // 8))
                        nc.vector.tensor_copy(xo[(n // 2) % 4][:, (n % 2) * 512:(n % 2) * 512 + 512], bank(n % 8)).then_inc(kept, 1)

                @block.sync
                def _(sp):
                    for t in range(LT):
                        sp.wait_ge(kept, 2 * t + 2)
                        sp.dma_start(out[0, t * P:(t + 1) * P, :], xo[t % 4][:, :]).then_inc(stored[t % 4], 16)
                    for i in range(4):
                        sp.wait_ge(stored[i], 32)

    def attention(tag, units, maps, lhs, rhs, keys, vals, yT, y0, out_gain=None, table=None):
        st = ExitStack()
        with st:
            width = max(len(keys(qt)) for qt, _ in units) * P
            nu = len(units)
            groups = sorted({qt for qt, _ in units})
            e = [[sb(f"e{m}{i}_{tag}", [P, width], st) for i in range(2)] for m in range(maps)]
            pt = sb(f"pt_{tag}", [P, width], st)
            mx, nm, zs, rz = (sb(f"{n}_{tag}", [P, 4], st) for n in ("mx", "nm", "zs", "rz"))
            o = [sb(f"o{i}_{tag}", [P, GW], st) for i in range(2)]
            osq, oss = sb(f"osq_{tag}", [P, GW], st), sb(f"oss_{tag}", [P, 2, H], st)
            scored, maxed, expd, probs = (sem(f"{n}_{tag}") for n in ("scored", "maxed", "expd", "probs"))
            turned, moved, summed, taken = (sem(f"{n}_{tag}") for n in ("turned", "moved", "summed", "taken"))
            finished, oturned, okept = (sem(f"{n}_{tag}") for n in ("finished", "o_turned", "o_kept"))
            osums, oinv, step_s, pstep = (sem(f"{n}_{tag}") for n in ("o_sums", "o_inv", "dve_step", "pool_step"))
            biased, tabled = sem(f"biased_{tag}"), sem(f"table_used_{tag}")
            bb = [sb(f"bb{i}_{tag}", [P, width], st) for i in range(2)] if table else None

            def segments(qt):
                out, col = [], 0
                for kt in keys(qt):
                    if out and out[-1][0] + out[-1][1] == kt * P and col % BANK:
                        out[-1][1] += P
                    else:
                        out.append([kt * P, P, col])
                    col += P
                return out

            def batches(u):
                n = len(keys(units[u][0]))
                return [(k, min(4, n - k)) for k in range(0, n, 4)]

            nb = [0]
            for u in range(nu):
                nb.append(nb[-1] + len(batches(u)))
            turns, where = [], {}
            for u in range(nu):
                for b in range(len(batches(u))):
                    where["batch", u, b] = len(turns)
                    turns.append((moved, nb[u] + b + 1))
                where["sum", u] = len(turns)
                turns.append((taken, u + 1))
                for g in range(len(groups)):
                    if u == min((g + 1) * H + 1, nu - 1) and ("out", g) not in where:
                        where["out", g] = len(turns)
                        turns.append((okept, g + 1))

            def turn_bank(key):
                return 6 + where[key] % 2

            def score_bank(u, m):
                return 3 * (m if maps == 2 else u % 2)

            with nc.Block() as block:
                @block.tensor
                def _(pe):
                    def scores(u):
                        qt, h = units[u]
                        if maps == 2 and u >= 1:
                            pe.wait_ge(expd, 2 * u)
                        if maps == 1 and u >= 2:
                            pe.wait_ge(expd, u - 1)
                        for m in range(maps):
                            for k0, n, col in segments(qt):
                                mm = nc.tensor.matmul(bank(score_bank(u, m), n, col), lhs(qt, h, m), rhs(h, m, k0, n), start=True, stop=True)
                            mm.then_inc(scored, 1)

                    def my_turn(key):
                        if where[key] >= 2:
                            pe.wait_ge(*turns[where[key] - 2])
                        return turn_bank(key)

                    scores(0)
                    for u in range(nu):
                        qt, h = units[u]
                        if u + 1 < nu:
                            scores(u + 1)
                        if maps == 2:
                            pe.wait_ge(probs, u + 1)
                        else:
                            pe.wait_ge(expd, u + 1)
                        for b, (k0, n) in enumerate(batches(u)):
                            tb = my_turn(("batch", u, b))
                            for k in range(n):
                                mm = nc.tensor.transpose(bank(tb, P, k * P), e[0][u % 2][:, (k0 + k) * P:(k0 + k + 1) * P], ident)
                            mm.then_inc(turned, 1)
                        ob = my_turn(("sum", u))
                        pe.wait_ge(moved, nb[u + 1])
                        kts = keys(qt)
                        for k, kt in enumerate(kts):
                            mm = nc.tensor.matmul(bank(ob, HD), pt[:, k * P:(k + 1) * P], vals(kt, h), start=(k == 0), stop=(k == len(kts) - 1))
                        mm.then_inc(summed, 1)
                        for g in range(len(groups)):
                            if u == min((g + 1) * H + 1, nu - 1) and where["out", g] > where["sum", u]:
                                tb = my_turn(("out", g))
                                if out_gain is None:
                                    pe.wait_ge(taken, (g + 1) * H)
                                else:
                                    pe.wait_ge(finished, g + 1)
                                for c in range(2):
                                    mm = nc.tensor.transpose(bank(tb, P, c * P), o[g % 2][:, c * P:(c + 1) * P], ident)
                                mm.then_inc(oturned, 1)

                @block.scalar
                def _(act):
                    def exps(u, m):
                        qt, h = units[u]
                        n = len(keys(qt)) * P
                        i = 2 * (u % 2) + m
                        act.wait_ge(maxed, maps * u + m + 1)
                        if maps == 2 and u >= 2:
                            act.wait_ge(probs, u - 1)
                            if m == 0:
                                act.wait_ge(turned, nb[u - 1])
                        if maps == 1 and u >= 2:
                            act.wait_ge(turned, nb[u - 1])
                            act.wait_ge(taken, u - 1)
                        src = e[0][u % 2][:, 0:n] if (table and qt < LT) else bank(score_bank(u, m), n)
                        ins = nc.scalar.activation(e[m][u % 2][:, 0:n], src, ACT.Exp, bias=nm[:, i:i + 1], accum_out=zs[:, i:i + 1])
                        ins.then_inc(expd, 1)

                    def moves(u):
                        for b, (k0, n) in enumerate(batches(u)):
                            act.wait_ge(turned, nb[u] + b + 1)
                            if b == 0 and u >= 1:
                                act.wait_ge(summed, u)
                            nc.scalar.activation(pt[:, k0 * P:(k0 + n) * P], bank(turn_bank(("batch", u, b)), n * P), ACT.Copy).then_inc(moved, 1)

                    def keep(g):
                        qt = groups[g]
                        act.wait_ge(oturned, g + 1)
                        nc.scalar.activation(yT[:, y0:y0 + 2, qt * P:(qt + 1) * P],
                                             bank(turn_bank(("out", g)), 2 * P).rearrange("p (c t) -> p c t", c=2), ACT.Copy).then_inc(okept, 1)

                    for m in range(maps):
                        exps(0, m)
                    for u in range(nu):
                        if maps == 2 and u + 1 < nu:
                            exps(u + 1, 0)
                        moves(u)
                        if u + 1 < nu:
                            exps(u + 1, maps - 1)
                        for g in range(len(groups)):
                            if where["out", g] == where["sum", u] + 1 or (u == nu - 1 and where["out", g] > where["sum", u]):
                                keep(g)

                @block.vector
                def _(dve):
                    step = Chain(dve, step_s)

                    def top(u):
                        qt, h = units[u]
                        n = len(keys(qt)) * P
                        for m in range(maps):
                            i = 2 * (u % 2) + m
                            dve.wait_ge(scored, maps * u + m + 1)
                            if u >= 2:
                                dve.wait_ge(expd, maps * (u - 2) + m + 1)
                            if table and qt < LT:
                                if u >= 2:
                                    dve.wait_ge(turned, nb[u - 1])
                                dve.wait_ge(biased, u + 1)
                                step.then(nc.vector.tensor_tensor_reduce(e[0][u % 2][:, 0:n], bank(score_bank(u, m), n), bb[u % 2][:, 0:n],
                                                                         1.0, 3.0 * NEG, ALU.add, ALU.max, mx[:, i:i + 1]))
                                step.wait()
                                nc.vector.tensor_scalar(nm[:, i:i + 1], mx[:, i:i + 1], -1.0, None, ALU.mult).then_inc(maxed, 1)
                            else:
                                nc.vector.tensor_reduce(nm[:, i:i + 1], bank(score_bank(u, m), n), AX, ALU.max, negate=True).then_inc(maxed, 1)

                    def combine(u):
                        n = len(keys(units[u][0])) * P
                        i = 2 * (u % 2)
                        dve.wait_ge(expd, 2 * u + 2)
                        step.then(nc.vector.reciprocal(rz[:, i:i + 2], zs[:, i:i + 2]))
                        step.wait()
                        step.then(nc.vector.tensor_scalar(e[1][u % 2][:, 0:n], e[1][u % 2][:, 0:n], rz[:, i + 1:i + 2], neglam[:, 0:1], ALU.mult, ALU.mult))
                        step.wait()
                        nc.vector.scalar_tensor_tensor(out=e[0][u % 2][:, 0:n], in0=e[0][u % 2][:, 0:n], scalar=rz[:, i:i + 1],
                                                       in1=e[1][u % 2][:, 0:n], op0=ALU.mult, op1=ALU.add).then_inc(probs, 1)

                    def take(u):
                        g, h = divmod(u, H)
                        i = 2 * (u % 2)
                        dst = o[g % 2][:, h * HD:(h + 1) * HD]
                        src = bank(turn_bank(("sum", u)), HD)
                        if maps == 1:
                            dve.wait_ge(expd, u + 1)
                            step.then(nc.vector.reciprocal(rz[:, i:i + 1], zs[:, i:i + 1]))
                            step.wait()
                        dve.wait_ge(summed, u + 1)
                        if h == 0 and g >= 2:
                            dve.wait_ge(oturned, g - 1)
                        if maps == 2:
                            nc.vector.tensor_copy(dst, src).then_inc(taken, 1)
                        else:
                            nc.vector.tensor_scalar(dst, src, rz[:, i:i + 1], None, ALU.mult).then_inc(taken, 1)
                        if h == H - 1:
                            dve.wait_ge(taken, u + 1)
                            if out_gain is not None:
                                step.then(nc.vector.tensor_tensor(osq[:, :], o[g % 2][:, :], o[g % 2][:, :], ALU.mult))
                                step.wait()
                                nc.vector.tensor_reduce(oss[:, g % 2, :], osq[:, :].rearrange("p (h d) -> p h d", h=H), AX, ALU.add).then_inc(osums, 1)

                    def finish(g):
                        ov = o[g % 2][:, :].rearrange("p (h d) -> p h d", h=H)
                        dve.wait_ge(oinv, g + 1)
                        step.then(nc.vector.tensor_tensor(ov, ov, oss[:, g % 2, :].unsqueeze(2).broadcast_to([P, H, HD]), ALU.mult))
                        step.wait()
                        nc.vector.tensor_tensor(ov, ov, out_gain.unsqueeze(1).broadcast_to([P, H, HD]), ALU.mult).then_inc(finished, 1)

                    top(0)
                    for u in range(nu):
                        if maps == 2:
                            combine(u)
                        if u + 1 < nu:
                            top(u + 1)
                        take(u)
                        if out_gain is not None:
                            for g in range(len(groups)):
                                if u == min((g + 1) * H, nu - 1) and not (u == nu - 1 and g < (nu - 1) // H and (g + 1) * H < nu - 1):
                                    finish(g)

                @block.gpsimd
                def _(pool):
                    step = Chain(pool, pstep)
                    if table:
                        tb, rowmask = table
                        nlat = sum(qt < LT for qt, _ in units)
                        for i in range(2):
                            step.then(nc.gpsimd.memset(bb[i][:, :], 0.0))
                        step.wait()
                        for u in range(nlat):
                            qt, h = units[u]
                            if u >= 2:
                                pool.wait_ge(maxed, u - 1)
                            s0 = 2 * window_start(qt) - 2 * qt + 8
                            nc.gpsimd.tensor_tensor(bb[u % 2][:, 0:640].rearrange("p (r c) -> p r c", r=10), tb[:, h, s0:s0 + 10, :],
                                                    rowmask(qt).unsqueeze(2).broadcast_to([P, 10, 64]), ALU.add).then_inc(biased, 1)
                    if out_gain is not None:
                        for g in range(len(groups)):
                            pool.wait_ge(osums, g + 1)
                            step.then(nc.gpsimd.tensor_scalar(oss[:, g % 2, :], oss[:, g % 2, :], 1.0 / HD, EPS, ALU.mult, ALU.add))
                            step.wait()
                            nc.gpsimd.tensor_tensor(oss[:, g % 2, :], oss[:, g % 2, :], half[:, 0:H], ALU.pow).then_inc(oinv, 1)

    def attention_units(need):
        return [(qt, h) for qt in range(NT if need else LT) for h in range(H)]

    def all_keys(qt):
        return list(range(NT)) if qt < LT else list(range(LT, NT))

    def load_rows(l, off, n, tile, s):
        def go(sp):
            sp.dma_start(tile[:, :, :], a["w_in"][l].rearrange("(c p) n -> p c n", p=P)[:, :, off:off + n]).then_inc(s, 16)
        return go

    def project_qkv(l, name, heads, hd, gq, gk, qkT, vbuf, rope):
        tag = f"{name}p{l}"
        st = ExitStack()
        with st:
            w = sb(f"w_{tag}", [P, DC, 768], st)
            sq = [sb(f"sq{i}_{tag}", [P, 512], st) for i in range(2)]
            n_ = [sb(f"n{i}_{tag}", [P, 512], st) for i in range(2)]
            r_ = sb(f"r_{tag}", [P, 512], st)
            u_ = sb(f"u_{tag}", [P, 512], st)
            ss = [sb(f"ss{i}_{tag}", [P, 2 * heads], st) for i in range(2)]
            loaded, projected, squared, sums = (sem(f"{n}_{tag}") for n in ("loaded", "projected", "squared", "sums"))
            inv, normed, vkept, turned = (sem(f"{n}_{tag}") for n in ("inv", "normed", "v_kept", "turned"))
            kept, ready, step_s, pstep, cosd = (sem(f"{n}_{tag}") for n in ("kept", "ready", "dve_step", "pool_step", "cos_done"))
            gained = sem(f"gained_{tag}")
            nh = 2 * heads
            go = load_rows(l, OFF[name], 768, w, loaded)
            with nc.Block() as block:
                @block.sync
                def _(sp):
                    go(sp)

                @block.tensor
                def _(pe):
                    pe.wait_ge(loaded, 16)
                    for t in range(NT + 1):
                        if t < NT:
                            if t >= 2:
                                pe.wait_ge(normed, t - 1)
                                pe.wait_ge(vkept, t - 1)
                            for b, c0, n in ((t % 2, 0, 512), (2 + t % 2, 512, 256)):
                                for c in range(DC):
                                    mm = nc.tensor.matmul(bank(b, n), hT[:, c, t * P:(t + 1) * P], w[:, c, c0:c0 + n], start=(c == 0), stop=(c == DC - 1))
                            mm.then_inc(projected, 1)
                        if t >= 1:
                            i = t - 1
                            pe.wait_ge(ready, i + 1)
                            if i >= 2:
                                pe.wait_ge(kept, i - 1)
                            for c in range(4):
                                mm = nc.tensor.transpose(bank(4 + i % 2, P, c * P), n_[i % 2][:, c * P:(c + 1) * P], ident)
                            mm.then_inc(turned, 1)

                @block.scalar
                def _(act):
                    for t in range(NT + 1):
                        if t < NT:
                            act.wait_ge(projected, t + 1)
                            if t >= 2:
                                act.wait_ge(sums, t - 1)
                            nc.scalar.activation(sq[t % 2][:, :], bank(t % 2), ACT.Square).then_inc(squared, 1)
                            nc.scalar.activation(vbuf[:, t, :], bank(2 + t % 2, 256), ACT.Copy).then_inc(vkept, 1)
                        if t >= 1:
                            i = t - 1
                            act.wait_ge(turned, i + 1)
                            nc.scalar.activation(qkT[:, :, i * P:(i + 1) * P], bank(4 + i % 2).rearrange("p (c t) -> p c t", c=4), ACT.Copy).then_inc(kept, 1)

                @block.gpsimd
                def _(pool):
                    step = Chain(pool, pstep)
                    for t in range(NT):
                        pool.wait_ge(sums, t + 1)
                        step.then(nc.gpsimd.tensor_scalar(ss[t % 2][:, :], ss[t % 2][:, :], 1.0 / hd, EPS, ALU.mult, ALU.add))
                        step.wait()
                        nc.gpsimd.tensor_tensor(ss[t % 2][:, :], ss[t % 2][:, :], half[:, 0:nh], ALU.pow).then_inc(inv, 1)

                @block.vector
                def _(dve):
                    step = Chain(dve, step_s)

                    def heads_of(x):
                        return x.rearrange("p (h d) -> p h d", h=nh)

                    def sum_squares(t):
                        dve.wait_ge(squared, t + 1)
                        if t >= 2:
                            dve.wait_ge(normed, t - 1)
                        nc.vector.tensor_reduce(ss[t % 2][:, :], heads_of(sq[t % 2][:, :]), AX, ALU.add).then_inc(sums, 1)

                    sum_squares(0)
                    for t in range(NT):
                        if t + 1 < NT:
                            sum_squares(t + 1)
                        n = n_[t % 2]
                        dve.wait_ge(inv, t + 1)
                        if t >= 2:
                            dve.wait_ge(turned, t - 1)
                        nc.vector.tensor_tensor(heads_of(n[:, :]), heads_of(bank(t % 2)), ss[t % 2][:, :].unsqueeze(2).broadcast_to([P, nh, hd]), ALU.mult).then_inc(normed, 1)
                        dve.wait_ge(normed, t + 1)
                        roped = rope and t < LT
                        for k, g in enumerate((gq, gk)):
                            half_n = heads_of(n[:, :])[:, k * heads:(k + 1) * heads, :]
                            ins = nc.vector.tensor_tensor(half_n, half_n, g.unsqueeze(1).broadcast_to([P, heads, hd]), ALU.mult)
                            if roped or k == 0:
                                step.then(ins)
                            else:
                                step.wait()
                                ins.then_inc(ready, 1)
                        if roped:
                            step.wait()
                            cos = cst[:, C_COS + 32 * t:C_COS + 32 * t + 32].unsqueeze(1).broadcast_to([P, nh, 32])
                            sin = cst[:, C_SIN + 32 * t:C_SIN + 32 * t + 32].rearrange("p (a b e) -> p a b e", a=2, b=2)
                            nv = n[:, :].rearrange("p (h a b e) -> p h a b e", h=nh, a=2, b=2)
                            rv = r_[:, :].rearrange("p (h a b e) -> p h a b e", h=nh, a=2, b=2)
                            for x in range(2):
                                for y in range(2):
                                    step.then(nc.vector.tensor_tensor(rv[:, :, x, y, :], nv[:, :, x, 1 - y, :],
                                                                      sin[:, x, y, :].unsqueeze(1).broadcast_to([P, nh, 8]), ALU.mult))
                            step.then(nc.vector.tensor_tensor(heads_of(u_[:, :]), heads_of(n[:, :]), cos, ALU.mult))
                            step.wait()
                            nc.vector.tensor_tensor(n[:, :], u_[:, :], r_[:, :], ALU.add).then_inc(ready, 1)

    def mixers(l, yT, need):
        R = {k: rows[:, l, o:o + w] for k, (o, w) in ROWS.items()}

        def diff():
            st = ExitStack()
            with st:
                qkT = sb(f"dqkT{l}", [P, 4, T], st)
                v = sb(f"dv{l}", [P, NT, GW], st)
                project_qkv(l, "diff", 2 * H, DQK, R["diff_g_q"], R["diff_g_k"], qkT, v, True)
                attention(f"diff{l}", attention_units(need), 2,
                          lambda qt, h, m: qkT[32 * ((2 * h + m) % 4):32 * ((2 * h + m) % 4) + 32, h // 2, qt * P:(qt + 1) * P],
                          lambda h, m, k0, n: qkT[32 * ((2 * h + m) % 4):32 * ((2 * h + m) % 4) + 32, 2 + h // 2, k0:k0 + n],
                          all_keys, lambda kt, h: v[:, kt, h * HD:(h + 1) * HD], yT, 0, out_gain=R["diff_g_out"])
        diff()
        clear_semaphores()

        def mla():
            st = ExitStack()
            with st:
                qkT = sb(f"mqkT{l}", [P, 2 * H, T], st)
                v = sb(f"mv{l}", [P, NT, GW], st)
                mla_project(l, R, qkT, v, yT)
                attention(f"mla{l}", attention_units(need), 1,
                          lambda qt, h, m: qkT[0:MD, h, qt * P:(qt + 1) * P],
                          lambda h, m, k0, n: qkT[0:MD, H + h, k0:k0 + n],
                          all_keys, lambda kt, h: v[:, kt, h * HD:(h + 1) * HD], yT, 2)
        mla()
        clear_semaphores()

        def na():
            st = ExitStack()
            with st:
                qkT = sb(f"nqkT{l}", [P, 4, T], st)
                v = sb(f"nv{l}", [P, NT, GW], st)
                project_qkv(l, "na", H, HD, R["na_g_q"], R["na_g_k"], qkT, v, False)
                tb = sb(f"ntb{l}", [P, H, NSLOT, GRID_W], st)
                position_table(l, tb, yT)

                def keys(qt):
                    if qt >= LT:
                        return [LT, LT + 1]
                    return list(range(window_start(qt), window_start(qt) + 5)) + [LT, LT + 1]
                attention(f"na{l}", attention_units(need), 1,
                          lambda qt, h, m: qkT[HD * (h % 2):HD * (h % 2) + HD, h // 2, qt * P:(qt + 1) * P],
                          lambda h, m, k0, n: qkT[HD * (h % 2):HD * (h % 2) + HD, 2 + h // 2, k0:k0 + n],
                          keys, lambda kt, h: v[:, kt, h * HD:(h + 1) * HD], yT, 6,
                          table=(tb, lambda qt: cst[:, C_ROW + 10 * qt:C_ROW + 10 * qt + 10]))
        na()
        clear_semaphores()

        mlstm(l, R, yT, need)
        clear_semaphores()

    def position_table(l, tb, yT):
        read, turned, masked = sem(f"rpb_read{l}"), sem(f"rpb_turned{l}"), sem(f"rpb_masked{l}")
        n = H * NSLOT * GRID_W
        raw = yT[:, 4:8, :].rearrange("p c t -> p (c t)")[:, 0:n]
        flat = tb[:, :, :, :].rearrange("p h s k -> p (h s) k")
        with nc.Block() as block:
            @block.sync
            def _(sp):
                for h in range(H):
                    for x in range(2):
                        off = ((l * H + h) * (NSLOT + 1) + x) * 127
                        sp.dma_start(raw[x * GRID_W:(x + 1) * GRID_W, :].rearrange("p (h s k) -> p h s k", h=H, s=NSLOT)[:, h, :, :],
                                     bass.AP(rpb_pad.tensor, off, [[1, GRID_W], [127, NSLOT], [1, GRID_W]])).then_inc(read, 16)

            @block.tensor
            def _(pe):
                pe.wait_ge(read, 16 * 2 * H)
                for i in range(n // 512):
                    if i >= 8:
                        pe.wait_ge(masked, i - 7)
                    nc.tensor.matmul(bank(i % 8), cst[:, C_REV:C_REV + P], raw[:, i * 512:(i + 1) * 512], start=True, stop=True).then_inc(turned, 1)

            @block.vector
            def _(dve):
                for i in range(n // 512):
                    dve.wait_ge(turned, i + 1)
                    nc.vector.tensor_tensor(flat[:, 8 * i:8 * i + 8, :], bank(i % 8).rearrange("p (s k) -> p s k", s=8),
                                            cst[:, C_COL:C_COL + 64].unsqueeze(1).broadcast_to([P, 8, GRID_W]), ALU.add).then_inc(masked, 1)

    def mla_project(l, R, qkT, v, yT):
        st = ExitStack()
        with st:
            tag = f"mlap{l}"
            w = yT[:, 4:8, :].rearrange("p c t -> p (c t)")[:, 0:DC * 416].rearrange("p (c n) -> p c n", c=DC)
            wq = sb(f"wq_{tag}", [P, 2, H * MD], st)
            wkv = sb(f"wkv_{tag}", [P, 2 * GW], st)
            sq = sb(f"sq_{tag}", [P, 256], st)
            sq2 = sb(f"sq2_{tag}", [P, 2 * H * MD], st)
            cn = [sb(f"cn{i}_{tag}", [P, 384], st) for i in range(2)]
            kr = [sb(f"kr{i}_{tag}", [P, ROPE], st) for i in range(2)]
            cT = sb(f"cT_{tag}", [P, 3, P], st)
            qk = sb(f"qk_{tag}", [P, 2 * H, MD], st)
            rt = sb(f"rt_{tag}", [P, 2 * H, ROPE], st)
            ss = sb(f"ss_{tag}", [P, 2, 2], st)
            s8 = sb(f"s8_{tag}", [P, 2, 2 * H], st)
            loaded, projected, sums, inv = (sem(f"{n}_{tag}") for n in ("loaded", "projected", "sums", "inv"))
            normed, cturned, ckept, up = (sem(f"{n}_{tag}") for n in ("normed", "c_turned", "c_kept", "up"))
            gathered, qsq, qsums, qinv = (sem(f"{n}_{tag}") for n in ("gathered", "q_squared", "q_sums", "q_inv"))
            ready, turned, kept, vkept = (sem(f"{n}_{tag}") for n in ("ready", "turned", "kept", "v_kept"))
            step_s, pstep = sem(f"dve_step_{tag}"), sem(f"pool_step_{tag}")
            go = load_rows(l, OFF["mla"], 416, w, loaded)
            with nc.Block() as block:
                @block.sync
                def _(sp):
                    go(sp)
                    sp.dma_start(wq[:, :, :], a["mla_w_uq"][l].rearrange("(c p) n -> p c n", p=P)).then_inc(loaded, 16)
                    sp.dma_start(wkv[:, :], a["mla_w_ukv"][l]).then_inc(loaded, 16)

                @block.tensor
                def _(pe):
                    pe.wait_ge(loaded, 48)

                    def down(t):
                        if t >= 2:
                            pe.wait_ge(normed, t - 1)
                        for c in range(DC):
                            mm = nc.tensor.matmul(bank(t % 2, 416), hT[:, c, t * P:(t + 1) * P], w[:, c, :], start=(c == 0), stop=(c == DC - 1))
                        mm.then_inc(projected, 1)

                    def turn_back(t):
                        pe.wait_ge(ready, t + 1)
                        for s in range(2):
                            if t >= 1:
                                pe.wait_ge(kept, 2 * (t - 1) + s + 1)
                            for h in range(H):
                                mm = nc.tensor.transpose(bank(5 + s, P, h * P)[0:MD, :], qk[:, s * H + h, :], ident)
                            mm.then_inc(turned, 1)

                    down(0)
                    for t in range(NT):
                        if t + 1 < NT:
                            down(t + 1)
                        pe.wait_ge(normed, t + 1)
                        if t >= 1:
                            pe.wait_ge(ckept, t)
                        for c in range(3):
                            mm = nc.tensor.transpose(bank(2, P, c * P), cn[t % 2][:, c * P:(c + 1) * P], ident)
                        mm.then_inc(cturned, 1)
                        if t >= 1:
                            turn_back(t - 1)
                        pe.wait_ge(ckept, t + 1)
                        if t >= 1:
                            pe.wait_ge(gathered, t)
                            pe.wait_ge(vkept, t)
                        for c in range(2):
                            nc.tensor.matmul(bank(3, H * MD), cT[:, c, :], wq[:, c, :], start=(c == 0), stop=(c == 1))
                        nc.tensor.matmul(bank(4), cT[:, 2, :], wkv[:, :], start=True, stop=True).then_inc(up, 1)
                    turn_back(NT - 1)

                @block.scalar
                def _(act):
                    def first(t):
                        act.wait_ge(projected, t + 1)
                        if t >= 2:
                            act.wait_ge(normed, t - 1)
                        nc.scalar.activation(sq[:, :], bank(t % 2, MQ), ACT.Square, scale=MQ ** -0.5, accum_out=ss[:, t % 2, 0:1]).then_inc(sums, 1)
                        act.wait_ge(sums, 2 * t + 1)
                        nc.scalar.activation(sq[:, 0:MKV], bank(t % 2, MKV, MQ), ACT.Square, scale=MKV ** -0.5, accum_out=ss[:, t % 2, 1:2]).then_inc(sums, 1)
                        act.wait_ge(sums, 2 * t + 2)

                    def move(t):
                        act.wait_ge(turned, 2 * t + 2)
                        for s in range(2):
                            nc.scalar.activation(qkT[0:MD, s * H:(s + 1) * H, t * P:(t + 1) * P],
                                                 bank(5 + s)[0:MD, :].rearrange("p (h t) -> p h t", h=H), ACT.Copy).then_inc(kept, 1)

                    first(0)
                    for t in range(NT):
                        if t + 1 < NT:
                            first(t + 1)
                        act.wait_ge(cturned, t + 1)
                        if t >= 1:
                            act.wait_ge(up, t)
                        nc.scalar.activation(cT[:, 0, :], bank(2, P), ACT.Copy, scale=vec[:, l, V_GCQ:V_GCQ + 1])
                        nc.scalar.activation(cT[:, 1, :], bank(2, P, P), ACT.Copy, scale=vec[:, l, V_GCQ + 1:V_GCQ + 2])
                        nc.scalar.activation(cT[:, 2, :], bank(2, P, 2 * P), ACT.Copy, scale=vec[:, l, V_GCKV:V_GCKV + 1]).then_inc(ckept, 1)
                        if t >= 1:
                            move(t - 1)
                        act.wait_ge(up, t + 1)
                        act.wait_ge(gathered, t + 1)
                        nc.scalar.activation(v[:, t, :].rearrange("p (h d) -> p h d", h=H),
                                             bank(4).rearrange("p (h d) -> p h d", h=H)[:, :, HD:2 * HD], ACT.Copy).then_inc(vkept, 1)
                        if t >= 1:
                            act.wait_ge(qsums, t)
                        nc.scalar.activation(sq2[:, :], qk[:, :, :].rearrange("p h d -> p (h d)"), ACT.Square).then_inc(qsq, 1)
                    move(NT - 1)

                @block.gpsimd
                def _(pool):
                    step = Chain(pool, pstep)
                    for t in range(NT + 1):
                        if t < NT:
                            pool.wait_ge(sums, 2 * t + 2)
                            step.then(nc.gpsimd.tensor_scalar(ss[:, t % 2, :], ss[:, t % 2, :], EPS, 1.0, ALU.add, ALU.mult))
                            step.wait()
                            nc.gpsimd.tensor_tensor(ss[:, t % 2, :], ss[:, t % 2, :], half[:, 0:2], ALU.pow).then_inc(inv, 1)
                        if t >= 1:
                            i = t - 1
                            pool.wait_ge(qsums, i + 1)
                            step.then(nc.gpsimd.tensor_scalar(s8[:, i % 2, :], s8[:, i % 2, :], 1.0 / MD, EPS, ALU.mult, ALU.add))
                            step.wait()
                            nc.gpsimd.tensor_tensor(s8[:, i % 2, :], s8[:, i % 2, :], half[:, 0:2 * H], ALU.pow).then_inc(qinv, 1)

                @block.vector
                def _(dve):
                    step = Chain(dve, step_s)

                    def norm_latents(t):
                        dve.wait_ge(inv, t + 1)
                        if t >= 2:
                            dve.wait_ge(cturned, t - 1)
                            dve.wait_ge(gathered, t - 1)
                        nc.vector.tensor_copy(kr[t % 2][:, :], bank(t % 2, ROPE, MQ + MKV))
                        nc.vector.tensor_scalar(cn[t % 2][:, 0:MQ], bank(t % 2, MQ), ss[:, t % 2, 0:1], None, ALU.mult)
                        nc.vector.tensor_scalar(cn[t % 2][:, MQ:MQ + MKV], bank(t % 2, MKV, MQ), ss[:, t % 2, 1:2], None, ALU.mult).then_inc(normed, 1)

                    norm_latents(0)
                    for t in range(NT):
                        if t + 1 < NT:
                            norm_latents(t + 1)
                        dve.wait_ge(up, t + 1)
                        if t >= 1:
                            dve.wait_ge(turned, 2 * t)
                        nc.vector.tensor_copy(qk[:, 0:H, :], bank(3, H * MD).rearrange("p (h d) -> p h d", h=H))
                        nc.vector.tensor_copy(qk[:, H:2 * H, 0:HD], bank(4).rearrange("p (h d) -> p h d", h=H)[:, :, 0:HD])
                        dve.wait_ge(normed, t + 1)
                        nc.vector.tensor_copy(qk[:, H:2 * H, HD:MD], kr[t % 2][:, :].unsqueeze(1).broadcast_to([P, H, ROPE])).then_inc(gathered, 1)
                        dve.wait_ge(qsq, t + 1)
                        if t >= 2:
                            dve.wait_ge(step_s, n2)
                        nc.vector.tensor_reduce(s8[:, t % 2, :], sq2[:, :].rearrange("p (h d) -> p h d", h=2 * H), AX, ALU.add).then_inc(qsums, 1)
                        dve.wait_ge(qinv, t + 1)
                        n2 = step.then(nc.vector.tensor_tensor(qk[:, :, :], qk[:, :, :], s8[:, t % 2, :].unsqueeze(2).broadcast_to([P, 2 * H, MD]), ALU.mult))
                        step.wait()
                        step.then(nc.vector.tensor_tensor(qk[:, 0:H, :], qk[:, 0:H, :], R["mla_g_q"].unsqueeze(1).broadcast_to([P, H, MD]), ALU.mult))
                        ins = nc.vector.tensor_tensor(qk[:, H:2 * H, :], qk[:, H:2 * H, :], R["mla_g_k"].unsqueeze(1).broadcast_to([P, H, MD]), ALU.mult)
                        if t >= LT:
                            step.wait()
                            ins.then_inc(ready, 1)
                        else:
                            step.then(ins)
                            step.wait()
                            cos = cst[:, C_COS + 32 * t:C_COS + 32 * t + 32].unsqueeze(1).broadcast_to([P, 2 * H, ROPE])
                            sin = cst[:, C_SIN + 32 * t:C_SIN + 32 * t + 32].rearrange("p (a b e) -> p a b e", a=2, b=2)
                            rq = qk[:, :, HD:MD]
                            for x in range(2):
                                for y in range(2):
                                    o0 = HD + 16 * x + 8 * (1 - y)
                                    step.then(nc.vector.tensor_tensor(rt[:, :, 16 * x + 8 * y:16 * x + 8 * y + 8], qk[:, :, o0:o0 + 8],
                                                                      sin[:, x, y, :].unsqueeze(1).broadcast_to([P, 2 * H, 8]), ALU.mult))
                            step.wait()
                            step.then(nc.vector.tensor_tensor(rq, rq, cos, ALU.mult))
                            step.wait()
                            nc.vector.tensor_tensor(rq, rq, rt[:, :, :], ALU.add).then_inc(ready, 1)

    def mlstm(l, R, yT, need):
        st = ExitStack()
        nq = NT if need else LT
        G4 = NT * H
        order = [[8, 9] + list(range(LT)), [9, 8] + list(range(LT))[::-1]]
        with st:
            qkT = sb(f"lqkT{l}", [P, 4, T], st)
            v = sb(f"lv1_{l}", [P, NT, H, HD + 1], st)
            def so(t):
                return yT[:, 4:6, t * P:(t + 1) * P]
            gt = sb(f"gt{l}", [P, NT, 16], st)
            A, M, EM = (sb(f"{n}{l}", [P, 2, NT, H], st) for n in ("gA", "gM", "gEM"))
            mlstm_project(l, R, qkT, v, so, gt)
            mlstm_gates(l, R, gt, A, M, EM, order)
            clear_semaphores()
            mlstm_mix(l, R, qkT, v, so, A, M, EM, yT, nq)

    def mlstm_project(l, R, qkT, v, so, gt):
        st = ExitStack()
        width = T + 4
        span = T + 2
        with st:
            tag = f"mlp{l}"
            wqk = sb(f"wqk_{tag}", [P, DC, 512], st)
            wg = sb(f"wg_{tag}", [P, DC, 16], st)
            u = [sb(f"u{i}_{tag}", [P, width], st) for i in range(2)]
            cv = [sb(f"cv{i}_{tag}", [P, width], st) for i in range(1)]
            loaded, loaded2, loaded3, up, copied = (sem(f"{n}_{tag}") for n in ("loaded", "loaded_vo", "loaded_g", "up", "copied"))
            zeroed, step_s, conv, silu = (sem(f"{n}_{tag}") for n in ("zeroed", "dve_step", "conv", "silu"))
            projected, vkept, okept, gkept = (sem(f"{n}_{tag}") for n in ("projected", "v_kept", "o_kept", "g_kept"))
            with nc.Block() as block:
                @block.sync
                def _(sp):
                    load_rows(l, OFF["mlqk"], 512, wqk, loaded)(sp)
                    load_rows(l, OFF["mlg"], 16, wg, loaded3)(sp)
                    sp.wait_ge(up, 4)
                    load_rows(l, OFF["mlvo"], 512, wqk, loaded2)(sp)

                @block.tensor
                def _(pe):
                    pe.wait_ge(loaded, 16)
                    for f in range(4):
                        if f >= 2:
                            pe.wait_ge(copied, 2 * (f - 1))
                        for j, (t0, m, s) in enumerate(BLOCKS):
                            for c in range(DC):
                                mm = nc.tensor.matmul(bank(3 * (f % 2) + j, m), wqk[:, c, f * P:(f + 1) * P], hT[:, c, t0:t0 + m], start=(c == 0), stop=(c == DC - 1))
                        mm.then_inc(up, 1)
                    pe.wait_ge(loaded2, 16)
                    pe.wait_ge(loaded3, 16)
                    pe.wait_ge(copied, 8)
                    for t in range(NT):
                        if t >= 2:
                            pe.wait_ge(vkept, t - 1)
                            pe.wait_ge(okept, t - 1)
                            pe.wait_ge(gkept, t - 1)
                        for c in range(DC):
                            nc.tensor.matmul(bank(t % 2), hT[:, c, t * P:(t + 1) * P], wqk[:, c, :], start=(c == 0), stop=(c == DC - 1))
                        for c in range(DC):
                            mm = nc.tensor.matmul(bank(2 + t % 2, 16), hT[:, c, t * P:(t + 1) * P], wg[:, c, :], start=(c == 0), stop=(c == DC - 1))
                        mm.then_inc(projected, 1)

                @block.scalar
                def _(act):
                    act.wait_ge(zeroed, 2)
                    for f in range(4):
                        act.wait_ge(up, f + 1)
                        if f >= 2:
                            act.wait_ge(conv, f - 1)
                        nc.scalar.activation(u[f % 2][:, 1:1 + SEQ], bank(3 * (f % 2), SEQ), ACT.Copy).then_inc(copied, 1)
                        nc.scalar.activation(u[f % 2][:, SEQ + 3:SEQ + 3 + CTX], bank(3 * (f % 2) + 2, CTX), ACT.Copy).then_inc(copied, 1)
                        act.wait_ge(conv, f + 1)
                        nc.scalar.activation(qkT[:, f, 0:SEQ], cv[0][:, 0:SEQ], ACT.Silu)
                        nc.scalar.activation(qkT[:, f, SEQ:T], cv[0][:, SEQ + 2:T + 2], ACT.Silu).then_inc(silu, 1)
                    for t in range(NT):
                        act.wait_ge(projected, t + 1)
                        nc.scalar.activation(so(t), bank(t % 2, GW, GW).rearrange("p (c d) -> p c d", c=2), ACT.Sigmoid).then_inc(okept, 1)

                @block.gpsimd
                def _(pool):
                    for i in range(2):
                        nc.gpsimd.memset(u[i][:, :], 0.0).then_inc(zeroed, 1)
                    nc.gpsimd.memset(v[:, :, :, HD:HD + 1], 1.0).then_inc(zeroed, 1)

                @block.vector
                def _(dve):
                    step = Chain(dve, step_s)
                    for f in range(4):
                        def w(k):
                            c = V_MCONV + 4 * k + f
                            return vec[:, l, c:c + 1]
                        dve.wait_ge(copied, 2 * f + 2)
                        if f >= 1:
                            dve.wait_ge(silu, f)
                        x = u[f % 2]
                        step.then(nc.vector.tensor_scalar(cv[0][:, 0:span], x[:, 0:span], w(0), None, ALU.mult))
                        step.wait()
                        step.then(nc.vector.scalar_tensor_tensor(out=cv[0][:, 0:span], in0=x[:, 1:1 + span], scalar=w(1), in1=cv[0][:, 0:span], op0=ALU.mult, op1=ALU.add))
                        step.wait()
                        nc.vector.scalar_tensor_tensor(out=cv[0][:, 0:span], in0=x[:, 2:2 + span], scalar=w(2), in1=cv[0][:, 0:span], op0=ALU.mult, op1=ALU.add).then_inc(conv, 1)
                    for t in range(NT):
                        dve.wait_ge(projected, t + 1)
                        dve.wait_ge(okept, t + 1)
                        nc.vector.tensor_copy(v[:, t, :, 0:HD], bank(t % 2, GW).rearrange("p (h d) -> p h d", h=H)).then_inc(vkept, 1)
                        nc.vector.tensor_copy(gt[:, t, :], bank(2 + t % 2, 16)).then_inc(gkept, 1)

    def mlstm_gates(l, R, gt, A, M, EM, order):
        st = ExitStack()
        G4 = NT * H
        PAD = 64
        with st:
            tag = f"mlg{l}"
            F, E1, B, TOT, TM = (sb(f"{n}_{tag}", [P, 2, NT, H], st) for n in ("F", "E1", "B", "TOT", "TM"))
            off = sb(f"off_{tag}", [P, 2, NT, H], st)
            run = sb(f"run_{tag}", [P, 2, NT, H], st)
            sc = [sb(f"sc{i}_{tag}", [G4, 2, PAD + P], st) for i in range(2)]
            back = sb(f"back_{tag}", [P, 2, G4], st)
            step_s, astep, pstep = sem(f"dve_step_{tag}"), sem(f"act_step_{tag}"), sem(f"pe_step_{tag}")
            padded = sem(f"padded_{tag}")
            flat = "p a t h -> p (a t h)"

            def d(x, i):
                return x[:, i, :, :].rearrange("p t h -> p (t h)")

            def both(x):
                return x[:, :, :, :].rearrange(flat)
            cum = (cst[:, C_CUM:C_CUM + P], cst[:, C_CUMR:C_CUMR + P])
            rev = cst[:, C_REV:C_REV + P]
            e127 = cst[:, C_E127:C_E127 + P]
            marks = {}
            with nc.Block() as block:
                @block.gpsimd
                def _(pool):
                    for i in range(2):
                        nc.gpsimd.memset(sc[i][:, :, :], 3.0 * NEG).then_inc(padded, 1)

                @block.vector
                def _(dve):
                    step = Chain(dve, step_s)

                    def go(ins):
                        step.then(ins)
                        step.wait()
                    for i in range(2):
                        for x, o, b in ((F, 8 + 4 * i, "mlstm_b_f"), (A, 4 * i, "mlstm_b_i")):
                            go(nc.vector.tensor_tensor(x[:, i, :, :], gt[:, :, o:o + 4],
                                                       R[b][:, 4 * i:4 * i + 4].unsqueeze(1).broadcast_to([P, NT, H]), ALU.add))
                    go(nc.vector.scalar_tensor_tensor(out=both(E1), in0=both(F), scalar=-1.0, in1=both(F), op0=ALU.mult, op1=ALU.max))
                    marks["abs"] = step.n
                    dve.wait_ge(astep, 2)
                    go(nc.vector.scalar_tensor_tensor(out=both(F), in0=both(F), scalar=0.0, in1=both(E1), op0=ALU.min, op1=ALU.subtract))
                    marks["lf"] = step.n
                    dve.wait_ge(pstep, 3)
                    go(nc.vector.tensor_copy(both(TOT), bank(2, 2 * G4)))
                    for i in range(2):
                        step.then(nc.vector.memset(off[:, i, order[i][0], :], 0.0))
                    step.wait()
                    for n in range(1, NT):
                        for i in range(2):
                            x, y = order[i][n], order[i][n - 1]
                            step.then(nc.vector.tensor_tensor(off[:, i, x, :], off[:, i, y, :], TOT[:, i, y, :], ALU.add))
                        step.wait()
                    for i in range(2):
                        go(nc.vector.tensor_tensor(d(B, i), bank(i, G4), d(off, i), ALU.add))
                    go(nc.vector.tensor_tensor(both(A), both(A), both(B), ALU.subtract))
                    marks["a"] = step.n
                    dve.wait_ge(pstep, 5)
                    dve.wait_ge(padded, 2)
                    for i in range(2):
                        go(nc.vector.tensor_copy(sc[0][:, i, PAD:PAD + P], bank(3 + i, P)[0:G4, :]))
                    for n in range(7):
                        x, y, k = sc[n % 2], sc[(n + 1) % 2], 1 << n
                        go(nc.vector.tensor_tensor(y[:, :, PAD:PAD + P], x[:, :, PAD:PAD + P], x[:, :, PAD - k:PAD + P - k], ALU.max))
                    marks["scan"] = step.n
                    dve.wait_ge(pstep, 6)
                    go(nc.vector.tensor_copy(back[:, :, :], bank(5, 2 * G4).rearrange("p (a n) -> p a n", a=2)))
                    marks["back"] = step.n
                    dve.wait_ge(pstep, 8)
                    go(nc.vector.tensor_copy(both(TM), bank(6, 2 * G4)))
                    for i in range(2):
                        step.then(nc.vector.memset(run[:, i, order[i][0], :], 3.0 * NEG))
                    step.wait()
                    for n in range(1, NT):
                        for i in range(2):
                            x, y = order[i][n], order[i][n - 1]
                            step.then(nc.vector.tensor_tensor(run[:, i, x, :], run[:, i, y, :], TM[:, i, y, :], ALU.max))
                        step.wait()
                    go(nc.vector.tensor_tensor(d(M, 0), back[:, 0, :], d(run, 0), ALU.max))
                    go(nc.vector.tensor_tensor(d(M, 1), bank(7, G4), d(run, 1), ALU.max))
                    go(nc.vector.tensor_tensor(both(B), both(B), both(M), ALU.add))
                    marks["bm"] = step.n

                @block.scalar
                def _(act):
                    act.wait_ge(step_s, marks["abs"])
                    nc.scalar.activation(both(E1), both(E1), ACT.Exp, scale=-1.0).then_inc(astep, 1)
                    act.wait_ge(astep, 1)
                    nc.scalar.activation(both(E1), both(E1), ACT.Ln, bias=1.0).then_inc(astep, 1)
                    act.wait_ge(step_s, marks["bm"])
                    nc.scalar.activation(both(EM), both(B), ACT.Exp, scale=-1.0).then_inc(astep, 1)

                @block.tensor
                def _(pe):
                    pe.wait_ge(step_s, marks["lf"])
                    for i in range(2):
                        nc.tensor.matmul(bank(i, G4), cum[i], d(F, i), start=True, stop=True).then_inc(pstep, 1)
                    nc.tensor.matmul(bank(2, 2 * G4), ones[:, :], both(F), start=True, stop=True).then_inc(pstep, 1)
                    pe.wait_ge(step_s, marks["a"])
                    nc.tensor.matmul(bank(3, P)[0:G4, :], d(A, 0), ident, start=True, stop=True).then_inc(pstep, 1)
                    nc.tensor.matmul(bank(4, P)[0:G4, :], d(A, 1), rev, start=True, stop=True).then_inc(pstep, 1)
                    pe.wait_ge(step_s, marks["scan"])
                    for i in range(2):
                        mm = nc.tensor.matmul(bank(5, G4, G4 * i), sc[1][:, i, PAD:PAD + P], ident[0:G4, 0:G4], start=True, stop=True)
                    mm.then_inc(pstep, 1)
                    pe.wait_ge(step_s, marks["back"])
                    nc.tensor.matmul(bank(6, 2 * G4), e127, back[:, :, :].rearrange("p a n -> p (a n)"), start=True, stop=True).then_inc(pstep, 1)
                    nc.tensor.matmul(bank(7, G4), rev, back[:, 1, :], start=True, stop=True).then_inc(pstep, 1)

    def mlstm_mix(l, R, qkT, v, so, A, M, EM, yT, nq):
        st = ExitStack()
        nblk = 3 if nq == NT else 2
        RING = 10
        with st:
            tag = f"mlm{l}"
            hs = sb(f"hs_{tag}", [P, NT, GW], st)
            dg = [sb(f"dg{i}_{tag}", [P, 512], st) for i in range(2)]
            nmd = sb(f"nmd_{tag}", [P, 2, 512], st)
            wt = [sb(f"wt{i}_{tag}", [P, 512], st) for i in range(2)]
            pr = [hT[:, :, :].rearrange("p c t -> p (c t)")[:, i * 512:(i + 1) * 512] for i in range(RING)]
            den = sb(f"den_{tag}", [P, 2, 4], st)
            ob = sb(f"ob_{tag}", [P, 2, 4, HD], st)
            ss = sb(f"ss_{tag}", [P, NT, H], st)
            step_s, diag, neg, masked, scored = (sem(f"{n}_{tag}") for n in ("dve_step", "diag", "neg_max", "masked", "scored"))
            weighed, product, summed, taken = (sem(f"{n}_{tag}") for n in ("weighed", "product", "summed", "taken"))
            sums, inv, ready, turned, kept, pstep = (sem(f"{n}_{tag}") for n in ("sums", "inv", "ready", "turned", "kept", "pool_step"))
            used = sem(f"used_{tag}")
            units = []
            for blk in range(nblk):
                t0, m, s = BLOCKS[blk]
                q0, q1 = t0 // P, (t0 + m) // P
                for h in range(H):
                    jobs = []
                    for kt in ([8, 9] + list(range(LT)) if s == 0 else [8, 9]):
                        for i in range(2):
                            if s == 0 and kt >= LT:
                                lo, hi = q0, q1
                            elif i == 0:
                                lo, hi = max(q0, kt), q1
                            else:
                                lo, hi = q0, min(q1, kt + 1)
                            if lo < hi:
                                jobs.append((i, kt, lo, hi))
                    units.append((blk, h, q0, q1, s, jobs))
            tiles = []
            for n, (blk, h, q0, q1, s, jobs) in enumerate(units):
                for kt in dict.fromkeys(j[1] for j in jobs):
                    tiles.append((n, kt, [j for j in jobs if j[1] == kt]))
            jobs_all = [(n, j) for n, kt, js in tiles for j in js]
            jobs_end = [sum(1 for n, _ in jobs_all if n <= u) for u in range(len(units))]
            first_tile = [min(x for x, t in enumerate(tiles) if t[0] == u) for u in range(len(units))]

            def diag_in(j, q0, q1):
                return q0 <= j[1] < q1

            def pieces(n, j):
                q0, q1 = units[n][2], units[n][3]
                d = diag_in(j, q0, q1)
                return int(d) + int(j[3] - j[2] > int(d))
            wjob, wcount, pcount, jfirst = [], {}, [], []
            w = 0
            for n, j in jobs_all:
                w += pieces(n, j)
                wjob.append(w)
                wcount[n] = w
            done = 0
            for n, kt, js in tiles:
                jfirst.append(done)
                done += len(js)
                pcount.append(done)
            last_job = [[[j for j in unit[5] if j[0] == i][-1] for i in range(2)] for unit in units]

            with nc.Block() as block:
                @block.tensor
                def _(pe):
                    def maxima(u):
                        blk, h, q0, q1, s, jobs = units[u]
                        w = (q1 - q0) * P
                        for i in range(2):
                            pe.wait_ge(diag, 2 * u + i + 1)
                            if u >= 1 and i == 0:
                                pe.wait_ge(weighed, wcount[u - 1])
                                pe.wait_ge(masked, 2 * u)
                            nc.tensor.matmul(bank(i, w), ones[:, :], dg[i][:, 0:w], start=True, stop=True).then_inc(neg, 1)

                    def scores(x):
                        u, kt, js = tiles[x]
                        blk, h, q0, q1, s, jobs = units[u]
                        if x >= 4:
                            pe.wait_ge(product, pcount[x - 4])
                        p0 = HD * (h % 2)
                        lo, hi = min(j[2] for j in js), max(j[3] for j in js)
                        nc.tensor.matmul(bank(2 + x % 4, (hi - lo) * P, (lo - q0) * P), qkT[p0:p0 + HD, 2 + h // 2, kt * P:(kt + 1) * P],
                                         qkT[p0:p0 + HD, h // 2, lo * P:hi * P], start=True, stop=True).then_inc(scored, 1)

                    def values(x):
                        u, kt, js = tiles[x]
                        blk, h, q0, q1, s, jobs = units[u]
                        for y, j in enumerate(js):
                            n = jfirst[x] + y
                            pe.wait_ge(product, n + 1)
                            if x == first_tile[u] and u >= 1 and y == 0:
                                pe.wait_ge(taken, u)
                            i = j[0]
                            first_job = jobs.index(j) == min(jobs.index(k) for k in jobs if k[0] == i)
                            for q in range(j[2], j[3]):
                                mm = nc.tensor.matmul(bank(6 + i, HD + 1, (q - q0) * (HD + 1)), pr[n % RING][:, (q - q0) * P:(q - q0 + 1) * P],
                                                      v[:, kt, h, :], start=(first_job and q == j[2]), stop=(j is last_job[u][i] and q == j[3] - 1),
                                                      skip_group_check=True)
                            mm.then_inc(used, 1)

                    LEAD = 2
                    maxima(0)
                    for x in range(len(tiles) + LEAD):
                        if x < len(tiles):
                            if x >= 1 and tiles[x][0] != tiles[x - 1][0]:
                                maxima(tiles[x][0])
                            scores(x)
                        if x >= LEAD:
                            values(x - LEAD)
                    for t in range(nq):
                        pe.wait_ge(ready, t + 1)
                        if t >= 2:
                            pe.wait_ge(kept, t - 1)
                        else:
                            pe.wait_ge(product, len(jobs_all))
                        for c in range(2):
                            mm = nc.tensor.transpose(bank(2 + t % 2, P, c * P), hs[:, t, c * P:(c + 1) * P], ident)
                        mm.then_inc(turned, 1)

                @block.scalar
                def _(act):
                    n = 0
                    for x, (u, kt, js) in enumerate(tiles):
                        blk, h, q0, q1, s, jobs = units[u]
                        for j in js:
                            i = j[0]
                            act.wait_ge(neg, 2 * u + i + 1)
                            act.wait_ge(masked, 2 * u + i + 1)
                            if n >= 2:
                                act.wait_ge(product, n - 1)
                            ak = A[:, i, kt, h:h + 1]
                            lo, hi = (j[2] - q0) * P, (j[3] - q0) * P
                            if diag_in(j, q0, q1):
                                dlo = (kt - q0) * P
                                nc.scalar.activation(wt[n % 2][:, dlo:dlo + P], nmd[:, i, dlo:dlo + P], ACT.Exp, bias=ak).then_inc(weighed, 1)
                                if i == 0:
                                    lo = dlo + P
                                else:
                                    hi = dlo
                            if lo < hi:
                                nc.scalar.activation(wt[n % 2][:, lo:hi], bank(i, hi - lo, lo), ACT.Exp, bias=ak).then_inc(weighed, 1)
                            n += 1
                    for t in range(nq):
                        act.wait_ge(turned, t + 1)
                        nc.scalar.activation(yT[:, 4:6, t * P:(t + 1) * P], bank(2 + t % 2, 2 * P).rearrange("p (c t) -> p c t", c=2), ACT.Copy).then_inc(kept, 1)

                @block.vector
                def _(dve):
                    step = Chain(dve, step_s)

                    def diagonals(u):
                        blk, h, q0, q1, s, jobs = units[u]
                        nt = q1 - q0
                        for i in range(2):
                            if u >= 1:
                                dve.wait_ge(neg, 2 * u)
                            nc.vector.scalar_tensor_tensor(out=dg[i][:, 0:nt * P].rearrange("p (t m) -> p t m", t=nt),
                                                           in0=ident.unsqueeze(1).broadcast_to([P, nt, P]), scalar=-1.0,
                                                           in1=M[:, i, q0:q1, h:h + 1].broadcast_to([P, nt, P]),
                                                           op0=ALU.mult, op1=ALU.mult).then_inc(diag, 1)

                    def mask(u):
                        blk, h, q0, q1, s, jobs = units[u]
                        nt = q1 - q0
                        for i in range(2):
                            dve.wait_ge(neg, 2 * u + i + 1)
                            if u >= 1:
                                dve.wait_ge(weighed, wcount[u - 1])
                            m = cst[:, (C_MASK0, C_MASK1)[i]:(C_MASK0, C_MASK1)[i] + P].unsqueeze(1).broadcast_to([P, nt, P])
                            nc.vector.tensor_tensor(nmd[:, i, 0:nt * P].rearrange("p (t m) -> p t m", t=nt),
                                                    bank(i, nt * P).rearrange("p (t m) -> p t m", t=nt), m, ALU.add).then_inc(masked, 1)

                    def take(u):
                        blk, h, q0, q1, s, jobs = units[u]
                        nt = q1 - q0
                        dve.wait_ge(used, jobs_end[u])
                        pv = [bank(6 + i, nt * (HD + 1)).rearrange("p (t d) -> p t d", t=nt) for i in range(2)]
                        for i in range(2):
                            step.then(nc.vector.tensor_tensor(den[:, i, 0:nt].unsqueeze(2), pv[i][:, :, HD:HD + 1], EM[:, i, q0:q1, h:h + 1], ALU.max))
                        step.wait()
                        for i in range(2):
                            step.then(nc.vector.scalar_tensor_tensor(out=den[:, i, 0:nt].unsqueeze(2), in0=pv[i][:, :, HD:HD + 1], scalar=-1.0,
                                                                     in1=den[:, i, 0:nt].unsqueeze(2), op0=ALU.mult, op1=ALU.max))
                        step.wait()
                        step.then(nc.vector.reciprocal(den[:, :, 0:nt], den[:, :, 0:nt]))
                        step.wait()
                        for i in range(2):
                            step.then(nc.vector.tensor_tensor(ob[:, i, 0:nt, :], pv[i][:, :, 0:HD],
                                                              den[:, i, 0:nt].unsqueeze(2).broadcast_to([P, nt, HD]), ALU.mult))
                        step.wait()
                        nc.vector.tensor_tensor(hs[:, q0:q1, h * HD:(h + 1) * HD], ob[:, 0, 0:nt, :], ob[:, 1, 0:nt, :], ALU.add).then_inc(taken, 1)

                    diagonals(0)
                    mask(0)
                    n = 0
                    for x, (u, kt, js) in enumerate(tiles):
                        blk, h, q0, q1, s, jobs = units[u]
                        if x >= 1 and tiles[x - 1][0] != u:
                            mask(u)
                        for j in js:
                            lo, hi = (j[2] - q0) * P, (j[3] - q0) * P
                            dve.wait_ge(scored, x + 1)
                            dve.wait_ge(weighed, wjob[n])
                            if n >= RING:
                                dve.wait_ge(used, n - RING + 1)
                            nc.vector.scalar_tensor_tensor(out=pr[n % RING][:, lo:hi], in0=bank(2 + x % 4, hi - lo, lo), scalar=HD ** -0.5,
                                                           in1=wt[n % 2][:, lo:hi], op0=ALU.mult, op1=ALU.mult).then_inc(product, 1)
                            n += 1
                        if x + 1 < len(tiles) and tiles[x + 1][0] != u:
                            diagonals(u + 1)
                        if x + 1 == len(tiles) or tiles[x + 1][0] != u:
                            take(u)
                    dve.wait_ge(taken, len(units))
                    for t in range(nq):
                        hv = hs[:, t, :].rearrange("p (h d) -> p h d", h=H)
                        sqv = pr[t % 2][:, 0:GW]
                        step.then(nc.vector.tensor_tensor(sqv, hs[:, t, :], hs[:, t, :], ALU.mult))
                        step.wait()
                        nc.vector.tensor_reduce(ss[:, t, :], sqv.rearrange("p (h d) -> p h d", h=H), AX, ALU.add).then_inc(sums, 1)
                    for t in range(nq):
                        hv = hs[:, t, :].rearrange("p (h d) -> p h d", h=H)
                        dve.wait_ge(inv, 1)
                        step.then(nc.vector.tensor_tensor(hv, hv, ss[:, t, :].unsqueeze(2).broadcast_to([P, H, HD]), ALU.mult))
                        step.wait()
                        step.then(nc.vector.tensor_tensor(hv, hv, R["mlstm_g_out"].unsqueeze(1).broadcast_to([P, H, HD]), ALU.mult))
                        step.wait()
                        nc.vector.tensor_tensor(hs[:, t, :].rearrange("p (c d) -> p c d", c=2), hs[:, t, :].rearrange("p (c d) -> p c d", c=2), so(t), ALU.mult).then_inc(ready, 1)

                @block.gpsimd
                def _(pool):
                    pool.wait_ge(sums, nq)
                    f = ss[:, 0:nq, :].rearrange("p t h -> p (t h)")
                    nc.gpsimd.tensor_scalar(f, f, 1.0 / HD, EPS, ALU.mult, ALU.add).then_inc(pstep, 1)
                    pool.wait_ge(pstep, 1)
                    nc.gpsimd.tensor_tensor(f, f, half[:, 0:1].broadcast_to([P, nq * H]), ALU.pow).then_inc(inv, 1)
    for l in range(DEPTH):
        need = l < DEPTH - 1
        mine = BLOCKS if need else BLOCKS[:2]
        modulation(l)
        norm(l, 0, BLOCKS)
        clear_semaphores()
        st = ExitStack()
        with st:
            yT = sb(f"yT{l}", [P, DC, T], st)
            mixers(l, yT, need)
            add_product(f"out{l}", l, a["w_out"][l], DC, yT, 16, mine)
        norm(l, 1, mine)
        ffn(l, mine)
        clear_semaphores()
    leave()


_INS = ['x', 'c', 'ctx', 'c_ctx', 'w_mod', 'b_mod', 'g_norm1', 'g_norm2', 'w_in', 'w_out',
        'diff_g_q', 'diff_g_k', 'diff_lam', 'diff_g_out', 'mla_g_cq', 'mla_g_ckv', 'mla_w_uq', 'mla_w_ukv',
        'mla_g_q', 'mla_g_k', 'mlstm_w_conv', 'mlstm_b_i', 'mlstm_b_f', 'mlstm_g_out',
        'na_g_q', 'na_g_k', 'na_rpb', 'ffn_w_up', 'ffn_w_conv', 'ffn_w_down']


def kernel(**inputs):
    import concourse.bacc as bacc
    from concourse.bass_utils import run_bass_kernel_spmd

    nc = bacc.Bacc("TRN2", target_bir_lowering=False, num_devices=1)
    arrays, args = {}, {}
    for name in _INS:
        v = np.ascontiguousarray(inputs[name])
        arrays[f"in_{name}"] = v
        args[name] = nc.dram_tensor(f"in_{name}", v.shape, F32, kind="ExternalInput").ap()
    arrays["in_consts"] = shape_constants()
    args["consts"] = nc.dram_tensor("in_consts", (P, C_N), F32, kind="ExternalInput").ap()
    out = nc.dram_tensor("out", (1, SEQ, D), F32, kind="ExternalOutput").ap()
    build(nc, args, out)
    r = run_bass_kernel_spmd(nc, [arrays], core_ids=[0])
    return r.results[0]["out"]
```

```python
import math
from contextlib import ExitStack

import numpy as np
import concourse.bass as bass
from concourse import mybir

F32 = mybir.dt.float32
F32R = mybir.dt.float32r
ALU = mybir.AluOpType
ACT = mybir.ActivationFunctionType
AX = mybir.AxisListType.X

P = 128
D = 1024
DC = D // P
DEPTH = 2
SEQ = 1024
CTX = 256
T = SEQ + CTX
NT = T // P
LT = SEQ // P
H = 4
HD = 64
GW = H * HD
GRID_W = 64
DQK = 32
ROPE = 32
MQ = 256
MKV = 128
MD = 96
HID = 2816
HC = HID // P
WIN_R = 8
WIN_C = 16
NROW = SEQ // GRID_W
EPS = 1e-6
NEG = -1e30
BANK = 512

OFF = {}
_o = 0
for _n, _w in (("diff", 768), ("mla", 416), ("mlqk", 512), ("mlvo", 512), ("mlg", 16), ("na", 768)):
    OFF[_n] = _o
    _o += _w
IN_WIDTH = _o
BLOCKS = [(0, 512, 0), (512, 512, 0), (1024, 256, 1)]

V_BMOD, V_G1, V_G2, V_MCONV, V_GCQ, V_GCKV, V_N = 0, 48, 56, 64, 76, 78, 79
V_FCONV = V_N
V_TOTAL = V_N + 3 * 2 * HC
ROWS = {}
_o = 0
for _n, _w in (("diff_g_q", 32), ("diff_g_k", 32), ("diff_lam", 128), ("diff_g_out", 64), ("mla_g_q", 96),
               ("mla_g_k", 96), ("mlstm_g_out", 64), ("mlstm_b_i", 8), ("mlstm_b_f", 8), ("na_g_q", 64),
               ("na_g_k", 64)):
    ROWS[_n] = (_o, _w)
    _o += _w
ROWS_N = _o

C_ID, C_REV, C_CUM, C_CUMR, C_E127, C_MASK0, C_MASK1, C_COS, C_SIN, C_COL, C_PAIR, C_ROW = (
    0, 128, 256, 384, 512, 640, 768, 896, 896 + 256, 896 + 512, 896 + 512 + 64, 896 + 512 + 128)
C_N = C_ROW + 8 * 12
NSLOT = 18


def row_window(r):
    return min(max(r - WIN_R // 2, 0), NROW - WIN_R)


def pair_window(p):
    return row_window(4 * p) // 2, (row_window(4 * p + 3) + WIN_R + 1) // 2


def shape_constants():
    c = np.zeros((P, C_N), np.float32)
    i = np.arange(P)
    c[:, C_ID:C_ID + P] = np.eye(P)
    c[:, C_REV:C_REV + P] = np.eye(P)[::-1]
    c[:, C_CUM:C_CUM + P] = i[:, None] <= i[None, :]
    c[:, C_CUMR:C_CUMR + P] = i[:, None] >= i[None, :]
    c[P - 1, C_E127:C_E127 + P] = 1.0
    c[:, C_MASK0:C_MASK0 + P] = np.where(i[:, None] <= i[None, :], 0.0, NEG)
    c[:, C_MASK1:C_MASK1 + P] = np.where(i[:, None] >= i[None, :], 0.0, NEG)
    nf = ROPE // 4
    t = np.arange(SEQ)
    inv = (10000.0 ** (-np.arange(nf, dtype=np.float32) / nf)).astype(np.float32)
    ar = (t // GRID_W).astype(np.float32)[:, None] * inv
    ac = (t % GRID_W).astype(np.float32)[:, None] * inv
    cos = np.concatenate([np.cos(ar), np.cos(ar), np.cos(ac), np.cos(ac)], 1)
    sin = np.concatenate([-np.sin(ar), np.sin(ar), -np.sin(ac), np.sin(ac)], 1)
    c[:, C_COS:C_COS + 256] = cos.reshape(LT, P, 32).transpose(1, 0, 2).reshape(P, 256)
    c[:, C_SIN:C_SIN + 256] = sin.reshape(LT, P, 32).transpose(1, 0, 2).reshape(P, 256)
    q = i % GRID_W
    cs = np.clip(q - WIN_C // 2, 0, GRID_W - WIN_C)
    k = np.arange(GRID_W)
    c[:, C_COL:C_COL + 64] = np.where((k[None] >= cs[:, None]) & (k[None] < cs[:, None] + WIN_C), 0.0, NEG)
    c[:, C_PAIR:C_PAIR + HD] = np.concatenate([np.eye(HD), np.eye(HD)])
    for j in range(LT):
        row = 2 * j + i // GRID_W
        rs = np.array([row_window(r) for r in row])
        kr = 2 * pair_window(j // 2)[0] + np.arange(12)
        ok = (kr[None] >= rs[:, None]) & (kr[None] < rs[:, None] + WIN_R)
        c[:, C_ROW + 12 * j:C_ROW + 12 * j + 12] = np.where(ok, 0.0, NEG)
    return c


class Chain:

    def __init__(self, eng, sem):
        self.eng, self.sem, self.n = eng, sem, 0

    def then(self, ins):
        self.n += 1
        ins.then_inc(self.sem, 1)
        return self.n

    def wait(self, n=None):
        self.eng.wait_ge(self.sem, self.n if n is None else n)


def build(nc, a, out):
    ctx = ExitStack()
    with ctx:
        _build(nc, a, out, ctx)


def _build(nc, a, out, ctx):
    def sb(name, shape, stack=ctx):
        return stack.enter_context(nc.sbuf_tensor(name, shape, F32))

    def sbr(name, shape, stack=ctx):
        return stack.enter_context(nc.sbuf_tensor(name, shape, F32R))

    in_use = []

    def sem(name):
        in_use.append(nc.alloc_semaphore(name=name))
        return in_use[-1]

    def clear_semaphores():
        nc.clear_and_free_semaphores(in_use)
        in_use.clear()
        nc.all_engine_barrier()

    cst = sb("cst", [P, C_N])
    ones = sb("ones", [P, P])
    vec = sb("vec", [P, DEPTH, V_TOTAL])
    rows = sb("rows", [P, DEPTH, ROWS_N])
    mod = sb("mod", [P, 48, 2])
    scl = sb("scl", [P, 2, DC, 2])
    cc = sb("cc", [P, DC, 2])
    neglam = sb("neglam", [P, 2])
    half = sb("half", [P, 16])
    ps = ctx.enter_context(nc.psum_tensor("ps", [P, 8 * BANK], F32))
    rpb_pad = nc.dram_tensor("rpb_pad", [DEPTH, H, NSLOT + 1, 127], F32).ap()

    ident = cst[:, C_ID:C_ID + P]
    x_home = nc.dram_tensor("x_home", [P, DC, T], F32).ap()

    def take_x(stack, name):
        return stack.enter_context(nc.sbuf_tensor(name, [P, DC, T], F32, side="right"))

    def bank(b, n=BANK, w=0):
        return ps[:, b * BANK + w:b * BANK + w + n]

    def entry(xT):
        st = ExitStack()
        with st:
            xin = sb("xin", [P, NT, D], st)
            vrows = sb("vrows", [P, 2, 3, P], st)
            craw = sb("craw", [P, DC, 2], st)
            padz = sb("padz", [P, H, 127], st)
            s_x = [sem(f"x_loaded{i}") for i in range(2)]
            s_c = sem("constants_loaded")
            s_c2 = sem("rows_loaded")
            s_r = sem("rpb_loaded")
            s_rd = sem("rpb_written")
            s_ones = sem("ones_set")
            s_zero = sem("pad_zeroed")
            s_turn = sem("x_turned")
            s_kept = sem("x_kept")
            s_vt = sem("vectors_turned")
            s_vk = sem("vectors_kept")
            s_silu = sem("cond_ready")
            s_rows = sem("rows_scaled")
            s_lam = sem("lam_sums")
            with nc.Block() as block:
                @block.sync
                def _(sp):
                    sp.dma_start(cst[:, :], a["consts"]).then_inc(s_c, 16)
                    sp.dma_start(xin[:, 0:4, :], a["x"][0].rearrange("(t p) d -> p t d", p=P)[:, 0:4, :]).then_inc(s_x[0], 16)
                    sp.dma_start(xin[:, 4:8, :], a["x"][0].rearrange("(t p) d -> p t d", p=P)[:, 4:8, :]).then_inc(s_x[1], 16)
                    sp.dma_start(xin[:, 8:10, :], a["ctx"][0].rearrange("(t p) d -> p t d", p=P)).then_inc(s_x[1], 16)
                    sp.wait_ge(s_zero, 1)
                    for l in range(DEPTH):
                        sp.dma_start(padz[64 * l + 2:64 * l + 2 + 2 * WIN_R - 1, :, 48:79],
                                     a["na_rpb"][l].rearrange("h s w -> s h w")).then_inc(s_r, 16)
                    sp.wait_ge(s_r, 16 * DEPTH)
                    for l in range(DEPTH):
                        sp.dma_start(rpb_pad[l].rearrange("h s w -> s h w"),
                                     padz[64 * l:64 * l + NSLOT + 1, :, :]).then_inc(s_rd, 16)
                    sp.wait_ge(s_rd, 16 * DEPTH)

                @block.gpsimd
                def _(pool):
                    nc.gpsimd.memset(padz[:, :, :], 0.0).then_inc(s_zero, 1)
                    nc.gpsimd.memset(half[:, :], -0.5)
                    nc.gpsimd.memset(ones[:, :], 1.0).then_inc(s_ones, 1)

                @block.scalar
                def _(act):
                    n = 0
                    for l in range(DEPTH):
                        parts = [(a["b_mod"][l].rearrange("(r p) -> r p", p=P), 0, 48, 0),
                                 (a["g_norm1"][l].rearrange("(r p) -> r p", p=P), V_G1, 8, 0),
                                 (a["g_norm2"][l].rearrange("(r p) -> r p", p=P), V_G2, 8, 0),
                                 (a["mlstm_w_conv"][l].rearrange("k (r p) -> (k r) p", p=P), V_MCONV, 12, 0),
                                 (a["mla_g_cq"][l].rearrange("(r p) -> r p", p=P), V_GCQ, 2, 0),
                                 (a["mla_g_ckv"][l].rearrange("(r p) -> r p", p=P), V_GCKV, 1, 0),
                                 (a["ffn_w_conv"][l].rearrange("k (r p) -> (k r) p", p=P)[0:66], 0, 66, 1),
                                 (a["ffn_w_conv"][l].rearrange("k (r p) -> (k r) p", p=P)[66:132], 0, 66, 2)]
                        for src, r0, nr, j in parts:
                            act.dma_start(vrows[r0:r0 + nr, l, j, :], src).then_inc(s_c, 16)
                            n += 1
                        for name, (o, w) in ROWS.items():
                            src = a[name][l]
                            if len(src.shape) == 2:
                                src = src.rearrange("a b -> (a b)")
                            act.dma_start(rows[:, l, o:o + w], src.partition_broadcast(P)).then_inc(s_c2, 16)
                    act.dma_start(craw[:, :, 0], a["c"][0].rearrange("(c p) -> p c", p=P),
                                  allow_slow_non_contiguous=True).then_inc(s_c2, 16)
                    act.dma_start(craw[:, :, 1], a["c_ctx"].rearrange("(c p) -> p c", p=P),
                                  allow_slow_non_contiguous=True).then_inc(s_c2, 16)
                    act.wait_ge(s_c2, 16 * (DEPTH * len(ROWS) + 2))
                    nc.scalar.activation(cc[:, :, :], craw[:, :, :], ACT.Silu).then_inc(s_silu, 1)
                    act.wait_ge(s_silu, 1)

                @block.tensor
                def _(pe):
                    pe.wait_ge(s_c, 16 * (1 + 8 * DEPTH))
                    for l in range(DEPTH):
                        if l >= 1:
                            pe.wait_ge(s_vk, 3 * l)
                        for j, (nr, b) in enumerate(((V_N, 0), (66, 1), (66, 2))):
                            mm = nc.tensor.transpose(bank(b, nr), vrows[0:nr, l, j, :], ident[0:nr, 0:nr])
                        mm.then_inc(s_vt, 1)
                    n = 0
                    for t in range(NT):
                        if t == 0:
                            pe.wait_ge(s_x[0], 16)
                        if t == 4:
                            pe.wait_ge(s_x[1], 32)
                        for g in range(2):
                            if n >= 4:
                                pe.wait_ge(s_kept, n - 3)
                            for c in range(4):
                                mm = nc.tensor.transpose(bank(4 + n % 4, P, c * P), xin[:, t, (4 * g + c) * P:(4 * g + c + 1) * P], ident)
                            mm.then_inc(s_turn, 1)
                            n += 1

                @block.vector
                def _(dve):
                    for l in range(DEPTH):
                        dve.wait_ge(s_vt, l + 1)
                        for j, (nr, o) in enumerate(((V_N, 0), (66, V_N), (66, V_N + 66))):
                            nc.vector.tensor_copy(vec[:, l, o:o + nr], bank(j, nr)).then_inc(s_vk, 1)
                    n = 0
                    for t in range(NT):
                        for g in range(2):
                            dve.wait_ge(s_turn, n + 1)
                            nc.vector.tensor_copy(xT[:, 4 * g:4 * g + 4, t * P:(t + 1) * P],
                                                  bank(4 + n % 4).rearrange("p (c t) -> p c t", c=4)).then_inc(s_kept, 1)
                            n += 1
                    dve.wait_ge(s_c2, 16 * (DEPTH * len(ROWS) + 2))
                    for l in range(DEPTH):
                        lam0 = 0.8 - 0.6 * math.exp(-0.3 * l)
                        for name, f in (("diff_g_q", DQK ** -0.5), ("diff_g_out", 1.0 - lam0),
                                        ("mla_g_q", MD ** -0.5), ("na_g_q", HD ** -0.5)):
                            o, w = ROWS[name]
                            nc.vector.tensor_scalar(rows[:, l, o:o + w], rows[:, l, o:o + w], f, None, ALU.mult).then_inc(s_rows, 1)
                    dve.wait_ge(s_rows, 8)
            return

    x_stack = ExitStack()
    xT = take_x(x_stack, "x0")
    entry(xT)
    clear_semaphores()
    def modulation(l, xT):
        st = ExitStack()
        CH = 6 * D // 512
        with st:
            wm = [sb(f"wm{i}_{l}", [P, DC, 512], st) for i in range(2)]
            row = [sb(f"row{i}_{l}", [P, 512], st) for i in range(2)]
            lv = sb(f"lv{l}", [P, 2, 32], st)
            ls = sb(f"ls{l}", [P, 2], st)
            w_in = [sem(f"mod_w{i}_{l}") for i in range(2)]
            w_used, rkept = sem(f"mod_w_used{l}"), sem(f"mod_row_kept{l}")
            turned, done = sem(f"mod_turned{l}"), sem(f"mod_kept{l}")
            lam = sem(f"lam{l}")
            lame = sem(f"lame{l}")
            x_back = sem(f"mod_x_back{l}")
            w = a["w_mod"][l].rearrange("(c p) n -> p c n", p=P)
            with nc.Block() as block:
                @block.sync
                def _(sp):
                    for i in range(2):
                        sp.dma_start(wm[i][:, :, :], w[:, :, i * 512:(i + 1) * 512]).then_inc(w_in[i], 16)
                    with sp.Fori(0, CH // 2 - 1) as n:
                        for i in range(2):
                            sp.wait_ge(w_used, n * 2 + (i + 1))
                            sp.dma_start(wm[i][:, :, :], w[:, :, bass.ds(n * 1024 + (1024 + 512 * i), 512)]).then_inc(w_in[i], 16)
                    if l > 0:
                        sp.dma_start(xT[:, :, :], x_home).then_inc(x_back, 16)
                        sp.wait_ge(x_back, 16)

                @block.tensor
                def _(pe):
                    def rows_of(i, t, n):
                        pe.wait_ge(w_in[i], n * 16 + 16)
                        pe.wait_ge(rkept, t + 1)
                        for c in range(DC):
                            mm = nc.tensor.matmul(bank(i)[0:2, :], cc[:, c, :], wm[i][:, c, :], start=(c == 0), stop=(c == DC - 1))
                        mm.then_inc(w_used, 1)

                    def turn(i, t):
                        pe.wait_ge(rkept, t + 3)
                        pe.wait_ge(done, t + 1)
                        for f in range(4):
                            mm = nc.tensor.matmul(bank(2 + i, 2, 2 * f), row[i][0:2, f * P:(f + 1) * P], ident[0:2, 0:2], start=True, stop=True)
                        mm.then_inc(turned, 1)

                    rows_of(0, 0, 0)
                    with pe.Fori(0, CH // 2 - 1) as n:
                        rows_of(1, n * 2 + 1, n)
                        turn(0, n * 2)
                        rows_of(0, n * 2 + 2, n + 1)
                        turn(1, n * 2 + 1)
                    rows_of(1, CH - 1, CH // 2 - 1)
                    turn(0, CH - 2)
                    turn(1, CH - 1)

                @block.vector
                def _(dve):
                    dve.sem_inc(done, 2)
                    with dve.Fori(0, CH // 2) as n:
                        for i in range(2):
                            dve.wait_ge(turned, n * 2 + (i + 3))
                            b = vec[:, l, bass.ds(n * 8 + 4 * i, 4)].unsqueeze(2).broadcast_to([P, 4, 2])
                            nc.vector.tensor_tensor(mod[:, bass.ds(n * 8 + 4 * i, 4), :],
                                                    bank(2 + i, 8).rearrange("p (f s) -> p f s", s=2), b, ALU.add).then_inc(done, 1)
                    dve.wait_ge(done, 14)
                    for k, (sc, g) in enumerate(((8, V_G1), (32, V_G2))):
                        gb = vec[:, l, g:g + DC].unsqueeze(2).broadcast_to([P, DC, 2])
                        nc.vector.scalar_tensor_tensor(out=scl[:, k, :, :], in0=mod[:, sc:sc + DC, :], scalar=1.0, in1=gb,
                                                       op0=ALU.add, op1=ALU.mult).then_inc(done, 1)
                    o, _w = ROWS["diff_lam"]
                    v = rows[:, l, o:o + 128].rearrange("p (a b d) -> p a b d", a=2, b=2)
                    nc.vector.tensor_tensor(lv[:, :, :], v[:, :, 0, :], v[:, :, 1, :], ALU.mult).then_inc(lam, 1)
                    dve.wait_ge(lam, 1)
                    nc.vector.tensor_reduce(ls[:, :], lv[:, :, :], AX, ALU.add).then_inc(lam, 1)
                    dve.wait_ge(lame, 1)
                    nc.vector.scalar_tensor_tensor(out=neglam[:, 0:1], in0=ls[:, 1:2], scalar=-(0.8 - 0.6 * math.exp(-0.3 * l)),
                                                   in1=ls[:, 0:1], op0=ALU.add, op1=ALU.subtract).then_inc(lam, 1)
                    dve.wait_ge(lam, 3)

                @block.scalar
                def _(act):
                    act.sem_inc(rkept, 2)
                    act.sem_inc(turned, 2)
                    with act.Fori(0, CH // 2) as n:
                        for i in range(2):
                            act.wait_ge(w_used, n * 2 + (i + 1))
                            act.wait_ge(turned, n * 2 + (i + 1))
                            nc.scalar.activation(row[i][0:2, :], bank(i)[0:2, :], ACT.Copy).then_inc(rkept, 1)
                    act.wait_ge(lam, 2)
                    nc.scalar.activation(ls[:, :], ls[:, :], ACT.Exp).then_inc(lame, 1)

    def norm(l, k, blocks, xT, dst, spill):
        st = ExitStack()
        split = len(dst) == 2
        with st:
            sq = [sb(f"sq{i}_{l}{k}", [P, DC, 512], st) for i in range(2)]
            rs = [sb(f"rs{i}_{l}{k}", [P, 512], st) for i in range(2)]
            squared, summed, mean, root, inv, normed, high, low, ready, spilled = (
                sem(f"{n}{l}{k}") for n in ("squared", "summed", "mean", "root", "inv", "normed", "h_high", "h_low", "h_ready", "x_spilled"))
            sh = 24 * k

            def scaled(i, c):
                t0, n, s = blocks[i]
                return sq[i % 2][:, c, 0:n] if split else dst[0][:, c, t0:t0 + n]

            with nc.Block() as block:
                @block.sync
                def _(sp):
                    if spill:
                        sp.dma_start(x_home, xT[:, :, :]).then_inc(spilled, 16)
                        sp.wait_ge(spilled, 16)

                @block.tensor
                def _(pe):
                    for i, (t0, n, s) in enumerate(blocks):
                        for c in range(DC):
                            pe.wait_ge(squared, DC * i + c + 1)
                            mm = nc.tensor.matmul(bank(i, n), ones[:, :], sq[i % 2][:, c, 0:n], start=(c == 0), stop=(c == DC - 1))
                        mm.then_inc(summed, 1)

                @block.scalar
                def _(act):
                    def squares(i):
                        t0, n, s = blocks[i]
                        if i >= 2:
                            act.wait_ge(summed, i - 1)
                            if split:
                                act.wait_ge(low, DC * (i - 1))
                        for c in range(DC):
                            nc.scalar.activation(sq[i % 2][:, c, 0:n], xT[:, c, t0:t0 + n], ACT.Square).then_inc(squared, 1)
                    squares(0)
                    for i, (t0, n, s) in enumerate(blocks):
                        if i + 1 < len(blocks):
                            squares(i + 1)
                        act.wait_ge(mean, i + 1)
                        nc.scalar.activation(rs[i % 2][:, 0:n], rs[i % 2][:, 0:n], ACT.Sqrt).then_inc(root, 1)
                        for c in range(DC):
                            act.wait_ge(normed, DC * i + c + 1)
                            x = scaled(i, c)
                            by = dict(bias=mod[:, sh + c, s:s + 1], scale=scl[:, k, c, s:s + 1])
                            if split:
                                nc.scalar.activation(dst[0][:, c, t0:t0 + n], x, ACT.Identity, **by).then_inc(high, 1)
                                act.wait_ge(high, DC * i + c + 1)
                            nc.scalar.activation(x, x, ACT.Identity, **by).then_inc(ready, 1)

                @block.gpsimd
                def _(pool):
                    if split:
                        for i, (t0, n, s) in enumerate(blocks):
                            for c in range(DC):
                                pool.wait_ge(ready, DC * i + c + 1)
                                nc.gpsimd.tensor_tensor(dst[1][:, c, t0:t0 + n], scaled(i, c), dst[0][:, c, t0:t0 + n].bitcast(F32),
                                                        ALU.subtract).then_inc(low, 1)

                @block.vector
                def _(dve):
                    for i, (t0, n, s) in enumerate(blocks):
                        dve.wait_ge(summed, i + 1)
                        if i >= 2:
                            dve.wait_ge(normed, DC * (i - 1))
                        nc.vector.tensor_scalar(rs[i % 2][:, 0:n], bank(i, n), 1.0 / D, EPS, ALU.mult, ALU.add).then_inc(mean, 1)
                        dve.wait_ge(root, i + 1)
                        nc.vector.reciprocal(rs[i % 2][:, 0:n], rs[i % 2][:, 0:n]).then_inc(inv, 1)
                        dve.wait_ge(inv, i + 1)
                        for c in range(DC):
                            nc.vector.tensor_tensor(scaled(i, c), xT[:, c, t0:t0 + n], rs[i % 2][:, 0:n],
                                                    ALU.mult).then_inc(normed, 1)

    def add_product(tag, l, w, kc, src, gate, blocks, xT, reload=False):
        st = ExitStack()
        with st:
            wb = [sb(f"wb{i}_{tag}", [P, kc, P], st) for i in range(2)]
            loaded = [sem(f"w_loaded{i}_{tag}") for i in range(2)]
            multiplied = sem(f"multiplied_{tag}")
            added = sem(f"added_{tag}")
            nb = len(blocks)
            x_back = sem(f"x_back_{tag}")
            wv = w.rearrange("(k p) n -> p k n", p=P)
            with nc.Block() as block:
                @block.sync
                def _(sp):
                    if reload:
                        sp.dma_start(xT[:, :, :], x_home).then_inc(x_back, 16)
                    for i in range(2):
                        sp.dma_start(wb[i][:, :, :], wv[:, :, i * P:(i + 1) * P]).then_inc(loaded[i], 16)
                    with sp.Fori(0, DC // 2 - 1) as n:
                        for i in range(2):
                            sp.wait_ge(multiplied, n * (2 * nb) + nb * (i + 1))
                            sp.dma_start(wb[i][:, :, :], wv[:, :, bass.ds(n * (2 * P) + (2 + i) * P, P)]).then_inc(loaded[i], 16)

                @block.tensor
                def _(pe):
                    with pe.Fori(0, DC // 2) as n:
                        for i in range(2):
                            pe.wait_ge(loaded[i], n * 16 + 16)
                            for j, (t0, m, s) in enumerate(blocks):
                                pe.wait_ge(added, n * (2 * nb) + (nb * i + j + 1))
                                for k in range(kc):
                                    mm = nc.tensor.matmul(bank(3 * i + j, m), wb[i][:, k, :], src[:, k, t0:t0 + m],
                                                          start=(k == 0), stop=(k == kc - 1))
                                mm.then_inc(multiplied, 1)

                @block.vector
                def _(dve):
                    dve.sem_inc(added, 2 * nb)
                    if reload:
                        dve.wait_ge(x_back, 16)
                    with dve.Fori(0, DC // 2) as n:
                        for i in range(2):
                            for j, (t0, m, s) in enumerate(blocks):
                                dve.wait_ge(multiplied, n * (2 * nb) + (nb * i + j + 1))
                                x = xT[:, bass.ds(n * 2 + i, 1), t0:t0 + m]
                                nc.vector.scalar_tensor_tensor(out=x, in0=bank(3 * i + j, m).unsqueeze(1),
                                                               scalar=mod[:, bass.ds(n * 2 + (gate + i), 1), s],
                                                               in1=x, op0=ALU.mult, op1=ALU.add).then_inc(added, 1)

    def ffn(l, blocks, hh, hl):
        st = ExitStack()
        sizes = [6, 6, 5, 5]
        assert sum(sizes) == HC
        ctx_too = len(blocks) == 3
        nb = len(blocks)
        width = T + 4
        span = (T + 2) if ctx_too else SEQ
        with st:
            wr = [sb(f"wr{i}_{l}", [P, DC, P], st) for i in range(2)]
            wh = [sbr(f"wh{i}_{l}", [P, DC, P], st) for i in range(2)]
            wl = [sbr(f"wl{i}_{l}", [P, DC, P], st) for i in range(2)]
            u = [sb(f"u{i}_{l}", [P, width], st) for i in range(2)]
            cv = [sb(f"cv{i}_{l}", [P, width], st) for i in range(2)]
            ah, al = sbr(f"ah_{l}", [P, max(sizes), T], st), sbr(f"al_{l}", [P, max(sizes), T], st)
            xs = sb(f"xs_{l}", [P, T], st)
            loaded, multiplied, high, low = ([sem(f"up_{n}{i}_{l}") for i in range(2)] for n in ("loaded", "mult", "w_high", "w_low"))
            copied, tap0, tap1, conv = ([sem(f"up_{n}{i}_{l}") for i in range(2)] for n in ("copied", "tap0_", "tap1_", "conv"))
            zeroed, silu, gated, acts = (sem(f"up_{n}_{l}") for n in ("zeroed", "silu", "gated", "acts"))
            a_high = sem(f"up_a_high_{l}")
            added = [sem(f"added{i}_down{l}") for i in range(2)]
            x_in, x_out = ([sem(f"{n}{j}_down{l}") for j in range(nb)] for n in ("x_in", "x_out"))
            wu = a["ffn_w_up"][l].rearrange("(c p) n -> p c n", p=P)
            wd = a["ffn_w_down"][l].rearrange("(k p) n -> p k n", p=P)
            first = [sum(sizes[:g]) for g in range(len(sizes))]
            use = [first[g] + DC // 2 * g for g in range(len(sizes))]
            groups = list(enumerate(sizes))
            last = len(sizes) - 1
            with nc.Block() as block:
                @block.sync
                def _(sp):
                    def load_up(i, n):
                        sp.dma_start(wr[i][:, :, :], wu[:, :, bass.ds(n * P + i * HID, P)]).then_inc(loaded[i], 16)

                    def load_down(i, g, n):
                        k = sizes[g]
                        sp.dma_start(wr[i][:, 0:k, :], wd[:, first[g]:first[g] + k, bass.ds(n * (2 * P) + i * P, P)]).then_inc(loaded[i], 16)

                    def bring_x(j, m):
                        t0, w, s = blocks[j]
                        sp.dma_start(xs[:, t0:t0 + w].unsqueeze(1), x_home[:, bass.ds(m, 1), t0:t0 + w]).then_inc(x_in[j], 16)

                    def store_x(i, g, n):
                        for j, (t0, w, s) in enumerate(blocks):
                            sp.wait_ge(added[i], n * nb + (nb * (4 * g + 1) + j + 1))
                            sp.dma_start(x_home[:, bass.ds(n * 2 + i, 1), t0:t0 + w], xs[:, t0:t0 + w].unsqueeze(1)).then_inc(x_out[j], 16)

                    def next_x(i, g, n, m):
                        for j in range(nb):
                            sp.wait_ge(x_out[j], n * 32 + 16 * (DC * g + i + 1))
                            bring_x(j, m)

                    for i in range(2):
                        load_up(i, 0)
                    for j in range(nb):
                        bring_x(j, 0)
                    for g, size in groups:
                        with sp.Fori(0, size - 1) as n:
                            for i in range(2):
                                sp.wait_ge(low[i], n + (use[g] + 1))
                                load_up(i, n + (first[g] + 1))
                        for i in range(2):
                            sp.wait_ge(low[i], use[g] + size)
                            load_down(i, g, 0)
                        with sp.Fori(0, DC // 2 - 1) as n:
                            for i in range(2):
                                sp.wait_ge(low[i], n + (use[g] + size + 1))
                                load_down(i, g, n + 1)
                                store_x(i, g, n)
                                next_x(i, g, n, n * 2 + (i + 1))
                        for i in range(2):
                            if g < last:
                                sp.wait_ge(low[i], use[g + 1])
                                load_up(i, first[g + 1])
                            store_x(i, g, DC // 2 - 1)
                            if i == 0:
                                next_x(i, g, DC // 2 - 1, DC - 1)
                            elif g < last:
                                next_x(i, g, DC // 2 - 1, 0)
                    for j in range(nb):
                        sp.wait_ge(x_out[j], 16 * DC * len(sizes))

                @block.tensor
                def _(pe):
                    def passes(i, j, src_h, src_l, ks, k_first, k_last):
                        t0, w, s = blocks[j]
                        for k in ks:
                            for x, (ww, src) in enumerate(((wh, src_h), (wh, src_l), (wl, src_h))):
                                mm = nc.tensor.matmul(bank(3 * i + j, w), ww[i][:, k, :], src[:, k, t0:t0 + w],
                                                      start=(k == k_first and x == 0), stop=(k == k_last and x == 2))
                        return mm

                    def hidden(i, g, n):
                        pe.wait_ge(low[i], n + (use[g] + 1))
                        pe.wait_ge(copied[i], n * 2 + (2 * first[g] + 1))
                        for j in range(nb):
                            passes(i, j, hh, hl, range(DC), 0, DC - 1).then_inc(multiplied[i], 1)

                    def output(i, g, n):
                        k = sizes[g]
                        pe.wait_ge(low[i], n + (use[g] + k + 1))
                        for j in range(nb):
                            pe.wait_ge(added[i], n * nb + (nb * 4 * g + j + 1))
                            passes(i, j, ah, al, range(k), 0, k - 1).then_inc(multiplied[i], 1)

                    for g, size in groups:
                        if g:
                            for i in range(2):
                                pe.wait_ge(added[i], nb * (4 * g + 1))
                        with pe.Fori(0, size) as n:
                            for i in range(2):
                                hidden(i, g, n)
                        pe.wait_ge(acts, nb * (first[g] + size))
                        for i in range(2):
                            pe.wait_ge(low[i], use[g] + size + 1)
                            pe.wait_ge(copied[i], 2 * (first[g] + size) + 1)
                            for j in range(nb):
                                passes(i, j, ah, al, range(size - 1), 0, size - 1)
                        pe.wait_ge(acts, nb * (first[g] + size + 1))
                        for i in range(2):
                            for j in range(nb):
                                passes(i, j, ah, al, [size - 1], 0, size - 1).then_inc(multiplied[i], 1)
                        with pe.Fori(0, DC // 2 - 1) as n:
                            for i in range(2):
                                output(i, g, n + 1)

                @block.scalar
                def _(act):
                    def split(i, r):
                        act.wait_ge(loaded[i], r * 16 + 16)
                        if not (isinstance(r, int) and r == 0):
                            act.wait_ge(multiplied[i], r * nb)
                        nc.scalar.activation(wh[i][:, :, :], wr[i][:, :, :], ACT.Copy).then_inc(high[i], 1)

                    def leave_banks(i, g, n):
                        act.wait_ge(multiplied[i], n * nb + nb * (use[g] + 1))
                        act.wait_ge(conv[i], n + (first[g] + 1))
                        nc.scalar.activation(u[i][:, 1:1 + SEQ], bank(3 * i, SEQ), ACT.Copy).then_inc(copied[i], 1)
                        src = bank(3 * i + 2, CTX) if ctx_too else bank(3 * i + 1, 1, 511)
                        dst = u[i][:, SEQ + 3:SEQ + 3 + CTX] if ctx_too else cv[i][:, width - 1:width]
                        nc.scalar.activation(dst, src, ACT.Copy).then_inc(copied[i], 1)

                    for i in range(2):
                        split(i, 0)
                    act.wait_ge(zeroed, 2)
                    for i in range(2):
                        act.sem_inc(copied[i], 1)
                    for g, size in groups:
                        with act.Fori(0, size) as n:
                            for i in range(2):
                                leave_banks(i, g, n)
                                split(i, n + (use[g] + 1))
                            act.wait_ge(conv[1], n + (first[g] + 2))
                            nc.scalar.activation(cv[1][:, 0:span], cv[1][:, 0:span], ACT.Silu).then_inc(silu, 1)
                        with act.Fori(0, DC // 2 - (g == last)) as n:
                            for i in range(2):
                                split(i, n + (use[g] + size + 1))

                @block.gpsimd
                def _(pool):
                    nc.gpsimd.memset(u[0][:, :], 0.0).then_inc(zeroed, 1)
                    nc.gpsimd.memset(u[1][:, :], 0.0).then_inc(zeroed, 1)
                    with pool.Fori(0, HC + DC // 2 * len(sizes)) as r:
                        for i in range(2):
                            pool.wait_ge(high[i], r + 1)
                            nc.gpsimd.tensor_tensor(wl[i][:, :, :], wr[i][:, :, :], wh[i][:, :, :].bitcast(F32), ALU.subtract).then_inc(low[i], 1)

                @block.vector
                def _(dve):
                    for i in range(2):
                        dve.sem_inc(conv[i], 1)
                        dve.sem_inc(added[i], nb)
                    dve.sem_inc(acts, nb)

                    def hidden(g, n):
                        c = n + first[g]
                        for i in range(2):
                            def w(k):
                                return vec[:, l, bass.ds(n + (V_FCONV + k * 2 * HC + i * HC + first[g]), 1)]
                            dve.wait_ge(copied[i], c * 2 + 3)
                            if i == 0:
                                dve.wait_ge(acts, c * nb + nb)
                            nc.vector.tensor_scalar(cv[i][:, 0:span], u[i][:, 0:span], w(0), None, ALU.mult).then_inc(tap0[i], 1)
                            dve.wait_ge(tap0[i], c + 1)
                            nc.vector.scalar_tensor_tensor(out=cv[i][:, 0:span], in0=u[i][:, 1:1 + span], scalar=w(1),
                                                           in1=cv[i][:, 0:span], op0=ALU.mult, op1=ALU.add).then_inc(tap1[i], 1)
                            dve.wait_ge(tap1[i], c + 1)
                            nc.vector.scalar_tensor_tensor(out=cv[i][:, 0:span], in0=u[i][:, 2:2 + span], scalar=w(2),
                                                           in1=cv[i][:, 0:span], op0=ALU.mult, op1=ALU.add).then_inc(conv[i], 1)
                        dve.wait_ge(silu, c + 1)
                        nc.vector.tensor_tensor(cv[0][:, 0:span], cv[0][:, 0:span], cv[1][:, 0:span], ALU.mult).then_inc(gated, 1)
                        dve.wait_ge(gated, c + 1)
                        for t0, m, s in blocks:
                            o = t0 + 2 * s
                            nc.vector.tensor_copy(ah[:, bass.ds(n, 1), t0:t0 + m], cv[0][:, o:o + m].unsqueeze(1)).then_inc(a_high, 1)
                        for j, (t0, m, s) in enumerate(blocks):
                            o = t0 + 2 * s
                            dve.wait_ge(a_high, c * nb + (j + 1))
                            nc.vector.tensor_tensor(al[:, bass.ds(n, 1), t0:t0 + m], cv[0][:, o:o + m].unsqueeze(1),
                                                    ah[:, bass.ds(n, 1), t0:t0 + m].bitcast(F32), ALU.subtract).then_inc(acts, 1)

                    def add(i, g, n):
                        for j, (t0, m, s) in enumerate(blocks):
                            dve.wait_ge(multiplied[i], n * nb + (nb * (use[g] + sizes[g]) + j + 1))
                            dve.wait_ge(x_in[j], n * 32 + 16 * (DC * g + i + 1))
                            nc.vector.scalar_tensor_tensor(out=xs[:, t0:t0 + m], in0=bank(3 * i + j, m),
                                                           scalar=mod[:, bass.ds(n * 2 + (40 + i), 1), s],
                                                           in1=xs[:, t0:t0 + m], op0=ALU.mult, op1=ALU.add).then_inc(added[i], 1)

                    for g, size in groups:
                        with dve.Fori(0, size) as n:
                            hidden(g, n)
                        with dve.Fori(0, DC // 2) as n:
                            for i in range(2):
                                add(i, g, n)

    def leave(xT):
        st = ExitStack()
        with st:
            xo = [sb(f"xo{i}", [P, D], st) for i in range(4)]
            turned = sem("out_turned")
            kept = sem("out_kept")
            stored = [sem(f"out_stored{i}") for i in range(4)]
            back = [sem(f"out_x_back{i}") for i in range(LT // 2)]
            with nc.Block() as block:
                @block.scalar
                def _(act):
                    for i in range(LT // 2):
                        act.dma_start(xT[:, :, 2 * i * P:(2 * i + 2) * P], x_home[:, :, 2 * i * P:(2 * i + 2) * P]).then_inc(back[i], 16)

                @block.tensor
                def _(pe):
                    n = 0
                    for t in range(LT):
                        pe.wait_ge(back[t // 2], 16)
                        for g in range(2):
                            if n >= 8:
                                pe.wait_ge(kept, n - 7)
                            for c in range(4):
                                mm = nc.tensor.transpose(bank(n % 8, P, c * P), xT[:, 4 * g + c, t * P:(t + 1) * P], ident)
                            mm.then_inc(turned, 1)
                            n += 1

                @block.vector
                def _(dve):
                    for n in range(2 * LT):
                        dve.wait_ge(turned, n + 1)
                        if n >= 8 and n % 2 == 0:
                            dve.wait_ge(stored[(n // 2) % 4], 16 * (n // 8))
                        nc.vector.tensor_copy(xo[(n // 2) % 4][:, (n % 2) * 512:(n % 2) * 512 + 512], bank(n % 8)).then_inc(kept, 1)

                @block.sync
                def _(sp):
                    for t in range(LT):
                        sp.wait_ge(kept, 2 * t + 2)
                        sp.dma_start(out[0, t * P:(t + 1) * P, :], xo[t % 4][:, :]).then_inc(stored[t % 4], 16)
                    for i in range(4):
                        sp.wait_ge(stored[i], 32)

    def attention(tag, l, heads, maps, parts, keys, vs, yT, y0, out_gain=None, table=None, need=True):
        st = ExitStack()
        pairs = list(range(NT // 2 if need else LT // 2))
        nh = len(heads)
        with st:
            width = max(len(keys(p)) for p in pairs) * P
            units = [(p, h, s) for p in pairs for h in range(nh) for s in range(2)]
            nu, nv = len(units), len(units) // 2
            e = [[sb(f"e{m}{i}_{tag}", [P, width], st) for i in range(2)] for m in range(maps)]
            hi = sbr(f"hi_{tag}", [P, width // P, 2 * P], st)
            lo = sbr(f"lo_{tag}", [P, width // P, 2 * P], st)
            mx, nm, zs = (sb(f"{n}_{tag}", [P, 4], st) for n in ("mx", "nm", "zs"))
            rz, rw = sb(f"rz_{tag}", [P, 8], st), sb(f"rw_{tag}", [P, 8], st)
            oT = sb(f"oT_{tag}", [P, 2 * P], st)
            o = [sb(f"o{i}_{tag}", [P, 2, nh * HD], st) for i in range(2)]
            osq, oss = sb(f"osq_{tag}", [P, 2 * nh * HD], st), sb(f"oss_{tag}", [P, 2, 2 * nh], st)
            scored, maxed, expd, probs = (sem(f"{n}_{tag}") for n in ("scored", "maxed", "expd", "probs"))
            turned, moved, split, summed = (sem(f"{n}_{tag}") for n in ("turned", "moved", "split", "summed"))
            okept, added, taken = (sem(f"{n}_{tag}") for n in ("o_kept", "added", "taken"))
            finished, oturned, ykept = (sem(f"{n}_{tag}") for n in ("finished", "o_turned", "y_kept"))
            osums, oinv, step_s, pstep, biased = (sem(f"{n}_{tag}") for n in ("o_sums", "o_inv", "dve_step", "pool_step", "biased"))
            bb = [sb(f"bb{i}_{tag}", [P, width], st) for i in range(2)] if table else None

            def nkeys(u):
                return len(keys(units[u][0]))

            def segments(p):
                out, col = [], 0
                for kt in keys(p):
                    if out and out[-1][0] + out[-1][1] == kt * P and col % BANK:
                        out[-1][1] += P
                    else:
                        out.append([kt * P, P, col])
                    col += P
                return out

            def batches(u):
                return [(k, min(4, nkeys(u) - k)) for k in range(0, nkeys(u), 4)]

            nb = [0]
            for u in range(nu):
                nb.append(nb[-1] + len(batches(u)))
            STEPS = nu + 5

            def sum_at(n):
                v = (n - 2) // 2
                return v if n % 2 == 0 and 0 <= v < nv else None

            def out_at(n):
                g = (n - 4) // (2 * nh) - 1
                return g if (n - 4) % (2 * nh) == 0 and 0 <= g < len(pairs) else None
            turns, where = [], {}
            for n in range(STEPS):
                if sum_at(n) is not None:
                    where["sum", sum_at(n)] = len(turns)
                    turns.append((taken, sum_at(n) + 1))
                if n < nu:
                    for b in range(len(batches(n))):
                        where["turn", n, b] = len(turns)
                        turns.append((split, nb[n] + b + 1))
                    if n % 2:
                        where["values", n // 2] = len(turns)
                        turns.append((okept, n // 2 + 1))
                if out_at(n) is not None:
                    where["out", out_at(n)] = len(turns)
                    turns.append((ykept, out_at(n) + 1))

            def turn_bank(*key):
                return 6 + where[key] % 2

            def score_bank(u, m):
                return 3 * (m if maps == 2 else u % 2)

            with nc.Block() as block:
                @block.tensor
                def _(pe):
                    def my_turn(*key):
                        if where[key] >= 2:
                            pe.wait_ge(*turns[where[key] - 2])
                        return turn_bank(*key)

                    def scores(u):
                        p, h, s = units[u]
                        if maps == 2 and u >= 1:
                            pe.wait_ge(expd, 2 * u)
                        if maps == 1 and u >= 2:
                            pe.wait_ge(expd, u - 1)
                        q0 = (2 * p + s) * P
                        for m in range(maps):
                            pr = parts(h, m)
                            for k0, n, col in segments(p):
                                for i, (q, k) in enumerate(pr):
                                    mm = nc.tensor.matmul(bank(score_bank(u, m), n, col), q[:, q0:q0 + P], k[:, k0:k0 + n],
                                                          start=(i == 0), stop=(i == len(pr) - 1))
                            mm.then_inc(scored, 1)

                    def turn(u):
                        pe.wait_ge(probs, u + 1)
                        for b, (k0, n) in enumerate(batches(u)):
                            tb = my_turn("turn", u, b)
                            for k in range(n):
                                mm = nc.tensor.transpose(bank(tb, P, k * P), e[0][u % 2][:, (k0 + k) * P:(k0 + k + 1) * P], ident)
                            mm.then_inc(turned, 1)

                    def values(v):
                        p, h, s = units[2 * v]
                        tb = my_turn("values", v)
                        kts = keys(p)
                        for i, part in enumerate((hi, lo)):
                            pe.wait_ge(*((moved, nb[2 * v + 2]), (split, nb[2 * v + 2]))[i])
                            for k, kt in enumerate(kts):
                                mm = nc.tensor.matmul(bank(tb, 2 * P), vs[:, kt, h, :], part[:, k, :],
                                                      start=(i == 0 and k == 0), stop=(i == 1 and k == len(kts) - 1))
                        mm.then_inc(summed, 1)

                    def add_parts(v):
                        tb = my_turn("sum", v)
                        pe.wait_ge(okept, v + 1)
                        for s in range(2):
                            mm = nc.tensor.matmul(bank(tb, HD, s * HD), oT[:, s * P:(s + 1) * P], cst[:, C_PAIR:C_PAIR + HD], start=True, stop=True)
                        mm.then_inc(added, 1)

                    def turn_out(g):
                        tb = my_turn("out", g)
                        pe.wait_ge(*((finished, g + 1) if out_gain is not None else (taken, (g + 1) * nh)))
                        n = nh * HD // P
                        for s in range(2):
                            for c in range(n):
                                mm = nc.tensor.transpose(bank(tb, P, (c * 2 + s) * P), o[g % 2][:, s, c * P:(c + 1) * P], ident)
                        mm.then_inc(oturned, 1)

                    scores(0)
                    for n in range(STEPS):
                        if n + 1 < nu:
                            scores(n + 1)
                        if sum_at(n) is not None:
                            add_parts(sum_at(n))
                        if n < nu:
                            turn(n)
                            if n % 2:
                                values(n // 2)
                        if out_at(n) is not None:
                            turn_out(out_at(n))

                @block.scalar
                def _(act):
                    def exps(u, m):
                        p, h, s = units[u]
                        n = nkeys(u) * P
                        i = 2 * (u % 2) + m
                        act.wait_ge(maxed, maps * u + m + 1)
                        if u >= 2:
                            act.wait_ge(probs, u - 1)
                            act.wait_ge(turned, nb[u - 1])
                        src = e[0][u % 2][:, 0:n] if (table and p < LT // 2) else bank(score_bank(u, m), n)
                        nc.scalar.activation(e[m][u % 2][:, 0:n], src, ACT.Exp, bias=nm[:, i:i + 1], accum_out=zs[:, i:i + 1]).then_inc(expd, 1)

                    def moves(u):
                        s = u % 2
                        for b, (k0, n) in enumerate(batches(u)):
                            act.wait_ge(turned, nb[u] + b + 1)
                            if b == 0 and s == 0 and u >= 2:
                                act.wait_ge(summed, u // 2)
                            nc.scalar.activation(hi[:, k0:k0 + n, s * P:(s + 1) * P],
                                                 bank(turn_bank("turn", u, b), n * P).rearrange("p (k q) -> p k q", k=n), ACT.Copy).then_inc(moved, 1)

                    def keep_sum(v):
                        act.wait_ge(summed, v + 1)
                        if v >= 1:
                            act.wait_ge(added, v)
                        nc.scalar.activation(oT[:, :], bank(turn_bank("values", v), 2 * P), ACT.Copy).then_inc(okept, 1)

                    def keep_out(g):
                        act.wait_ge(oturned, g + 1)
                        n = nh * HD // P
                        nc.scalar.activation(yT[:, y0:y0 + n, 2 * g * P:(2 * g + 2) * P],
                                             bank(turn_bank("out", g), n * 2 * P).rearrange("p (c t) -> p c t", c=n), ACT.Copy).then_inc(ykept, 1)

                    for m in range(maps):
                        exps(0, m)
                    for n in range(STEPS):
                        if maps == 2 and n + 1 < nu:
                            exps(n + 1, 0)
                        if n < nu:
                            moves(n)
                        if n + 1 < nu:
                            exps(n + 1, maps - 1)
                        if n < nu and n % 2:
                            keep_sum(n // 2)
                        if out_at(n) is not None:
                            keep_out(out_at(n))

                @block.vector
                def _(dve):
                    step = Chain(dve, step_s)

                    def top(u):
                        p, h, s = units[u]
                        n = nkeys(u) * P
                        for m in range(maps):
                            i = 2 * (u % 2) + m
                            dve.wait_ge(scored, maps * u + m + 1)
                            if u >= 2:
                                dve.wait_ge(expd, maps * (u - 2) + m + 1)
                            if table and p < LT // 2:
                                if u >= 2:
                                    dve.wait_ge(turned, nb[u - 1])
                                dve.wait_ge(biased, u + 1)
                                step.then(nc.vector.tensor_tensor_reduce(e[0][u % 2][:, 0:n], bank(score_bank(u, m), n), bb[u % 2][:, 0:n],
                                                                         1.0, 3.0 * NEG, ALU.add, ALU.max, mx[:, i:i + 1]))
                                step.wait()
                                nc.vector.tensor_scalar(nm[:, i:i + 1], mx[:, i:i + 1], -1.0, None, ALU.mult).then_inc(maxed, 1)
                            else:
                                nc.vector.tensor_reduce(nm[:, i:i + 1], bank(score_bank(u, m), n), AX, ALU.max, negate=True).then_inc(maxed, 1)

                    def weigh(u):
                        i, j = 2 * (u % 2), u % 8
                        dve.wait_ge(expd, maps * (u + 1))
                        if u >= 8:
                            dve.wait_ge(taken, (u - 8) // 2 + 1)
                        if maps == 1:
                            nc.vector.reciprocal(rz[:, j:j + 1], zs[:, i:i + 1]).then_inc(probs, 1)
                            return
                        n = nkeys(u) * P
                        step.then(nc.vector.reciprocal(rw[:, j:j + 1], zs[:, i + 1:i + 2]))
                        step.then(nc.vector.reciprocal(rz[:, j:j + 1], zs[:, i:i + 1]))
                        step.wait()
                        step.then(nc.vector.tensor_scalar(rw[:, j:j + 1], rw[:, j:j + 1], zs[:, i:i + 1], neglam[:, 0:1], ALU.mult, ALU.mult))
                        step.wait()
                        nc.vector.scalar_tensor_tensor(out=e[0][u % 2][:, 0:n], in0=e[1][u % 2][:, 0:n], scalar=rw[:, j:j + 1],
                                                       in1=e[0][u % 2][:, 0:n], op0=ALU.mult, op1=ALU.add).then_inc(probs, 1)

                    def splits(u):
                        s = u % 2
                        for b, (k0, n) in enumerate(batches(u)):
                            dve.wait_ge(moved, nb[u] + b + 1)
                            nc.vector.tensor_tensor(lo[:, k0:k0 + n, s * P:(s + 1) * P],
                                                    bank(turn_bank("turn", u, b), n * P).rearrange("p (k q) -> p k q", k=n),
                                                    hi[:, k0:k0 + n, s * P:(s + 1) * P].bitcast(F32), ALU.subtract).then_inc(split, 1)

                    def take(v):
                        g, h = divmod(v, nh)
                        dve.wait_ge(added, v + 1)
                        if maps == 1:
                            dve.wait_ge(probs, 2 * v + 2)
                        if h == 0 and g >= 2:
                            dve.wait_ge(oturned, g - 1)
                        for s in range(2):
                            j = (2 * v + s) % 8
                            ins = nc.vector.tensor_scalar(o[g % 2][:, s, h * HD:(h + 1) * HD], bank(turn_bank("sum", v), HD, s * HD), rz[:, j:j + 1], None, ALU.mult)
                        ins.then_inc(taken, 1)
                        if h == nh - 1 and out_gain is not None:
                            ov = o[g % 2][:, :, :].rearrange("p s d -> p (s d)")
                            dve.wait_ge(taken, v + 1)
                            step.then(nc.vector.tensor_tensor(osq[:, :], ov, ov, ALU.mult))
                            step.wait()
                            nc.vector.tensor_reduce(oss[:, g % 2, :], osq[:, :].rearrange("p (h d) -> p h d", d=HD), AX, ALU.add).then_inc(osums, 1)

                    def finish(g):
                        ov = o[g % 2][:, :, :].rearrange("p s (h d) -> p (s h) d", d=HD)
                        dve.wait_ge(oinv, g + 1)
                        step.then(nc.vector.tensor_tensor(ov, ov, oss[:, g % 2, :].unsqueeze(2).broadcast_to([P, 2 * nh, HD]), ALU.mult))
                        step.wait()
                        nc.vector.tensor_tensor(ov, ov, out_gain.unsqueeze(1).broadcast_to([P, 2 * nh, HD]), ALU.mult).then_inc(finished, 1)

                    top(0)
                    for n in range(STEPS):
                        if n < nu:
                            weigh(n)
                        if n + 1 < nu:
                            top(n + 1)
                        if sum_at(n) is not None:
                            take(sum_at(n))
                        if n < nu:
                            splits(n)
                        if out_gain is not None and n >= 1 and out_at(n + 1) is not None:
                            finish(out_at(n + 1))

                @block.gpsimd
                def _(pool):
                    step = Chain(pool, pstep)
                    if table:
                        tb, rowmask = table
                        for i in range(2):
                            step.then(nc.gpsimd.memset(bb[i][:, :], 0.0))
                        step.wait()
                        for u, (p, h, s) in enumerate(units):
                            if p >= LT // 2:
                                continue
                            if u >= 2:
                                pool.wait_ge(maxed, u - 1)
                            kts = keys(p)
                            rows_n = 2 * (len(kts) - 2)
                            qt = 2 * p + s
                            s0 = 2 * kts[0] - 2 * qt + 8
                            if u >= 2 and len(keys(units[u - 2][0])) != len(kts):
                                step.then(nc.gpsimd.memset(bb[u % 2][:, rows_n * GRID_W:], 0.0))
                                step.wait()
                            nc.gpsimd.tensor_tensor(bb[u % 2][:, 0:rows_n * GRID_W].rearrange("p (r c) -> p r c", c=GRID_W), tb[:, h, s0:s0 + rows_n, :],
                                                    rowmask(qt, rows_n).unsqueeze(2).broadcast_to([P, rows_n, GRID_W]), ALU.add).then_inc(biased, 1)
                    if out_gain is not None:
                        for g in range(len(pairs)):
                            pool.wait_ge(osums, g + 1)
                            step.then(nc.gpsimd.tensor_scalar(oss[:, g % 2, :], oss[:, g % 2, :], 1.0 / HD, EPS, ALU.mult, ALU.add))
                            step.wait()
                            nc.gpsimd.tensor_tensor(oss[:, g % 2, :], oss[:, g % 2, :], half[:, 0:2 * nh], ALU.pow).then_inc(oinv, 1)

    def all_keys(p):
        return list(range(NT)) if p < LT // 2 else list(range(LT, NT))

    def window_keys(p):
        if p >= LT // 2:
            return [LT, LT + 1]
        a, b = pair_window(p)
        return list(range(a, b)) + [LT, LT + 1]

    def load_rows(l, off, n, tile, s):
        def go(sp):
            sp.dma_start(tile[:, :, :], a["w_in"][l].rearrange("(c p) n -> p c n", p=P)[:, :, off:off + n]).then_inc(s, 16)
        return go

    def project_qkv(l, name, half_i, hd, gq, gk, stack, vs, rope):
        tag = f"{name}p{l}{half_i}"
        st = ExitStack()
        nh = P // hd
        four = hd == 32
        ns = 8 if four else 6
        with st:
            w = sb(f"w_{tag}", [P, DC, 3, P], st)
            sq = [sb(f"sq{i}_{tag}", [P, 256], st) for i in range(2)]
            n_ = [sb(f"n{i}_{tag}", [P, 256], st) for i in range(2)]
            r_, u_ = sb(f"r_{tag}", [P, 256], st), sb(f"u_{tag}", [P, 256], st)
            so = [sb(f"so{i}_{tag}", [P, ns * P], st) for i in range(2)]
            ss = [sb(f"ss{i}_{tag}", [P, 2 * nh], st) for i in range(2)]
            loaded, projected, squared, sums = (sem(f"{n}_{tag}") for n in ("loaded", "projected", "squared", "sums"))
            inv, normed, vhigh, vlow, turned = (sem(f"{n}_{tag}") for n in ("inv", "normed", "v_high", "v_low", "turned"))
            kept, ready, high, step_s, pstep = (sem(f"{n}_{tag}") for n in ("kept", "ready", "high", "dve_step", "pool_step"))
            lows = sem(f"lows_{tag}")
            wv = a["w_in"][l].rearrange("(c p) n -> p c n", p=P)
            def high_q(s):
                v = s[:, 0:nh * (4 if four else 2) * hd].rearrange("p (h c d) -> p h c d", h=nh, d=hd)
                return v[:, :, 0:4:2, :] if four else v[:, :, 0:1, :]

            def low_q(s):
                v = s[:, 0:nh * (4 if four else 2) * hd].rearrange("p (h c d) -> p h c d", h=nh, d=hd)
                return v[:, :, 1:4:2, :] if four else v[:, :, 1:2, :]

            def high_k(s):
                if four:
                    return s[:, 512:1024].rearrange("p (h c d) -> p h c d", h=nh, d=hd)[:, :, 0:2, :]
                return s[:, 256:512].rearrange("p (h c d) -> p h c d", h=nh, d=hd)

            def low_k(s):
                if four:
                    return s[:, 512:1024].rearrange("p (h c d) -> p h c d", h=nh, d=hd)[:, :, 2:4, :]
                return s[:, 512:768].rearrange("p (h c d) -> p h c d", h=nh, d=hd)

            with nc.Block() as block:
                @block.sync
                def _(sp):
                    for j in range(3):
                        c0 = OFF[name] + j * GW + half_i * P
                        sp.dma_start(w[:, :, j, :], wv[:, :, c0:c0 + P]).then_inc(loaded, 16)

                @block.tensor
                def _(pe):
                    pe.wait_ge(loaded, 48)
                    for t in range(NT + 2):
                        if t < NT:
                            if t >= 2:
                                pe.wait_ge(vlow, t - 1)
                                pe.wait_ge(normed, t - 1)
                            for c in range(DC):
                                mm = nc.tensor.matmul(bank(t % 2, 384), hT[:, c, t * P:(t + 1) * P], w[:, c, :, :].rearrange("p j n -> p (j n)"),
                                                      start=(c == 0), stop=(c == DC - 1))
                            mm.then_inc(projected, 1)
                        if t >= 2:
                            i = t - 2
                            pe.wait_ge(lows, 2 * (i + 1))
                            if i >= 2:
                                pe.wait_ge(kept, i - 1)
                            for c in range(ns):
                                mm = nc.tensor.transpose(bank(2 + 2 * (i % 2), P, c * P), so[i % 2][:, c * P:(c + 1) * P], ident)
                            mm.then_inc(turned, 1)

                @block.scalar
                def _(act):
                    def stacked(t):
                        act.wait_ge(ready, t + 1)
                        if t >= 2:
                            act.wait_ge(turned, t - 1)
                        q, k = n_[t % 2][:, 0:P], n_[t % 2][:, P:2 * P]
                        for x, dst in ((q, high_q(so[t % 2])), (k, high_k(so[t % 2]))):
                            c = dst.shape[2]
                            nc.scalar.activation(dst.bitcast(F32R), x.rearrange("p (h d) -> p h d", d=hd).unsqueeze(2).broadcast_to([P, nh, c, hd]), ACT.Copy).then_inc(high, 1)

                    for t in range(NT + 2):
                        if t < NT:
                            act.wait_ge(projected, t + 1)
                            if t >= 2:
                                act.wait_ge(sums, t - 1)
                            nc.scalar.activation(sq[t % 2][:, :], bank(t % 2, 256), ACT.Square).then_inc(squared, 1)
                            nc.scalar.activation(vs[:, t, :, 0:HD], bank(t % 2, P, 256).rearrange("p (h d) -> p h d", d=HD), ACT.Copy).then_inc(vhigh, 1)
                        if 1 <= t <= NT:
                            stacked(t - 1)
                        if t >= 2:
                            i = t - 2
                            act.wait_ge(turned, i + 1)
                            nc.scalar.activation(stack[:, :, i * P:(i + 1) * P], bank(2 + 2 * (i % 2), ns * P).rearrange("p (c t) -> p c t", c=ns), ACT.Copy).then_inc(kept, 1)

                @block.gpsimd
                def _(pool):
                    step = Chain(pool, pstep)
                    for t in range(NT):
                        pool.wait_ge(sums, t + 1)
                        step.then(nc.gpsimd.tensor_scalar(ss[t % 2][:, :], ss[t % 2][:, :], 1.0 / hd, EPS, ALU.mult, ALU.add))
                        step.wait()
                        nc.gpsimd.tensor_tensor(ss[t % 2][:, :], ss[t % 2][:, :], half[:, 0:2 * nh], ALU.pow).then_inc(inv, 1)

                @block.vector
                def _(dve):
                    step = Chain(dve, step_s)

                    def heads_of(x):
                        return x.rearrange("p (h d) -> p h d", d=hd)

                    def sum_squares(t):
                        dve.wait_ge(squared, t + 1)
                        if t >= 2:
                            dve.wait_ge(normed, t - 1)
                        nc.vector.tensor_reduce(ss[t % 2][:, :], heads_of(sq[t % 2][:, :]), AX, ALU.add).then_inc(sums, 1)
                        dve.wait_ge(vhigh, t + 1)
                        nc.vector.tensor_tensor(vs[:, t, :, HD:2 * HD], bank(t % 2, P, 256).rearrange("p (h d) -> p h d", d=HD),
                                                vs[:, t, :, 0:HD].bitcast(F32), ALU.subtract).then_inc(vlow, 1)

                    def low_parts(t):
                        dve.wait_ge(high, 2 * (t + 1))
                        for x, hp, lp in ((n_[t % 2][:, 0:P], high_q, low_q), (n_[t % 2][:, P:2 * P], high_k, low_k)):
                            dst = lp(so[t % 2])
                            c = dst.shape[2]
                            nc.vector.tensor_tensor(dst, heads_of(x).unsqueeze(2).broadcast_to([P, nh, c, hd]),
                                                    hp(so[t % 2])[:, :, 0:1, :].broadcast_to([P, nh, c, hd]), ALU.subtract).then_inc(lows, 1)

                    sum_squares(0)
                    for t in range(NT):
                        if t + 1 < NT:
                            sum_squares(t + 1)
                        n = n_[t % 2]
                        dve.wait_ge(inv, t + 1)
                        if t >= 2:
                            dve.wait_ge(lows, 2 * (t - 1))
                            dve.wait_ge(high, 2 * (t - 1))
                        nc.vector.tensor_tensor(heads_of(n[:, :]), heads_of(bank(t % 2, 256)), ss[t % 2][:, :].unsqueeze(2).broadcast_to([P, 2 * nh, hd]), ALU.mult).then_inc(normed, 1)
                        dve.wait_ge(normed, t + 1)
                        roped = rope and t < LT
                        for k, g in enumerate((gq, gk)):
                            part = heads_of(n[:, :])[:, k * nh:(k + 1) * nh, :]
                            ins = nc.vector.tensor_tensor(part, part, g.unsqueeze(1).broadcast_to([P, nh, hd]), ALU.mult)
                            if roped or k == 0:
                                step.then(ins)
                            else:
                                step.wait()
                                ins.then_inc(ready, 1)
                        if roped:
                            step.wait()
                            cos = cst[:, C_COS + 32 * t:C_COS + 32 * t + 32].unsqueeze(1).broadcast_to([P, 2 * nh, 32])
                            sin = cst[:, C_SIN + 32 * t:C_SIN + 32 * t + 32].rearrange("p (a b e) -> p a b e", a=2, b=2)
                            nv = n[:, :].rearrange("p (h a b e) -> p h a b e", a=2, b=2, e=8)
                            rv = r_[:, :].rearrange("p (h a b e) -> p h a b e", a=2, b=2, e=8)
                            for x in range(2):
                                for y in range(2):
                                    step.then(nc.vector.tensor_tensor(rv[:, :, x, y, :], nv[:, :, x, 1 - y, :],
                                                                      sin[:, x, y, :].unsqueeze(1).broadcast_to([P, 2 * nh, 8]), ALU.mult))
                            step.then(nc.vector.tensor_tensor(heads_of(u_[:, :]), heads_of(n[:, :]), cos, ALU.mult))
                            step.wait()
                            nc.vector.tensor_tensor(n[:, :], u_[:, :], r_[:, :], ALU.add).then_inc(ready, 1)
                        if t >= 1:
                            low_parts(t - 1)
                    low_parts(NT - 1)

    def mixers(l, yT, need):
        R = {k: rows[:, l, o:o + w] for k, (o, w) in ROWS.items()}

        def two_heads(name, i, hd, maps, y0, rope, keys, out_gain=None):
            st = ExitStack()
            with st:
                tag = f"{name}{l}{i}"
                four = hd == 32
                stack = sbr(f"stack_{tag}", [P, 8 if four else 6, T], st)
                vs = sbr(f"vs_{tag}", [P, NT, 2, 2 * HD], st)
                project_qkv(l, name, i, hd, R[f"{name}_g_q"], R[f"{name}_g_k"], stack, vs, rope)
                if four:
                    def parts(h, m):
                        return [(stack[:, 2 * h + m, :], stack[:, 4 + 2 * h + m, :])]
                else:
                    def parts(h, m):
                        return [(stack[:, h, :], stack[:, 2 + h, :]), (stack[:, h, :], stack[:, 4 + h, :])]
                table = None
                if name == "na":
                    tb = sb(f"tb_{tag}", [P, 2, NSLOT, GRID_W], st)
                    position_table(l, i, tb, yT)
                    table = (tb, lambda qt, n: cst[:, C_ROW + 12 * qt:C_ROW + 12 * qt + n])
                attention(tag, l, [2 * i, 2 * i + 1], maps, parts, keys, vs, yT, y0 + i, out_gain=out_gain, table=table, need=need)
            clear_semaphores()

        for i in range(2):
            two_heads("diff", i, DQK, 2, 0, True, all_keys, R["diff_g_out"])

        def mla():
            st = ExitStack()
            with st:
                qkT = sb(f"mqkT{l}", [P, 2 * H, T], st)
                vs = sbr(f"mvs{l}", [P, NT, H, 2 * HD], st)
                mla_project(l, R, qkT, vs, yT)
                attention(f"mla{l}", l, range(H), 1, lambda h, m: [(qkT[0:MD, h, :], qkT[0:MD, H + h, :])],
                          all_keys, vs, yT, 2, need=need)
        mla()
        clear_semaphores()

        for i in range(2):
            two_heads("na", i, HD, 1, 6, False, window_keys)

        mlstm(l, R, yT, need)
        clear_semaphores()

    def position_table(l, i, tb, yT):
        read, turned, masked = (sem(f"{n}{l}{i}") for n in ("rpb_read", "rpb_turned", "rpb_masked"))
        n, step = 2 * NSLOT * GRID_W, 6 * GRID_W
        raw = yT[:, 4:6, :].rearrange("p c t -> p (c t)")[:, 0:n]
        flat = tb[:, :, :, :].rearrange("p h s k -> p (h s) k")
        with nc.Block() as block:
            @block.sync
            def _(sp):
                for h in range(2):
                    for x in range(2):
                        off = ((l * H + 2 * i + h) * (NSLOT + 1) + x) * 127
                        sp.dma_start(raw[x * GRID_W:(x + 1) * GRID_W, :].rearrange("p (h s k) -> p h s k", h=2, s=NSLOT)[:, h, :, :],
                                     bass.AP(rpb_pad.tensor, off, [[1, GRID_W], [127, NSLOT], [1, GRID_W]])).then_inc(read, 16)

            @block.tensor
            def _(pe):
                pe.wait_ge(read, 16 * 4)
                for j in range(n // step):
                    nc.tensor.matmul(bank(j, step), cst[:, C_REV:C_REV + P], raw[:, j * step:(j + 1) * step], start=True, stop=True).then_inc(turned, 1)

            @block.vector
            def _(dve):
                for j in range(n // step):
                    dve.wait_ge(turned, j + 1)
                    nc.vector.tensor_tensor(flat[:, 6 * j:6 * j + 6, :], bank(j, step).rearrange("p (s k) -> p s k", k=GRID_W),
                                            cst[:, C_COL:C_COL + 64].unsqueeze(1).broadcast_to([P, 6, GRID_W]), ALU.add).then_inc(masked, 1)

    def mla_project(l, R, qkT, vs, yT):
        st = ExitStack()
        with st:
            tag = f"mlap{l}"
            w = yT[:, 4:8, :].rearrange("p c t -> p (c t)")[:, 0:DC * 416].rearrange("p (c n) -> p c n", c=DC)
            wq = sb(f"wq_{tag}", [P, 2, H * MD], st)
            wkv = sb(f"wkv_{tag}", [P, 2 * GW], st)
            sq = sb(f"sq_{tag}", [P, 256], st)
            sq2 = sb(f"sq2_{tag}", [P, 2 * H * MD], st)
            cn = [sb(f"cn{i}_{tag}", [P, 384], st) for i in range(2)]
            kr = [sb(f"kr{i}_{tag}", [P, ROPE], st) for i in range(2)]
            cT = sb(f"cT_{tag}", [P, 3, P], st)
            qk = sb(f"qk_{tag}", [P, 2 * H, MD], st)
            rt = sb(f"rt_{tag}", [P, 2 * H, ROPE], st)
            ss = sb(f"ss_{tag}", [P, 2, 2], st)
            s8 = sb(f"s8_{tag}", [P, 2, 2 * H], st)
            loaded, projected, sums, inv = (sem(f"{n}_{tag}") for n in ("loaded", "projected", "sums", "inv"))
            normed, cturned, ckept, up = (sem(f"{n}_{tag}") for n in ("normed", "c_turned", "c_kept", "up"))
            gathered, qsq, qsums, qinv = (sem(f"{n}_{tag}") for n in ("gathered", "q_squared", "q_sums", "q_inv"))
            ready, turned, kept, vkept = (sem(f"{n}_{tag}") for n in ("ready", "turned", "kept", "v_kept"))
            step_s, pstep, vlow = sem(f"dve_step_{tag}"), sem(f"pool_step_{tag}"), sem(f"v_low_{tag}")
            go = load_rows(l, OFF["mla"], 416, w, loaded)
            with nc.Block() as block:
                @block.sync
                def _(sp):
                    go(sp)
                    sp.dma_start(wq[:, :, :], a["mla_w_uq"][l].rearrange("(c p) n -> p c n", p=P)).then_inc(loaded, 16)
                    sp.dma_start(wkv[:, :], a["mla_w_ukv"][l]).then_inc(loaded, 16)

                @block.tensor
                def _(pe):
                    pe.wait_ge(loaded, 48)

                    def down(t):
                        if t >= 2:
                            pe.wait_ge(normed, t - 1)
                        for c in range(DC):
                            mm = nc.tensor.matmul(bank(t % 2, 416), hT[:, c, t * P:(t + 1) * P], w[:, c, :], start=(c == 0), stop=(c == DC - 1))
                        mm.then_inc(projected, 1)

                    def turn_back(t):
                        pe.wait_ge(ready, t + 1)
                        for s in range(2):
                            if t >= 1:
                                pe.wait_ge(kept, 2 * (t - 1) + s + 1)
                            for h in range(H):
                                mm = nc.tensor.transpose(bank(5 + s, P, h * P)[0:MD, :], qk[:, s * H + h, :], ident)
                            mm.then_inc(turned, 1)

                    down(0)
                    for t in range(NT):
                        if t + 1 < NT:
                            down(t + 1)
                        pe.wait_ge(normed, t + 1)
                        if t >= 1:
                            pe.wait_ge(ckept, t)
                        for c in range(3):
                            mm = nc.tensor.transpose(bank(2, P, c * P), cn[t % 2][:, c * P:(c + 1) * P], ident)
                        mm.then_inc(cturned, 1)
                        if t >= 1:
                            turn_back(t - 1)
                        pe.wait_ge(ckept, t + 1)
                        if t >= 1:
                            pe.wait_ge(gathered, t)
                            pe.wait_ge(vlow, t)
                        for c in range(2):
                            nc.tensor.matmul(bank(3, H * MD), cT[:, c, :], wq[:, c, :], start=(c == 0), stop=(c == 1))
                        nc.tensor.matmul(bank(4), cT[:, 2, :], wkv[:, :], start=True, stop=True).then_inc(up, 1)
                    turn_back(NT - 1)

                @block.scalar
                def _(act):
                    def first(t):
                        act.wait_ge(projected, t + 1)
                        if t >= 2:
                            act.wait_ge(normed, t - 1)
                        nc.scalar.activation(sq[:, :], bank(t % 2, MQ), ACT.Square, scale=MQ ** -0.5, accum_out=ss[:, t % 2, 0:1]).then_inc(sums, 1)
                        act.wait_ge(sums, 2 * t + 1)
                        nc.scalar.activation(sq[:, 0:MKV], bank(t % 2, MKV, MQ), ACT.Square, scale=MKV ** -0.5, accum_out=ss[:, t % 2, 1:2]).then_inc(sums, 1)
                        act.wait_ge(sums, 2 * t + 2)

                    def move(t):
                        act.wait_ge(turned, 2 * t + 2)
                        for s in range(2):
                            nc.scalar.activation(qkT[0:MD, s * H:(s + 1) * H, t * P:(t + 1) * P],
                                                 bank(5 + s)[0:MD, :].rearrange("p (h t) -> p h t", h=H), ACT.Copy).then_inc(kept, 1)

                    first(0)
                    for t in range(NT):
                        if t + 1 < NT:
                            first(t + 1)
                        act.wait_ge(cturned, t + 1)
                        if t >= 1:
                            act.wait_ge(up, t)
                        nc.scalar.activation(cT[:, 0, :], bank(2, P), ACT.Copy, scale=vec[:, l, V_GCQ:V_GCQ + 1])
                        nc.scalar.activation(cT[:, 1, :], bank(2, P, P), ACT.Copy, scale=vec[:, l, V_GCQ + 1:V_GCQ + 2])
                        nc.scalar.activation(cT[:, 2, :], bank(2, P, 2 * P), ACT.Copy, scale=vec[:, l, V_GCKV:V_GCKV + 1]).then_inc(ckept, 1)
                        if t >= 1:
                            move(t - 1)
                        act.wait_ge(up, t + 1)
                        act.wait_ge(gathered, t + 1)
                        nc.scalar.activation(vs[:, t, :, 0:HD],
                                             bank(4).rearrange("p (h d) -> p h d", h=H)[:, :, HD:2 * HD], ACT.Copy).then_inc(vkept, 1)
                        if t >= 1:
                            act.wait_ge(qsums, t)
                        nc.scalar.activation(sq2[:, :], qk[:, :, :].rearrange("p h d -> p (h d)"), ACT.Square).then_inc(qsq, 1)
                    move(NT - 1)

                @block.gpsimd
                def _(pool):
                    step = Chain(pool, pstep)
                    for t in range(NT + 1):
                        if t < NT:
                            pool.wait_ge(sums, 2 * t + 2)
                            step.then(nc.gpsimd.tensor_scalar(ss[:, t % 2, :], ss[:, t % 2, :], EPS, 1.0, ALU.add, ALU.mult))
                            step.wait()
                            nc.gpsimd.tensor_tensor(ss[:, t % 2, :], ss[:, t % 2, :], half[:, 0:2], ALU.pow).then_inc(inv, 1)
                        if t >= 1:
                            i = t - 1
                            pool.wait_ge(qsums, i + 1)
                            step.then(nc.gpsimd.tensor_scalar(s8[:, i % 2, :], s8[:, i % 2, :], 1.0 / MD, EPS, ALU.mult, ALU.add))
                            step.wait()
                            nc.gpsimd.tensor_tensor(s8[:, i % 2, :], s8[:, i % 2, :], half[:, 0:2 * H], ALU.pow).then_inc(qinv, 1)

                @block.vector
                def _(dve):
                    step = Chain(dve, step_s)

                    def norm_latents(t):
                        dve.wait_ge(inv, t + 1)
                        if t >= 2:
                            dve.wait_ge(cturned, t - 1)
                            dve.wait_ge(gathered, t - 1)
                        nc.vector.tensor_copy(kr[t % 2][:, :], bank(t % 2, ROPE, MQ + MKV))
                        nc.vector.tensor_scalar(cn[t % 2][:, 0:MQ], bank(t % 2, MQ), ss[:, t % 2, 0:1], None, ALU.mult)
                        nc.vector.tensor_scalar(cn[t % 2][:, MQ:MQ + MKV], bank(t % 2, MKV, MQ), ss[:, t % 2, 1:2], None, ALU.mult).then_inc(normed, 1)

                    norm_latents(0)
                    for t in range(NT):
                        if t + 1 < NT:
                            norm_latents(t + 1)
                        dve.wait_ge(up, t + 1)
                        if t >= 1:
                            dve.wait_ge(turned, 2 * t)
                        nc.vector.tensor_copy(qk[:, 0:H, :], bank(3, H * MD).rearrange("p (h d) -> p h d", h=H))
                        nc.vector.tensor_copy(qk[:, H:2 * H, 0:HD], bank(4).rearrange("p (h d) -> p h d", h=H)[:, :, 0:HD])
                        dve.wait_ge(normed, t + 1)
                        nc.vector.tensor_copy(qk[:, H:2 * H, HD:MD], kr[t % 2][:, :].unsqueeze(1).broadcast_to([P, H, ROPE])).then_inc(gathered, 1)
                        dve.wait_ge(vkept, t + 1)
                        nc.vector.tensor_tensor(vs[:, t, :, HD:2 * HD], bank(4).rearrange("p (h d) -> p h d", h=H)[:, :, HD:2 * HD],
                                                vs[:, t, :, 0:HD].bitcast(F32), ALU.subtract).then_inc(vlow, 1)
                        dve.wait_ge(qsq, t + 1)
                        if t >= 2:
                            dve.wait_ge(step_s, n2)
                        nc.vector.tensor_reduce(s8[:, t % 2, :], sq2[:, :].rearrange("p (h d) -> p h d", h=2 * H), AX, ALU.add).then_inc(qsums, 1)
                        dve.wait_ge(qinv, t + 1)
                        n2 = step.then(nc.vector.tensor_tensor(qk[:, :, :], qk[:, :, :], s8[:, t % 2, :].unsqueeze(2).broadcast_to([P, 2 * H, MD]), ALU.mult))
                        step.wait()
                        step.then(nc.vector.tensor_tensor(qk[:, 0:H, :], qk[:, 0:H, :], R["mla_g_q"].unsqueeze(1).broadcast_to([P, H, MD]), ALU.mult))
                        ins = nc.vector.tensor_tensor(qk[:, H:2 * H, :], qk[:, H:2 * H, :], R["mla_g_k"].unsqueeze(1).broadcast_to([P, H, MD]), ALU.mult)
                        if t >= LT:
                            step.wait()
                            ins.then_inc(ready, 1)
                        else:
                            step.then(ins)
                            step.wait()
                            cos = cst[:, C_COS + 32 * t:C_COS + 32 * t + 32].unsqueeze(1).broadcast_to([P, 2 * H, ROPE])
                            sin = cst[:, C_SIN + 32 * t:C_SIN + 32 * t + 32].rearrange("p (a b e) -> p a b e", a=2, b=2)
                            rq = qk[:, :, HD:MD]
                            for x in range(2):
                                for y in range(2):
                                    o0 = HD + 16 * x + 8 * (1 - y)
                                    step.then(nc.vector.tensor_tensor(rt[:, :, 16 * x + 8 * y:16 * x + 8 * y + 8], qk[:, :, o0:o0 + 8],
                                                                      sin[:, x, y, :].unsqueeze(1).broadcast_to([P, 2 * H, 8]), ALU.mult))
                            step.wait()
                            step.then(nc.vector.tensor_tensor(rq, rq, cos, ALU.mult))
                            step.wait()
                            nc.vector.tensor_tensor(rq, rq, rt[:, :, :], ALU.add).then_inc(ready, 1)

    def mlstm(l, R, yT, need):
        st = ExitStack()
        nq = NT if need else LT
        G4 = NT * H
        order = [[8, 9] + list(range(LT)), [9, 8] + list(range(LT))[::-1]]
        with st:
            qkT = sb(f"lqkT{l}", [P, 4, T], st)
            v = sb(f"lv1_{l}", [P, NT, H, HD + 1], st)
            def so(t):
                return yT[:, 4:6, t * P:(t + 1) * P]
            gt = sb(f"gt{l}", [P, NT, 16], st)
            A, M, EM = (sb(f"{n}{l}", [P, 2, NT, H], st) for n in ("gA", "gM", "gEM"))
            mlstm_project(l, R, qkT, v, so, gt)
            mlstm_gates(l, R, gt, A, M, EM, order)
            clear_semaphores()
            mlstm_mix(l, R, qkT, v, so, A, M, EM, yT, nq)

    def mlstm_project(l, R, qkT, v, so, gt):
        st = ExitStack()
        width = T + 4
        span = T + 2
        with st:
            tag = f"mlp{l}"
            wqk = sb(f"wqk_{tag}", [P, DC, 512], st)
            wg = sb(f"wg_{tag}", [P, DC, 16], st)
            u = [sb(f"u{i}_{tag}", [P, width], st) for i in range(2)]
            cv = [sb(f"cv{i}_{tag}", [P, width], st) for i in range(1)]
            loaded, loaded2, loaded3, up, copied = (sem(f"{n}_{tag}") for n in ("loaded", "loaded_vo", "loaded_g", "up", "copied"))
            zeroed, step_s, conv, silu = (sem(f"{n}_{tag}") for n in ("zeroed", "dve_step", "conv", "silu"))
            projected, vkept, okept, gkept = (sem(f"{n}_{tag}") for n in ("projected", "v_kept", "o_kept", "g_kept"))
            with nc.Block() as block:
                @block.sync
                def _(sp):
                    load_rows(l, OFF["mlqk"], 512, wqk, loaded)(sp)
                    load_rows(l, OFF["mlg"], 16, wg, loaded3)(sp)
                    sp.wait_ge(up, 4)
                    load_rows(l, OFF["mlvo"], 512, wqk, loaded2)(sp)

                @block.tensor
                def _(pe):
                    pe.wait_ge(loaded, 16)
                    for f in range(4):
                        if f >= 2:
                            pe.wait_ge(copied, 2 * (f - 1))
                        for j, (t0, m, s) in enumerate(BLOCKS):
                            for c in range(DC):
                                mm = nc.tensor.matmul(bank(3 * (f % 2) + j, m), wqk[:, c, f * P:(f + 1) * P], hT[:, c, t0:t0 + m], start=(c == 0), stop=(c == DC - 1))
                        mm.then_inc(up, 1)
                    pe.wait_ge(loaded2, 16)
                    pe.wait_ge(loaded3, 16)
                    pe.wait_ge(copied, 8)
                    for t in range(NT):
                        if t >= 2:
                            pe.wait_ge(vkept, t - 1)
                            pe.wait_ge(okept, t - 1)
                            pe.wait_ge(gkept, t - 1)
                        for c in range(DC):
                            nc.tensor.matmul(bank(t % 2), hT[:, c, t * P:(t + 1) * P], wqk[:, c, :], start=(c == 0), stop=(c == DC - 1))
                        for c in range(DC):
                            mm = nc.tensor.matmul(bank(2 + t % 2, 16), hT[:, c, t * P:(t + 1) * P], wg[:, c, :], start=(c == 0), stop=(c == DC - 1))
                        mm.then_inc(projected, 1)

                @block.scalar
                def _(act):
                    act.wait_ge(zeroed, 2)
                    for f in range(4):
                        act.wait_ge(up, f + 1)
                        if f >= 2:
                            act.wait_ge(conv, f - 1)
                        nc.scalar.activation(u[f % 2][:, 1:1 + SEQ], bank(3 * (f % 2), SEQ), ACT.Copy).then_inc(copied, 1)
                        nc.scalar.activation(u[f % 2][:, SEQ + 3:SEQ + 3 + CTX], bank(3 * (f % 2) + 2, CTX), ACT.Copy).then_inc(copied, 1)
                        act.wait_ge(conv, f + 1)
                        nc.scalar.activation(qkT[:, f, 0:SEQ], cv[0][:, 0:SEQ], ACT.Silu)
                        nc.scalar.activation(qkT[:, f, SEQ:T], cv[0][:, SEQ + 2:T + 2], ACT.Silu).then_inc(silu, 1)
                    for t in range(NT):
                        act.wait_ge(projected, t + 1)
                        nc.scalar.activation(so(t), bank(t % 2, GW, GW).rearrange("p (c d) -> p c d", c=2), ACT.Sigmoid).then_inc(okept, 1)

                @block.gpsimd
                def _(pool):
                    for i in range(2):
                        nc.gpsimd.memset(u[i][:, :], 0.0).then_inc(zeroed, 1)
                    nc.gpsimd.memset(v[:, :, :, HD:HD + 1], 1.0).then_inc(zeroed, 1)

                @block.vector
                def _(dve):
                    step = Chain(dve, step_s)
                    for f in range(4):
                        def w(k):
                            c = V_MCONV + 4 * k + f
                            return vec[:, l, c:c + 1]
                        dve.wait_ge(copied, 2 * f + 2)
                        if f >= 1:
                            dve.wait_ge(silu, f)
                        x = u[f % 2]
                        step.then(nc.vector.tensor_scalar(cv[0][:, 0:span], x[:, 0:span], w(0), None, ALU.mult))
                        step.wait()
                        step.then(nc.vector.scalar_tensor_tensor(out=cv[0][:, 0:span], in0=x[:, 1:1 + span], scalar=w(1), in1=cv[0][:, 0:span], op0=ALU.mult, op1=ALU.add))
                        step.wait()
                        nc.vector.scalar_tensor_tensor(out=cv[0][:, 0:span], in0=x[:, 2:2 + span], scalar=w(2), in1=cv[0][:, 0:span], op0=ALU.mult, op1=ALU.add).then_inc(conv, 1)
                    for t in range(NT):
                        dve.wait_ge(projected, t + 1)
                        dve.wait_ge(okept, t + 1)
                        nc.vector.tensor_copy(v[:, t, :, 0:HD], bank(t % 2, GW).rearrange("p (h d) -> p h d", h=H)).then_inc(vkept, 1)
                        nc.vector.tensor_copy(gt[:, t, :], bank(2 + t % 2, 16)).then_inc(gkept, 1)

    def mlstm_gates(l, R, gt, A, M, EM, order):
        st = ExitStack()
        G4 = NT * H
        PAD = 64
        with st:
            tag = f"mlg{l}"
            F, E1, B, TOT, TM = (sb(f"{n}_{tag}", [P, 2, NT, H], st) for n in ("F", "E1", "B", "TOT", "TM"))
            off = sb(f"off_{tag}", [P, 2, NT, H], st)
            run = sb(f"run_{tag}", [P, 2, NT, H], st)
            sc = [sb(f"sc{i}_{tag}", [G4, 2, PAD + P], st) for i in range(2)]
            back = sb(f"back_{tag}", [P, 2, G4], st)
            step_s, astep, pstep = sem(f"dve_step_{tag}"), sem(f"act_step_{tag}"), sem(f"pe_step_{tag}")
            padded = sem(f"padded_{tag}")
            flat = "p a t h -> p (a t h)"

            def d(x, i):
                return x[:, i, :, :].rearrange("p t h -> p (t h)")

            def both(x):
                return x[:, :, :, :].rearrange(flat)
            cum = (cst[:, C_CUM:C_CUM + P], cst[:, C_CUMR:C_CUMR + P])
            rev = cst[:, C_REV:C_REV + P]
            e127 = cst[:, C_E127:C_E127 + P]
            marks = {}
            with nc.Block() as block:
                @block.gpsimd
                def _(pool):
                    for i in range(2):
                        nc.gpsimd.memset(sc[i][:, :, :], 3.0 * NEG).then_inc(padded, 1)

                @block.vector
                def _(dve):
                    step = Chain(dve, step_s)

                    def go(ins):
                        step.then(ins)
                        step.wait()
                    for i in range(2):
                        for x, o, b in ((F, 8 + 4 * i, "mlstm_b_f"), (A, 4 * i, "mlstm_b_i")):
                            go(nc.vector.tensor_tensor(x[:, i, :, :], gt[:, :, o:o + 4],
                                                       R[b][:, 4 * i:4 * i + 4].unsqueeze(1).broadcast_to([P, NT, H]), ALU.add))
                    go(nc.vector.scalar_tensor_tensor(out=both(E1), in0=both(F), scalar=-1.0, in1=both(F), op0=ALU.mult, op1=ALU.max))
                    marks["abs"] = step.n
                    dve.wait_ge(astep, 2)
                    go(nc.vector.scalar_tensor_tensor(out=both(F), in0=both(F), scalar=0.0, in1=both(E1), op0=ALU.min, op1=ALU.subtract))
                    marks["lf"] = step.n
                    dve.wait_ge(pstep, 3)
                    go(nc.vector.tensor_copy(both(TOT), bank(2, 2 * G4)))
                    for i in range(2):
                        step.then(nc.vector.memset(off[:, i, order[i][0], :], 0.0))
                    step.wait()
                    for n in range(1, NT):
                        for i in range(2):
                            x, y = order[i][n], order[i][n - 1]
                            step.then(nc.vector.tensor_tensor(off[:, i, x, :], off[:, i, y, :], TOT[:, i, y, :], ALU.add))
                        step.wait()
                    for i in range(2):
                        go(nc.vector.tensor_tensor(d(B, i), bank(i, G4), d(off, i), ALU.add))
                    go(nc.vector.tensor_tensor(both(A), both(A), both(B), ALU.subtract))
                    marks["a"] = step.n
                    dve.wait_ge(pstep, 5)
                    dve.wait_ge(padded, 2)
                    for i in range(2):
                        go(nc.vector.tensor_copy(sc[0][:, i, PAD:PAD + P], bank(3 + i, P)[0:G4, :]))
                    for n in range(7):
                        x, y, k = sc[n % 2], sc[(n + 1) % 2], 1 << n
                        go(nc.vector.tensor_tensor(y[:, :, PAD:PAD + P], x[:, :, PAD:PAD + P], x[:, :, PAD - k:PAD + P - k], ALU.max))
                    marks["scan"] = step.n
                    dve.wait_ge(pstep, 6)
                    go(nc.vector.tensor_copy(back[:, :, :], bank(5, 2 * G4).rearrange("p (a n) -> p a n", a=2)))
                    marks["back"] = step.n
                    dve.wait_ge(pstep, 8)
                    go(nc.vector.tensor_copy(both(TM), bank(6, 2 * G4)))
                    for i in range(2):
                        step.then(nc.vector.memset(run[:, i, order[i][0], :], 3.0 * NEG))
                    step.wait()
                    for n in range(1, NT):
                        for i in range(2):
                            x, y = order[i][n], order[i][n - 1]
                            step.then(nc.vector.tensor_tensor(run[:, i, x, :], run[:, i, y, :], TM[:, i, y, :], ALU.max))
                        step.wait()
                    go(nc.vector.tensor_tensor(d(M, 0), back[:, 0, :], d(run, 0), ALU.max))
                    go(nc.vector.tensor_tensor(d(M, 1), bank(7, G4), d(run, 1), ALU.max))
                    go(nc.vector.tensor_tensor(both(B), both(B), both(M), ALU.add))
                    marks["bm"] = step.n

                @block.scalar
                def _(act):
                    act.wait_ge(step_s, marks["abs"])
                    nc.scalar.activation(both(E1), both(E1), ACT.Exp, scale=-1.0).then_inc(astep, 1)
                    act.wait_ge(astep, 1)
                    nc.scalar.activation(both(E1), both(E1), ACT.Ln, bias=1.0).then_inc(astep, 1)
                    act.wait_ge(step_s, marks["bm"])
                    nc.scalar.activation(both(EM), both(B), ACT.Exp, scale=-1.0).then_inc(astep, 1)

                @block.tensor
                def _(pe):
                    pe.wait_ge(step_s, marks["lf"])
                    for i in range(2):
                        nc.tensor.matmul(bank(i, G4), cum[i], d(F, i), start=True, stop=True).then_inc(pstep, 1)
                    nc.tensor.matmul(bank(2, 2 * G4), ones[:, :], both(F), start=True, stop=True).then_inc(pstep, 1)
                    pe.wait_ge(step_s, marks["a"])
                    nc.tensor.matmul(bank(3, P)[0:G4, :], d(A, 0), ident, start=True, stop=True).then_inc(pstep, 1)
                    nc.tensor.matmul(bank(4, P)[0:G4, :], d(A, 1), rev, start=True, stop=True).then_inc(pstep, 1)
                    pe.wait_ge(step_s, marks["scan"])
                    for i in range(2):
                        mm = nc.tensor.matmul(bank(5, G4, G4 * i), sc[1][:, i, PAD:PAD + P], ident[0:G4, 0:G4], start=True, stop=True)
                    mm.then_inc(pstep, 1)
                    pe.wait_ge(step_s, marks["back"])
                    nc.tensor.matmul(bank(6, 2 * G4), e127, back[:, :, :].rearrange("p a n -> p (a n)"), start=True, stop=True).then_inc(pstep, 1)
                    nc.tensor.matmul(bank(7, G4), rev, back[:, 1, :], start=True, stop=True).then_inc(pstep, 1)

    def mlstm_mix(l, R, qkT, v, so, A, M, EM, yT, nq):
        st = ExitStack()
        nblk = 3 if nq == NT else 2
        RING = 10
        with st:
            tag = f"mlm{l}"
            hs = sb(f"hs_{tag}", [P, NT, GW], st)
            dg = [sb(f"dg{i}_{tag}", [P, 512], st) for i in range(2)]
            nmd = sb(f"nmd_{tag}", [P, 2, 512], st)
            wt = [sb(f"wt{i}_{tag}", [P, 512], st) for i in range(2)]
            pr = [hT[:, :, :].rearrange("p c t -> p (c t)")[:, i * 512:(i + 1) * 512] for i in range(RING)]
            den = sb(f"den_{tag}", [P, 2, 4], st)
            ob = sb(f"ob_{tag}", [P, 2, 4, HD], st)
            ss = sb(f"ss_{tag}", [P, NT, H], st)
            step_s, diag, neg, masked, scored = (sem(f"{n}_{tag}") for n in ("dve_step", "diag", "neg_max", "masked", "scored"))
            weighed, product, summed, taken = (sem(f"{n}_{tag}") for n in ("weighed", "product", "summed", "taken"))
            sums, inv, ready, turned, kept, pstep = (sem(f"{n}_{tag}") for n in ("sums", "inv", "ready", "turned", "kept", "pool_step"))
            used = sem(f"used_{tag}")
            units = []
            for blk in range(nblk):
                t0, m, s = BLOCKS[blk]
                q0, q1 = t0 // P, (t0 + m) // P
                for h in range(H):
                    jobs = []
                    for kt in ([8, 9] + list(range(LT)) if s == 0 else [8, 9]):
                        for i in range(2):
                            if s == 0 and kt >= LT:
                                lo, hi = q0, q1
                            elif i == 0:
                                lo, hi = max(q0, kt), q1
                            else:
                                lo, hi = q0, min(q1, kt + 1)
                            if lo < hi:
                                jobs.append((i, kt, lo, hi))
                    units.append((blk, h, q0, q1, s, jobs))
            tiles = []
            for n, (blk, h, q0, q1, s, jobs) in enumerate(units):
                for kt in dict.fromkeys(j[1] for j in jobs):
                    tiles.append((n, kt, [j for j in jobs if j[1] == kt]))
            jobs_all = [(n, j) for n, kt, js in tiles for j in js]
            jobs_end = [sum(1 for n, _ in jobs_all if n <= u) for u in range(len(units))]
            first_tile = [min(x for x, t in enumerate(tiles) if t[0] == u) for u in range(len(units))]

            def diag_in(j, q0, q1):
                return q0 <= j[1] < q1

            def pieces(n, j):
                q0, q1 = units[n][2], units[n][3]
                d = diag_in(j, q0, q1)
                return int(d) + int(j[3] - j[2] > int(d))
            wjob, wcount, pcount, jfirst = [], {}, [], []
            w = 0
            for n, j in jobs_all:
                w += pieces(n, j)
                wjob.append(w)
                wcount[n] = w
            done = 0
            for n, kt, js in tiles:
                jfirst.append(done)
                done += len(js)
                pcount.append(done)
            last_job = [[[j for j in unit[5] if j[0] == i][-1] for i in range(2)] for unit in units]

            with nc.Block() as block:
                @block.tensor
                def _(pe):
                    def maxima(u):
                        blk, h, q0, q1, s, jobs = units[u]
                        w = (q1 - q0) * P
                        for i in range(2):
                            pe.wait_ge(diag, 2 * u + i + 1)
                            if u >= 1 and i == 0:
                                pe.wait_ge(weighed, wcount[u - 1])
                                pe.wait_ge(masked, 2 * u)
                            nc.tensor.matmul(bank(i, w), ones[:, :], dg[i][:, 0:w], start=True, stop=True).then_inc(neg, 1)

                    def scores(x):
                        u, kt, js = tiles[x]
                        blk, h, q0, q1, s, jobs = units[u]
                        if x >= 4:
                            pe.wait_ge(product, pcount[x - 4])
                        p0 = HD * (h % 2)
                        lo, hi = min(j[2] for j in js), max(j[3] for j in js)
                        nc.tensor.matmul(bank(2 + x % 4, (hi - lo) * P, (lo - q0) * P), qkT[p0:p0 + HD, 2 + h // 2, kt * P:(kt + 1) * P],
                                         qkT[p0:p0 + HD, h // 2, lo * P:hi * P], start=True, stop=True).then_inc(scored, 1)

                    def values(x):
                        u, kt, js = tiles[x]
                        blk, h, q0, q1, s, jobs = units[u]
                        for y, j in enumerate(js):
                            n = jfirst[x] + y
                            pe.wait_ge(product, n + 1)
                            if x == first_tile[u] and u >= 1 and y == 0:
                                pe.wait_ge(taken, u)
                            i = j[0]
                            first_job = jobs.index(j) == min(jobs.index(k) for k in jobs if k[0] == i)
                            for q in range(j[2], j[3]):
                                mm = nc.tensor.matmul(bank(6 + i, HD + 1, (q - q0) * (HD + 1)), pr[n % RING][:, (q - q0) * P:(q - q0 + 1) * P],
                                                      v[:, kt, h, :], start=(first_job and q == j[2]), stop=(j is last_job[u][i] and q == j[3] - 1),
                                                      skip_group_check=True)
                            mm.then_inc(used, 1)

                    LEAD = 2
                    maxima(0)
                    for x in range(len(tiles) + LEAD):
                        if x < len(tiles):
                            if x >= 1 and tiles[x][0] != tiles[x - 1][0]:
                                maxima(tiles[x][0])
                            scores(x)
                        if x >= LEAD:
                            values(x - LEAD)
                    for t in range(nq):
                        pe.wait_ge(ready, t + 1)
                        if t >= 2:
                            pe.wait_ge(kept, t - 1)
                        else:
                            pe.wait_ge(product, len(jobs_all))
                        for c in range(2):
                            mm = nc.tensor.transpose(bank(2 + t % 2, P, c * P), hs[:, t, c * P:(c + 1) * P], ident)
                        mm.then_inc(turned, 1)

                @block.scalar
                def _(act):
                    n = 0
                    for x, (u, kt, js) in enumerate(tiles):
                        blk, h, q0, q1, s, jobs = units[u]
                        for j in js:
                            i = j[0]
                            act.wait_ge(neg, 2 * u + i + 1)
                            act.wait_ge(masked, 2 * u + i + 1)
                            if n >= 2:
                                act.wait_ge(product, n - 1)
                            ak = A[:, i, kt, h:h + 1]
                            lo, hi = (j[2] - q0) * P, (j[3] - q0) * P
                            if diag_in(j, q0, q1):
                                dlo = (kt - q0) * P
                                nc.scalar.activation(wt[n % 2][:, dlo:dlo + P], nmd[:, i, dlo:dlo + P], ACT.Exp, bias=ak).then_inc(weighed, 1)
                                if i == 0:
                                    lo = dlo + P
                                else:
                                    hi = dlo
                            if lo < hi:
                                nc.scalar.activation(wt[n % 2][:, lo:hi], bank(i, hi - lo, lo), ACT.Exp, bias=ak).then_inc(weighed, 1)
                            n += 1
                    for t in range(nq):
                        act.wait_ge(turned, t + 1)
                        nc.scalar.activation(yT[:, 4:6, t * P:(t + 1) * P], bank(2 + t % 2, 2 * P).rearrange("p (c t) -> p c t", c=2), ACT.Copy).then_inc(kept, 1)

                @block.vector
                def _(dve):
                    step = Chain(dve, step_s)

                    def diagonals(u):
                        blk, h, q0, q1, s, jobs = units[u]
                        nt = q1 - q0
                        for i in range(2):
                            if u >= 1:
                                dve.wait_ge(neg, 2 * u)
                            nc.vector.scalar_tensor_tensor(out=dg[i][:, 0:nt * P].rearrange("p (t m) -> p t m", t=nt),
                                                           in0=ident.unsqueeze(1).broadcast_to([P, nt, P]), scalar=-1.0,
                                                           in1=M[:, i, q0:q1, h:h + 1].broadcast_to([P, nt, P]),
                                                           op0=ALU.mult, op1=ALU.mult).then_inc(diag, 1)

                    def mask(u):
                        blk, h, q0, q1, s, jobs = units[u]
                        nt = q1 - q0
                        for i in range(2):
                            dve.wait_ge(neg, 2 * u + i + 1)
                            if u >= 1:
                                dve.wait_ge(weighed, wcount[u - 1])
                            m = cst[:, (C_MASK0, C_MASK1)[i]:(C_MASK0, C_MASK1)[i] + P].unsqueeze(1).broadcast_to([P, nt, P])
                            nc.vector.tensor_tensor(nmd[:, i, 0:nt * P].rearrange("p (t m) -> p t m", t=nt),
                                                    bank(i, nt * P).rearrange("p (t m) -> p t m", t=nt), m, ALU.add).then_inc(masked, 1)

                    def take(u):
                        blk, h, q0, q1, s, jobs = units[u]
                        nt = q1 - q0
                        dve.wait_ge(used, jobs_end[u])
                        pv = [bank(6 + i, nt * (HD + 1)).rearrange("p (t d) -> p t d", t=nt) for i in range(2)]
                        for i in range(2):
                            step.then(nc.vector.tensor_tensor(den[:, i, 0:nt].unsqueeze(2), pv[i][:, :, HD:HD + 1], EM[:, i, q0:q1, h:h + 1], ALU.max))
                        step.wait()
                        for i in range(2):
                            step.then(nc.vector.scalar_tensor_tensor(out=den[:, i, 0:nt].unsqueeze(2), in0=pv[i][:, :, HD:HD + 1], scalar=-1.0,
                                                                     in1=den[:, i, 0:nt].unsqueeze(2), op0=ALU.mult, op1=ALU.max))
                        step.wait()
                        step.then(nc.vector.reciprocal(den[:, :, 0:nt], den[:, :, 0:nt]))
                        step.wait()
                        for i in range(2):
                            step.then(nc.vector.tensor_tensor(ob[:, i, 0:nt, :], pv[i][:, :, 0:HD],
                                                              den[:, i, 0:nt].unsqueeze(2).broadcast_to([P, nt, HD]), ALU.mult))
                        step.wait()
                        nc.vector.tensor_tensor(hs[:, q0:q1, h * HD:(h + 1) * HD], ob[:, 0, 0:nt, :], ob[:, 1, 0:nt, :], ALU.add).then_inc(taken, 1)

                    diagonals(0)
                    mask(0)
                    n = 0
                    for x, (u, kt, js) in enumerate(tiles):
                        blk, h, q0, q1, s, jobs = units[u]
                        if x >= 1 and tiles[x - 1][0] != u:
                            mask(u)
                        for j in js:
                            lo, hi = (j[2] - q0) * P, (j[3] - q0) * P
                            dve.wait_ge(scored, x + 1)
                            dve.wait_ge(weighed, wjob[n])
                            if n >= RING:
                                dve.wait_ge(used, n - RING + 1)
                            nc.vector.scalar_tensor_tensor(out=pr[n % RING][:, lo:hi], in0=bank(2 + x % 4, hi - lo, lo), scalar=HD ** -0.5,
                                                           in1=wt[n % 2][:, lo:hi], op0=ALU.mult, op1=ALU.mult).then_inc(product, 1)
                            n += 1
                        if x + 1 < len(tiles) and tiles[x + 1][0] != u:
                            diagonals(u + 1)
                        if x + 1 == len(tiles) or tiles[x + 1][0] != u:
                            take(u)
                    dve.wait_ge(taken, len(units))
                    for t in range(nq):
                        hv = hs[:, t, :].rearrange("p (h d) -> p h d", h=H)
                        sqv = pr[t % 2][:, 0:GW]
                        step.then(nc.vector.tensor_tensor(sqv, hs[:, t, :], hs[:, t, :], ALU.mult))
                        step.wait()
                        nc.vector.tensor_reduce(ss[:, t, :], sqv.rearrange("p (h d) -> p h d", h=H), AX, ALU.add).then_inc(sums, 1)
                    for t in range(nq):
                        hv = hs[:, t, :].rearrange("p (h d) -> p h d", h=H)
                        dve.wait_ge(inv, 1)
                        step.then(nc.vector.tensor_tensor(hv, hv, ss[:, t, :].unsqueeze(2).broadcast_to([P, H, HD]), ALU.mult))
                        step.wait()
                        step.then(nc.vector.tensor_tensor(hv, hv, R["mlstm_g_out"].unsqueeze(1).broadcast_to([P, H, HD]), ALU.mult))
                        step.wait()
                        nc.vector.tensor_tensor(hs[:, t, :].rearrange("p (c d) -> p c d", c=2), hs[:, t, :].rearrange("p (c d) -> p c d", c=2), so(t), ALU.mult).then_inc(ready, 1)

                @block.gpsimd
                def _(pool):
                    pool.wait_ge(sums, nq)
                    f = ss[:, 0:nq, :].rearrange("p t h -> p (t h)")
                    nc.gpsimd.tensor_scalar(f, f, 1.0 / HD, EPS, ALU.mult, ALU.add).then_inc(pstep, 1)
                    pool.wait_ge(pstep, 1)
                    nc.gpsimd.tensor_tensor(f, f, half[:, 0:1].broadcast_to([P, nq * H]), ALU.pow).then_inc(inv, 1)
    for l in range(DEPTH):
        need = l < DEPTH - 1
        mine = BLOCKS if need else BLOCKS[:2]
        modulation(l, xT)
        st = ExitStack()
        with st:
            hT = sb(f"hT{l}", [P, DC, T], st)
            norm(l, 0, BLOCKS, xT, (hT,), spill=(l == 0))
            x_stack.close()
            clear_semaphores()
            yT = sb(f"yT{l}", [P, DC, T], st)
            mixers(l, yT, need)
            x_stack = ExitStack()
            xT = take_x(x_stack, f"x_mid{l}")
            add_product(f"out{l}", l, a["w_out"][l], DC, yT, 16, mine, xT, reload=True)
        st = ExitStack()
        with st:
            hh, hl = sbr(f"h_high{l}", [P, DC, T], st), sbr(f"h_low{l}", [P, DC, T], st)
            norm(l, 1, mine, xT, (hh, hl), spill=True)
            x_stack.close()
            clear_semaphores()
            ffn(l, mine, hh, hl)
            clear_semaphores()
        x_stack = ExitStack()
        xT = take_x(x_stack, f"x_end{l}")
    leave(xT)
    x_stack.close()


_INS = ['x', 'c', 'ctx', 'c_ctx', 'w_mod', 'b_mod', 'g_norm1', 'g_norm2', 'w_in', 'w_out',
        'diff_g_q', 'diff_g_k', 'diff_lam', 'diff_g_out', 'mla_g_cq', 'mla_g_ckv', 'mla_w_uq', 'mla_w_ukv',
        'mla_g_q', 'mla_g_k', 'mlstm_w_conv', 'mlstm_b_i', 'mlstm_b_f', 'mlstm_g_out',
        'na_g_q', 'na_g_k', 'na_rpb', 'ffn_w_up', 'ffn_w_conv', 'ffn_w_down']


def kernel(**inputs):
    import concourse.bacc as bacc
    from concourse.bass_utils import run_bass_kernel_spmd

    nc = bacc.Bacc("TRN2", target_bir_lowering=False, num_devices=1)
    arrays, args = {}, {}
    for name in _INS:
        v = np.ascontiguousarray(inputs[name])
        arrays[f"in_{name}"] = v
        args[name] = nc.dram_tensor(f"in_{name}", v.shape, F32, kind="ExternalInput").ap()
    arrays["in_consts"] = shape_constants()
    args["consts"] = nc.dram_tensor("in_consts", (P, C_N), F32, kind="ExternalInput").ap()
    out = nc.dram_tensor("out", (1, SEQ, D), F32, kind="ExternalOutput").ap()
    build(nc, args, out)
    r = run_bass_kernel_spmd(nc, [arrays], core_ids=[0])
    return r.results[0]["out"]
```

```python
import math
from contextlib import ExitStack

import numpy as np
import concourse.bass as bass
from concourse import mybir

F32 = mybir.dt.float32
F32R = mybir.dt.float32r
ALU = mybir.AluOpType
ACT = mybir.ActivationFunctionType
AX = mybir.AxisListType.X

P = 128
D = 1024
DC = D // P
DEPTH = 2
SEQ = 1024
CTX = 256
T = SEQ + CTX
NT = T // P
LT = SEQ // P
H = 4
HD = 64
GW = H * HD
GRID_W = 64
DQK = 32
ROPE = 32
MQ = 256
MKV = 128
MD = 96
HID = 2816
HC = HID // P
WIN_R = 8
WIN_C = 16
NROW = SEQ // GRID_W
EPS = 1e-6
NEG = -1e30
BANK = 512

OFF = {}
_o = 0
for _n, _w in (("diff", 768), ("mla", 416), ("mlqk", 512), ("mlvo", 512), ("mlg", 16), ("na", 768)):
    OFF[_n] = _o
    _o += _w
IN_WIDTH = _o
BLOCKS = [(0, 512, 0), (512, 512, 0), (1024, 256, 1)]

V_BMOD, V_G1, V_G2, V_MCONV, V_GCQ, V_GCKV, V_N = 0, 48, 56, 64, 76, 78, 79
V_FCONV = V_N
V_TOTAL = V_N + 3 * 2 * HC
ROWS = {}
_o = 0
for _n, _w in (("diff_g_q", 32), ("diff_g_k", 32), ("diff_lam", 128), ("diff_g_out", 64), ("mla_g_q", 96),
               ("mla_g_k", 96), ("mlstm_g_out", 64), ("mlstm_b_i", 8), ("mlstm_b_f", 8), ("na_g_q", 64),
               ("na_g_k", 64)):
    ROWS[_n] = (_o, _w)
    _o += _w
ROWS_N = _o

C_ID, C_REV, C_CUM, C_CUMR, C_E127, C_MASK0, C_MASK1, C_COS, C_SIN, C_COL, C_PAIR, C_ROW = (
    0, 128, 256, 384, 512, 640, 768, 896, 896 + 256, 896 + 512, 896 + 512 + 64, 896 + 512 + 128)
C_N = C_ROW + 8 * 12
NSLOT = 18


def row_window(r):
    return min(max(r - WIN_R // 2, 0), NROW - WIN_R)


def pair_window(p):
    return row_window(4 * p) // 2, (row_window(4 * p + 3) + WIN_R + 1) // 2


def shape_constants():
    c = np.zeros((P, C_N), np.float32)
    i = np.arange(P)
    c[:, C_ID:C_ID + P] = np.eye(P)
    c[:, C_REV:C_REV + P] = np.eye(P)[::-1]
    c[:, C_CUM:C_CUM + P] = i[:, None] <= i[None, :]
    c[:, C_CUMR:C_CUMR + P] = i[:, None] >= i[None, :]
    c[P - 1, C_E127:C_E127 + P] = 1.0
    c[:, C_MASK0:C_MASK0 + P] = np.where(i[:, None] <= i[None, :], 0.0, NEG)
    c[:, C_MASK1:C_MASK1 + P] = np.where(i[:, None] >= i[None, :], 0.0, NEG)
    nf = ROPE // 4
    t = np.arange(SEQ)
    inv = (10000.0 ** (-np.arange(nf, dtype=np.float32) / nf)).astype(np.float32)
    ar = (t // GRID_W).astype(np.float32)[:, None] * inv
    ac = (t % GRID_W).astype(np.float32)[:, None] * inv
    cos = np.concatenate([np.cos(ar), np.cos(ar), np.cos(ac), np.cos(ac)], 1)
    sin = np.concatenate([-np.sin(ar), np.sin(ar), -np.sin(ac), np.sin(ac)], 1)
    c[:, C_COS:C_COS + 256] = cos.reshape(LT, P, 32).transpose(1, 0, 2).reshape(P, 256)
    c[:, C_SIN:C_SIN + 256] = sin.reshape(LT, P, 32).transpose(1, 0, 2).reshape(P, 256)
    q = i % GRID_W
    cs = np.clip(q - WIN_C // 2, 0, GRID_W - WIN_C)
    k = np.arange(GRID_W)
    c[:, C_COL:C_COL + 64] = np.where((k[None] >= cs[:, None]) & (k[None] < cs[:, None] + WIN_C), 0.0, NEG)
    c[:, C_PAIR:C_PAIR + HD] = np.concatenate([np.eye(HD), np.eye(HD)])
    for j in range(LT):
        row = 2 * j + i // GRID_W
        rs = np.array([row_window(r) for r in row])
        kr = 2 * pair_window(j // 2)[0] + np.arange(12)
        ok = (kr[None] >= rs[:, None]) & (kr[None] < rs[:, None] + WIN_R)
        c[:, C_ROW + 12 * j:C_ROW + 12 * j + 12] = np.where(ok, 0.0, NEG)
    return c


class Chain:

    def __init__(self, eng, sem):
        self.eng, self.sem, self.n = eng, sem, 0

    def then(self, ins):
        self.n += 1
        ins.then_inc(self.sem, 1)
        return self.n

    def wait(self, n=None):
        self.eng.wait_ge(self.sem, self.n if n is None else n)


def build(nc, a, out):
    ctx = ExitStack()
    with ctx:
        _build(nc, a, out, ctx)


def _build(nc, a, out, ctx):
    def sb(name, shape, stack=ctx):
        return stack.enter_context(nc.sbuf_tensor(name, shape, F32))

    def sbr(name, shape, stack=ctx):
        return stack.enter_context(nc.sbuf_tensor(name, shape, F32R))

    in_use = []

    def sem(name):
        in_use.append(nc.alloc_semaphore(name=name))
        return in_use[-1]

    def clear_semaphores():
        nc.clear_and_free_semaphores(in_use)
        in_use.clear()
        nc.all_engine_barrier()

    ahead = nc.alloc_semaphore(name="fetched_ahead")
    fetched = [0]

    def fetch(eng, dst, src):
        fetched[0] += 16
        eng.dma_start(dst, src).then_inc(ahead, 16)

    cst = sb("cst", [P, C_N])
    ones = sb("ones", [P, P])
    vec = sb("vec", [P, DEPTH, V_TOTAL])
    rows = sb("rows", [P, DEPTH, ROWS_N])
    mod = sb("mod", [P, 48, 2])
    scl = sb("scl", [P, 2, DC, 2])
    cc = sb("cc", [P, DC, 2])
    neglam = sb("neglam", [P, 2])
    half = sb("half", [P, 16])
    ps = ctx.enter_context(nc.psum_tensor("ps", [P, 8 * BANK], F32))
    rpb_pad = nc.dram_tensor("rpb_pad", [DEPTH, H, NSLOT + 1, 127], F32).ap()

    ident = cst[:, C_ID:C_ID + P]
    x_home = nc.dram_tensor("x_home", [P, DC, T], F32).ap()

    def take_x(stack, name):
        return stack.enter_context(nc.sbuf_tensor(name, [P, DC, T], F32, side="right"))

    def bank(b, n=BANK, w=0):
        return ps[:, b * BANK + w:b * BANK + w + n]

    def entry(xT):
        st = ExitStack()
        with st:
            xin = sb("xin", [P, NT, D], st)
            vrows = sb("vrows", [P, 2, 3, P], st)
            craw = sb("craw", [P, DC, 2], st)
            padz = sb("padz", [P, H, 127], st)
            s_x = [sem(f"x_loaded{i}") for i in range(2)]
            s_c = sem("constants_loaded")
            s_c2 = sem("rows_loaded")
            s_r = sem("rpb_loaded")
            s_rd = sem("rpb_written")
            s_ones = sem("ones_set")
            s_zero = sem("pad_zeroed")
            s_turn = sem("x_turned")
            s_kept = sem("x_kept")
            s_vt = sem("vectors_turned")
            s_vk = sem("vectors_kept")
            s_silu = sem("cond_ready")
            s_rows = sem("rows_scaled")
            with nc.Block() as block:
                @block.sync
                def _(sp):
                    sp.dma_start(cst[:, :], a["consts"]).then_inc(s_c, 16)
                    sp.dma_start(xin[:, 0:4, :], a["x"][0].rearrange("(t p) d -> p t d", p=P)[:, 0:4, :]).then_inc(s_x[0], 16)
                    sp.dma_start(xin[:, 4:8, :], a["x"][0].rearrange("(t p) d -> p t d", p=P)[:, 4:8, :]).then_inc(s_x[1], 16)
                    sp.dma_start(xin[:, 8:10, :], a["ctx"][0].rearrange("(t p) d -> p t d", p=P)).then_inc(s_x[1], 16)
                    sp.wait_ge(s_zero, 1)
                    for l in range(DEPTH):
                        sp.dma_start(padz[64 * l + 2:64 * l + 2 + 2 * WIN_R - 1, :, 48:79],
                                     a["na_rpb"][l].rearrange("h s w -> s h w")).then_inc(s_r, 16)
                    sp.wait_ge(s_r, 16 * DEPTH)
                    for l in range(DEPTH):
                        sp.dma_start(rpb_pad[l].rearrange("h s w -> s h w"),
                                     padz[64 * l:64 * l + NSLOT + 1, :, :]).then_inc(s_rd, 16)
                    sp.wait_ge(s_rd, 16 * DEPTH)

                @block.gpsimd
                def _(pool):
                    nc.gpsimd.memset(padz[:, :, :], 0.0).then_inc(s_zero, 1)
                    nc.gpsimd.memset(half[:, :], -0.5)
                    nc.gpsimd.memset(ones[:, :], 1.0).then_inc(s_ones, 1)

                @block.scalar
                def _(act):
                    n = 0
                    for l in range(DEPTH):
                        parts = [(a["b_mod"][l].rearrange("(r p) -> r p", p=P), 0, 48, 0),
                                 (a["g_norm1"][l].rearrange("(r p) -> r p", p=P), V_G1, 8, 0),
                                 (a["g_norm2"][l].rearrange("(r p) -> r p", p=P), V_G2, 8, 0),
                                 (a["mlstm_w_conv"][l].rearrange("k (r p) -> (k r) p", p=P), V_MCONV, 12, 0),
                                 (a["mla_g_cq"][l].rearrange("(r p) -> r p", p=P), V_GCQ, 2, 0),
                                 (a["mla_g_ckv"][l].rearrange("(r p) -> r p", p=P), V_GCKV, 1, 0),
                                 (a["ffn_w_conv"][l].rearrange("k (r p) -> (k r) p", p=P)[0:66], 0, 66, 1),
                                 (a["ffn_w_conv"][l].rearrange("k (r p) -> (k r) p", p=P)[66:132], 0, 66, 2)]
                        for src, r0, nr, j in parts:
                            act.dma_start(vrows[r0:r0 + nr, l, j, :], src).then_inc(s_c, 16)
                            n += 1
                        for name, (o, w) in ROWS.items():
                            src = a[name][l]
                            if len(src.shape) == 2:
                                src = src.rearrange("a b -> (a b)")
                            act.dma_start(rows[:, l, o:o + w], src.partition_broadcast(P)).then_inc(s_c2, 16)
                    act.dma_start(craw[:, :, 0], a["c"][0].rearrange("(c p) -> p c", p=P),
                                  allow_slow_non_contiguous=True).then_inc(s_c2, 16)
                    act.dma_start(craw[:, :, 1], a["c_ctx"].rearrange("(c p) -> p c", p=P),
                                  allow_slow_non_contiguous=True).then_inc(s_c2, 16)
                    act.wait_ge(s_c2, 16 * (DEPTH * len(ROWS) + 2))
                    nc.scalar.activation(cc[:, :, :], craw[:, :, :], ACT.Silu).then_inc(s_silu, 1)
                    act.wait_ge(s_silu, 1)

                @block.tensor
                def _(pe):
                    pe.wait_ge(s_c, 16 * (1 + 8 * DEPTH))
                    for l in range(DEPTH):
                        if l >= 1:
                            pe.wait_ge(s_vk, 3 * l)
                        for j, (nr, b) in enumerate(((V_N, 0), (66, 1), (66, 2))):
                            mm = nc.tensor.transpose(bank(b, nr), vrows[0:nr, l, j, :], ident[0:nr, 0:nr])
                        mm.then_inc(s_vt, 1)
                    n = 0
                    for t in range(NT):
                        if t == 0:
                            pe.wait_ge(s_x[0], 16)
                        if t == 4:
                            pe.wait_ge(s_x[1], 32)
                        for g in range(2):
                            if n >= 4:
                                pe.wait_ge(s_kept, n - 3)
                            for c in range(4):
                                mm = nc.tensor.transpose(bank(4 + n % 4, P, c * P), xin[:, t, (4 * g + c) * P:(4 * g + c + 1) * P], ident)
                            mm.then_inc(s_turn, 1)
                            n += 1

                @block.vector
                def _(dve):
                    for l in range(DEPTH):
                        dve.wait_ge(s_vt, l + 1)
                        for j, (nr, o) in enumerate(((V_N, 0), (66, V_N), (66, V_N + 66))):
                            nc.vector.tensor_copy(vec[:, l, o:o + nr], bank(j, nr)).then_inc(s_vk, 1)
                    n = 0
                    for t in range(NT):
                        for g in range(2):
                            dve.wait_ge(s_turn, n + 1)
                            nc.vector.tensor_copy(xT[:, 4 * g:4 * g + 4, t * P:(t + 1) * P],
                                                  bank(4 + n % 4).rearrange("p (c t) -> p c t", c=4)).then_inc(s_kept, 1)
                            n += 1
                    dve.wait_ge(s_c2, 16 * (DEPTH * len(ROWS) + 2))
                    for l in range(DEPTH):
                        lam0 = 0.8 - 0.6 * math.exp(-0.3 * l)
                        for name, f in (("diff_g_q", DQK ** -0.5), ("diff_g_out", 1.0 - lam0),
                                        ("mla_g_q", MD ** -0.5), ("na_g_q", HD ** -0.5)):
                            o, w = ROWS[name]
                            nc.vector.tensor_scalar(rows[:, l, o:o + w], rows[:, l, o:o + w], f, None, ALU.mult).then_inc(s_rows, 1)
                    dve.wait_ge(s_rows, 8)

    x_stack = ExitStack()
    xT = take_x(x_stack, "x0")
    entry(xT)
    clear_semaphores()
    def modulation(l, xT):
        st = ExitStack()
        CH = 6 * D // 512
        with st:
            wm = [sb(f"wm{i}_{l}", [P, DC, 512], st) for i in range(2)]
            row = [sb(f"row{i}_{l}", [P, 512], st) for i in range(2)]
            lv = sb(f"lv{l}", [P, 2, 32], st)
            ls = sb(f"ls{l}", [P, 2], st)
            w_in = [sem(f"mod_w{i}_{l}") for i in range(2)]
            w_used, rkept = sem(f"mod_w_used{l}"), sem(f"mod_row_kept{l}")
            turned, done = sem(f"mod_turned{l}"), sem(f"mod_kept{l}")
            lam = sem(f"lam{l}")
            lame = sem(f"lame{l}")
            x_back = sem(f"mod_x_back{l}")
            w = a["w_mod"][l].rearrange("(c p) n -> p c n", p=P)
            with nc.Block() as block:
                @block.sync
                def _(sp):
                    for i in range(2):
                        sp.dma_start(wm[i][:, :, :], w[:, :, i * 512:(i + 1) * 512]).then_inc(w_in[i], 16)
                    with sp.Fori(0, CH // 2 - 1) as n:
                        for i in range(2):
                            sp.wait_ge(w_used, n * 2 + (i + 1))
                            sp.dma_start(wm[i][:, :, :], w[:, :, bass.ds(n * 1024 + (1024 + 512 * i), 512)]).then_inc(w_in[i], 16)
                    if l > 0:
                        sp.dma_start(xT[:, :, :], x_home).then_inc(x_back, 16)
                        sp.wait_ge(x_back, 16)

                @block.tensor
                def _(pe):
                    def rows_of(i, t, n):
                        pe.wait_ge(w_in[i], n * 16 + 16)
                        pe.wait_ge(rkept, t + 1)
                        for c in range(DC):
                            mm = nc.tensor.matmul(bank(i)[0:2, :], cc[:, c, :], wm[i][:, c, :], start=(c == 0), stop=(c == DC - 1))
                        mm.then_inc(w_used, 1)

                    def turn(i, t):
                        pe.wait_ge(rkept, t + 3)
                        pe.wait_ge(done, t + 1)
                        for f in range(4):
                            mm = nc.tensor.matmul(bank(2 + i, 2, 2 * f), row[i][0:2, f * P:(f + 1) * P], ident[0:2, 0:2], start=True, stop=True)
                        mm.then_inc(turned, 1)

                    rows_of(0, 0, 0)
                    with pe.Fori(0, CH // 2 - 1) as n:
                        rows_of(1, n * 2 + 1, n)
                        turn(0, n * 2)
                        rows_of(0, n * 2 + 2, n + 1)
                        turn(1, n * 2 + 1)
                    rows_of(1, CH - 1, CH // 2 - 1)
                    turn(0, CH - 2)
                    turn(1, CH - 1)

                @block.vector
                def _(dve):
                    dve.sem_inc(done, 2)
                    with dve.Fori(0, CH // 2) as n:
                        for i in range(2):
                            dve.wait_ge(turned, n * 2 + (i + 3))
                            b = vec[:, l, bass.ds(n * 8 + 4 * i, 4)].unsqueeze(2).broadcast_to([P, 4, 2])
                            nc.vector.tensor_tensor(mod[:, bass.ds(n * 8 + 4 * i, 4), :],
                                                    bank(2 + i, 8).rearrange("p (f s) -> p f s", s=2), b, ALU.add).then_inc(done, 1)
                    dve.wait_ge(done, 14)
                    for k, (sc, g) in enumerate(((8, V_G1), (32, V_G2))):
                        gb = vec[:, l, g:g + DC].unsqueeze(2).broadcast_to([P, DC, 2])
                        nc.vector.scalar_tensor_tensor(out=scl[:, k, :, :], in0=mod[:, sc:sc + DC, :], scalar=1.0, in1=gb,
                                                       op0=ALU.add, op1=ALU.mult).then_inc(done, 1)
                    o = ROWS["diff_lam"][0]
                    v = rows[:, l, o:o + 128].rearrange("p (a b d) -> p a b d", a=2, b=2)
                    nc.vector.tensor_tensor(lv[:, :, :], v[:, :, 0, :], v[:, :, 1, :], ALU.mult).then_inc(lam, 1)
                    dve.wait_ge(lam, 1)
                    nc.vector.tensor_reduce(ls[:, :], lv[:, :, :], AX, ALU.add).then_inc(lam, 1)
                    dve.wait_ge(lame, 1)
                    nc.vector.scalar_tensor_tensor(out=neglam[:, 0:1], in0=ls[:, 1:2], scalar=-(0.8 - 0.6 * math.exp(-0.3 * l)),
                                                   in1=ls[:, 0:1], op0=ALU.add, op1=ALU.subtract).then_inc(lam, 1)
                    dve.wait_ge(lam, 3)

                @block.scalar
                def _(act):
                    act.sem_inc(rkept, 2)
                    act.sem_inc(turned, 2)
                    with act.Fori(0, CH // 2) as n:
                        for i in range(2):
                            act.wait_ge(w_used, n * 2 + (i + 1))
                            act.wait_ge(turned, n * 2 + (i + 1))
                            nc.scalar.activation(row[i][0:2, :], bank(i)[0:2, :], ACT.Copy).then_inc(rkept, 1)
                    act.wait_ge(lam, 2)
                    nc.scalar.activation(ls[:, :], ls[:, :], ACT.Exp).then_inc(lame, 1)

    def norm(l, k, blocks, xT, dst, spill, meanwhile=None):
        st = ExitStack()
        split = len(dst) == 2
        with st:
            sq = [sb(f"sq{i}_{l}{k}", [P, DC, 512], st) for i in range(2)]
            rs = [sb(f"rs{i}_{l}{k}", [P, 512], st) for i in range(2)]
            squared, summed, mean, root, inv, normed, high, low, low_odd, ready, spilled = (
                sem(f"{n}{l}{k}") for n in ("squared", "summed", "mean", "root", "inv", "normed", "h_high", "h_low", "h_low_odd", "h_ready", "x_spilled"))
            sh = 24 * k

            def scaled(i, c):
                t0, n, s = blocks[i]
                return sq[i % 2][:, c, 0:n] if split else dst[0][:, c, t0:t0 + n]

            with nc.Block() as block:
                @block.sync
                def _(sp):
                    if meanwhile:
                        meanwhile(sp)
                    if spill:
                        sp.dma_start(x_home, xT[:, :, :]).then_inc(spilled, 16)
                        sp.wait_ge(spilled, 16)

                @block.tensor
                def _(pe):
                    for i, (t0, n, s) in enumerate(blocks):
                        for c in range(DC):
                            pe.wait_ge(squared, DC * i + c + 1)
                            mm = nc.tensor.matmul(bank(i, n), ones[:, :], sq[i % 2][:, c, 0:n], start=(c == 0), stop=(c == DC - 1))
                        mm.then_inc(summed, 1)

                @block.scalar
                def _(act):
                    def squares(i):
                        t0, n, s = blocks[i]
                        if i >= 2:
                            act.wait_ge(summed, i - 1)
                            if split:
                                act.wait_ge(low, DC // 2 * (i - 1))
                                act.wait_ge(low_odd, DC // 2 * (i - 1))
                        for c in range(DC):
                            nc.scalar.activation(sq[i % 2][:, c, 0:n], xT[:, c, t0:t0 + n], ACT.Square).then_inc(squared, 1)
                    squares(0)
                    for i, (t0, n, s) in enumerate(blocks):
                        if i + 1 < len(blocks):
                            squares(i + 1)
                        act.wait_ge(mean, i + 1)
                        nc.scalar.activation(rs[i % 2][:, 0:n], rs[i % 2][:, 0:n], ACT.Sqrt).then_inc(root, 1)
                        for c in range(DC):
                            act.wait_ge(normed, DC * i + c + 1)
                            x = scaled(i, c)
                            by = dict(bias=mod[:, sh + c, s:s + 1], scale=scl[:, k, c, s:s + 1])
                            if split:
                                act.wait_ge(ready, DC * i + c + 1)
                                nc.scalar.activation(dst[0][:, c, t0:t0 + n], x, ACT.Copy).then_inc(high, 1)
                            else:
                                nc.scalar.activation(x, x, ACT.Identity, **by).then_inc(ready, 1)

                @block.gpsimd
                def _(pool):
                    if split:
                        for i, (t0, n, s) in enumerate(blocks):
                            for c in range(0, DC, 2):
                                pool.wait_ge(high, DC * i + c + 1)
                                nc.gpsimd.tensor_tensor(dst[1][:, c, t0:t0 + n], scaled(i, c), dst[0][:, c, t0:t0 + n].bitcast(F32),
                                                        ALU.subtract).then_inc(low, 1)

                @block.vector
                def _(dve):
                    for i, (t0, n, s) in enumerate(blocks):
                        dve.wait_ge(summed, i + 1)
                        if i >= 2:
                            dve.wait_ge(normed, DC * (i - 1))
                        nc.vector.tensor_scalar(rs[i % 2][:, 0:n], bank(i, n), 1.0 / D, EPS, ALU.mult, ALU.add).then_inc(mean, 1)
                        dve.wait_ge(root, i + 1)
                        nc.vector.reciprocal(rs[i % 2][:, 0:n], rs[i % 2][:, 0:n]).then_inc(inv, 1)
                        dve.wait_ge(inv, i + 1)
                        for c in range(DC):
                            nc.vector.tensor_tensor(scaled(i, c), xT[:, c, t0:t0 + n], rs[i % 2][:, 0:n],
                                                    ALU.mult).then_inc(normed, 1)
                        if split:
                            for c in range(DC):
                                dve.wait_ge(normed, DC * i + c + 1)
                                nc.vector.tensor_scalar(scaled(i, c), scaled(i, c), scl[:, k, c, s:s + 1], mod[:, sh + c, s:s + 1],
                                                        ALU.mult, ALU.add).then_inc(ready, 1)
                            for c in range(1, DC, 2):
                                dve.wait_ge(high, DC * i + c + 1)
                                nc.vector.tensor_tensor(dst[1][:, c, t0:t0 + n], scaled(i, c), dst[0][:, c, t0:t0 + n].bitcast(F32),
                                                        ALU.subtract).then_inc(low_odd, 1)

    def project_out(l, blocks, yT, xT):
        st = ExitStack()
        nb = len(blocks)
        with st:
            yh, yl = sbr(f"y_high{l}", [P, DC, T], st), sbr(f"y_low{l}", [P, DC, T], st)
            wr = [sb(f"wo{i}_{l}", [P, DC, P], st) for i in range(2)]
            wh = [sbr(f"woh{i}_{l}", [P, DC, P], st) for i in range(2)]
            wl = [sbr(f"wol{i}_{l}", [P, DC, P], st) for i in range(2)]
            loaded, high, low, multiplied = ([sem(f"{n}{i}_out{l}") for i in range(2)] for n in ("loaded", "w_high", "w_low", "mult"))
            y_high, y_low, added, x_back = (sem(f"{n}_out{l}") for n in ("y_high", "y_low", "added", "x_back"))
            wv = a["w_out"][l].rearrange("(k p) n -> p k n", p=P)
            with nc.Block() as block:
                @block.sync
                def _(sp):
                    for i in range(2):
                        sp.dma_start(wr[i][:, :, :], wv[:, :, i * P:(i + 1) * P]).then_inc(loaded[i], 16)
                    sp.dma_start(xT[:, :, :], x_home).then_inc(x_back, 16)
                    with sp.Fori(0, DC // 2 - 1) as n:
                        for i in range(2):
                            sp.wait_ge(low[i], n + 1)
                            sp.dma_start(wr[i][:, :, :], wv[:, :, bass.ds(n * (2 * P) + (2 + i) * P, P)]).then_inc(loaded[i], 16)

                @block.tensor
                def _(pe):
                    def output(i, n, first):
                        pe.wait_ge(low[i], n + 1)
                        for j, (t0, w, s) in enumerate(blocks):
                            pe.wait_ge(added, n * (2 * nb) + (nb * i + j + 1))
                            for c in range(DC):
                                if first:
                                    pe.wait_ge(y_low, DC * j + c + 1)
                                for x, (ww, src) in enumerate(((wh, yh), (wh, yl), (wl, yh))):
                                    mm = nc.tensor.matmul(bank(3 * i + j, w), ww[i][:, c, :], src[:, c, t0:t0 + w],
                                                          start=(c == 0 and x == 0), stop=(c == DC - 1 and x == 2))
                            mm.then_inc(multiplied[i], 1)

                    output(0, 0, True)
                    output(1, 0, False)
                    with pe.Fori(0, DC // 2 - 1) as n:
                        for i in range(2):
                            output(i, n + 1, False)

                @block.scalar
                def _(act):
                    def split(i, n):
                        act.wait_ge(loaded[i], n * 16 + 16)
                        nc.scalar.activation(wh[i][:, :, :], wr[i][:, :, :], ACT.Copy).then_inc(high[i], 1)

                    for i in range(2):
                        split(i, 0)
                    for t0, w, s in blocks:
                        for c in range(DC):
                            nc.scalar.activation(yh[:, c, t0:t0 + w], yT[:, c, t0:t0 + w], ACT.Copy).then_inc(y_high, 1)
                    with act.Fori(0, DC // 2 - 1) as n:
                        for i in range(2):
                            act.wait_ge(multiplied[i], n * nb + nb)
                            split(i, n + 1)

                @block.gpsimd
                def _(pool):
                    with pool.Fori(0, DC // 2) as n:
                        for i in range(2):
                            pool.wait_ge(high[i], n + 1)
                            nc.gpsimd.tensor_tensor(wl[i][:, :, :], wr[i][:, :, :], wh[i][:, :, :].bitcast(F32), ALU.subtract).then_inc(low[i], 1)

                @block.vector
                def _(dve):
                    dve.sem_inc(added, 2 * nb)
                    for j, (t0, w, s) in enumerate(blocks):
                        for c in range(DC):
                            dve.wait_ge(y_high, DC * j + c + 1)
                            nc.vector.tensor_tensor(yl[:, c, t0:t0 + w], yT[:, c, t0:t0 + w], yh[:, c, t0:t0 + w].bitcast(F32), ALU.subtract).then_inc(y_low, 1)
                    dve.wait_ge(x_back, 16)
                    with dve.Fori(0, DC // 2) as n:
                        for i in range(2):
                            for j, (t0, w, s) in enumerate(blocks):
                                dve.wait_ge(multiplied[i], n * nb + (j + 1))
                                x = xT[:, bass.ds(n * 2 + i, 1), t0:t0 + w]
                                nc.vector.scalar_tensor_tensor(out=x, in0=bank(3 * i + j, w).unsqueeze(1),
                                                               scalar=mod[:, bass.ds(n * 2 + (16 + i), 1), s],
                                                               in1=x, op0=ALU.mult, op1=ALU.add).then_inc(added, 1)

    def ffn(l, blocks, hh, hl):
        st = ExitStack()
        sizes = [6, 6, 5, 5]
        assert sum(sizes) == HC
        ctx_too = len(blocks) == 3
        nb = len(blocks)
        width = T + 4
        span = (T + 2) if ctx_too else SEQ
        with st:
            wr = [sb(f"wr{i}_{l}", [P, DC, P], st) for i in range(2)]
            wh = [sbr(f"wh{i}_{l}", [P, DC, P], st) for i in range(2)]
            wl = [sbr(f"wl{i}_{l}", [P, DC, P], st) for i in range(2)]
            u = [sb(f"u{i}_{l}", [P, width], st) for i in range(2)]
            cv = [sb(f"cv{i}_{l}", [P, width], st) for i in range(2)]
            ah, al = sbr(f"ah_{l}", [P, max(sizes), T], st), sbr(f"al_{l}", [P, max(sizes), T], st)
            xs = sb(f"xs_{l}", [P, T], st)
            loaded, multiplied, high, low = ([sem(f"up_{n}{i}_{l}") for i in range(2)] for n in ("loaded", "mult", "w_high", "w_low"))
            copied, tap0, tap1, conv = ([sem(f"up_{n}{i}_{l}") for i in range(2)] for n in ("copied", "tap0_", "tap1_", "conv"))
            zeroed, silu, gated, acts = (sem(f"up_{n}_{l}") for n in ("zeroed", "silu", "gated", "acts"))
            a_high = sem(f"up_a_high_{l}")
            added = [sem(f"added{i}_down{l}") for i in range(2)]
            x_in, x_out = ([sem(f"{n}{j}_down{l}") for j in range(nb)] for n in ("x_in", "x_out"))
            wu = a["ffn_w_up"][l].rearrange("(c p) n -> p c n", p=P)
            wd = a["ffn_w_down"][l].rearrange("(k p) n -> p k n", p=P)
            first = [sum(sizes[:g]) for g in range(len(sizes))]
            use = [first[g] + DC // 2 * g for g in range(len(sizes))]
            groups = list(enumerate(sizes))
            last = len(sizes) - 1
            with nc.Block() as block:
                @block.sync
                def _(sp):
                    def load_up(i, n):
                        sp.dma_start(wr[i][:, :, :], wu[:, :, bass.ds(n * P + i * HID, P)]).then_inc(loaded[i], 16)

                    def load_down(i, g, n):
                        k = sizes[g]
                        sp.dma_start(wr[i][:, 0:k, :], wd[:, first[g]:first[g] + k, bass.ds(n * (2 * P) + i * P, P)]).then_inc(loaded[i], 16)

                    def bring_x(j, m):
                        t0, w, s = blocks[j]
                        sp.dma_start(xs[:, t0:t0 + w].unsqueeze(1), x_home[:, bass.ds(m, 1), t0:t0 + w]).then_inc(x_in[j], 16)

                    def store_x(i, g, n):
                        for j, (t0, w, s) in enumerate(blocks):
                            sp.wait_ge(added[i], n * nb + (nb * (4 * g + 1) + j + 1))
                            sp.dma_start(x_home[:, bass.ds(n * 2 + i, 1), t0:t0 + w], xs[:, t0:t0 + w].unsqueeze(1)).then_inc(x_out[j], 16)

                    def next_x(i, g, n, m):
                        for j in range(nb):
                            sp.wait_ge(x_out[j], n * 32 + 16 * (DC * g + i + 1))
                            bring_x(j, m)

                    for i in range(2):
                        load_up(i, 0)
                    for j in range(nb):
                        bring_x(j, 0)
                    for g, size in groups:
                        with sp.Fori(0, size - 1) as n:
                            for i in range(2):
                                sp.wait_ge(low[i], n + (use[g] + 1))
                                load_up(i, n + (first[g] + 1))
                        for i in range(2):
                            sp.wait_ge(low[i], use[g] + size)
                            load_down(i, g, 0)
                        with sp.Fori(0, DC // 2 - 1) as n:
                            for i in range(2):
                                sp.wait_ge(low[i], n + (use[g] + size + 1))
                                load_down(i, g, n + 1)
                                store_x(i, g, n)
                                next_x(i, g, n, n * 2 + (i + 1))
                        for i in range(2):
                            if g < last:
                                sp.wait_ge(low[i], use[g + 1])
                                load_up(i, first[g + 1])
                            store_x(i, g, DC // 2 - 1)
                            if i == 0:
                                next_x(i, g, DC // 2 - 1, DC - 1)
                            elif g < last:
                                next_x(i, g, DC // 2 - 1, 0)
                    for j in range(nb):
                        sp.wait_ge(x_out[j], 16 * DC * len(sizes))

                @block.tensor
                def _(pe):
                    def passes(i, j, src_h, src_l, ks, k_first, k_last):
                        t0, w, s = blocks[j]
                        for k in ks:
                            for x, (ww, src) in enumerate(((wh, src_h), (wh, src_l), (wl, src_h))):
                                mm = nc.tensor.matmul(bank(3 * i + j, w), ww[i][:, k, :], src[:, k, t0:t0 + w],
                                                      start=(k == k_first and x == 0), stop=(k == k_last and x == 2))
                        return mm

                    def hidden(i, g, n):
                        pe.wait_ge(low[i], n + (use[g] + 1))
                        pe.wait_ge(copied[i], n * 2 + (2 * first[g] + 1))
                        for j in range(nb):
                            passes(i, j, hh, hl, range(DC), 0, DC - 1).then_inc(multiplied[i], 1)

                    def output(i, g, n):
                        k = sizes[g]
                        pe.wait_ge(low[i], n + (use[g] + k + 1))
                        for j in range(nb):
                            pe.wait_ge(added[i], n * nb + (nb * 4 * g + j + 1))
                            passes(i, j, ah, al, range(k), 0, k - 1).then_inc(multiplied[i], 1)

                    for g, size in groups:
                        if g:
                            for i in range(2):
                                pe.wait_ge(added[i], nb * (4 * g + 1))
                        with pe.Fori(0, size) as n:
                            for i in range(2):
                                hidden(i, g, n)
                        pe.wait_ge(acts, nb * (first[g] + size))
                        for i in range(2):
                            pe.wait_ge(low[i], use[g] + size + 1)
                            pe.wait_ge(copied[i], 2 * (first[g] + size) + 1)
                            for j in range(nb):
                                passes(i, j, ah, al, range(size - 1), 0, size - 1)
                        pe.wait_ge(acts, nb * (first[g] + size + 1))
                        for i in range(2):
                            for j in range(nb):
                                passes(i, j, ah, al, [size - 1], 0, size - 1).then_inc(multiplied[i], 1)
                        with pe.Fori(0, DC // 2 - 1) as n:
                            for i in range(2):
                                output(i, g, n + 1)

                @block.scalar
                def _(act):
                    def split(i, r):
                        act.wait_ge(loaded[i], r * 16 + 16)
                        if not (isinstance(r, int) and r == 0):
                            act.wait_ge(multiplied[i], r * nb)
                        nc.scalar.activation(wh[i][:, :, :], wr[i][:, :, :], ACT.Copy).then_inc(high[i], 1)

                    def leave_banks(i, g, n):
                        act.wait_ge(multiplied[i], n * nb + nb * (use[g] + 1))
                        act.wait_ge(conv[i], n + (first[g] + 1))
                        nc.scalar.activation(u[i][:, 1:1 + SEQ], bank(3 * i, SEQ), ACT.Copy).then_inc(copied[i], 1)
                        src = bank(3 * i + 2, CTX) if ctx_too else bank(3 * i + 1, 1, 511)
                        dst = u[i][:, SEQ + 3:SEQ + 3 + CTX] if ctx_too else cv[i][:, width - 1:width]
                        nc.scalar.activation(dst, src, ACT.Copy).then_inc(copied[i], 1)

                    for i in range(2):
                        split(i, 0)
                    act.wait_ge(zeroed, 2)
                    for i in range(2):
                        act.sem_inc(copied[i], 1)
                    for g, size in groups:
                        with act.Fori(0, size) as n:
                            for i in range(2):
                                leave_banks(i, g, n)
                                split(i, n + (use[g] + 1))
                            act.wait_ge(conv[1], n + (first[g] + 2))
                            nc.scalar.activation(cv[1][:, 0:span], cv[1][:, 0:span], ACT.Silu).then_inc(silu, 1)
                        with act.Fori(0, DC // 2 - (g == last)) as n:
                            for i in range(2):
                                split(i, n + (use[g] + size + 1))

                @block.gpsimd
                def _(pool):
                    nc.gpsimd.memset(u[0][:, :], 0.0).then_inc(zeroed, 1)
                    nc.gpsimd.memset(u[1][:, :], 0.0).then_inc(zeroed, 1)
                    with pool.Fori(0, HC + DC // 2 * len(sizes)) as r:
                        for i in range(2):
                            pool.wait_ge(high[i], r + 1)
                            nc.gpsimd.tensor_tensor(wl[i][:, :, :], wr[i][:, :, :], wh[i][:, :, :].bitcast(F32), ALU.subtract).then_inc(low[i], 1)

                @block.vector
                def _(dve):
                    for i in range(2):
                        dve.sem_inc(conv[i], 1)
                        dve.sem_inc(added[i], nb)
                    dve.sem_inc(acts, nb)

                    def hidden(g, n):
                        c = n + first[g]
                        for i in range(2):
                            def w(k):
                                return vec[:, l, bass.ds(n + (V_FCONV + k * 2 * HC + i * HC + first[g]), 1)]
                            dve.wait_ge(copied[i], c * 2 + 3)
                            if i == 0:
                                dve.wait_ge(acts, c * nb + nb)
                            nc.vector.tensor_scalar(cv[i][:, 0:span], u[i][:, 0:span], w(0), None, ALU.mult).then_inc(tap0[i], 1)
                            dve.wait_ge(tap0[i], c + 1)
                            nc.vector.scalar_tensor_tensor(out=cv[i][:, 0:span], in0=u[i][:, 1:1 + span], scalar=w(1),
                                                           in1=cv[i][:, 0:span], op0=ALU.mult, op1=ALU.add).then_inc(tap1[i], 1)
                            dve.wait_ge(tap1[i], c + 1)
                            nc.vector.scalar_tensor_tensor(out=cv[i][:, 0:span], in0=u[i][:, 2:2 + span], scalar=w(2),
                                                           in1=cv[i][:, 0:span], op0=ALU.mult, op1=ALU.add).then_inc(conv[i], 1)
                        dve.wait_ge(silu, c + 1)
                        nc.vector.tensor_tensor(cv[0][:, 0:span], cv[0][:, 0:span], cv[1][:, 0:span], ALU.mult).then_inc(gated, 1)
                        dve.wait_ge(gated, c + 1)
                        for t0, m, s in blocks:
                            o = t0 + 2 * s
                            nc.vector.tensor_copy(ah[:, bass.ds(n, 1), t0:t0 + m], cv[0][:, o:o + m].unsqueeze(1)).then_inc(a_high, 1)
                        for j, (t0, m, s) in enumerate(blocks):
                            o = t0 + 2 * s
                            dve.wait_ge(a_high, c * nb + (j + 1))
                            nc.vector.tensor_tensor(al[:, bass.ds(n, 1), t0:t0 + m], cv[0][:, o:o + m].unsqueeze(1),
                                                    ah[:, bass.ds(n, 1), t0:t0 + m].bitcast(F32), ALU.subtract).then_inc(acts, 1)

                    def add(i, g, n):
                        for j, (t0, m, s) in enumerate(blocks):
                            dve.wait_ge(multiplied[i], n * nb + (nb * (use[g] + sizes[g]) + j + 1))
                            dve.wait_ge(x_in[j], n * 32 + 16 * (DC * g + i + 1))
                            nc.vector.scalar_tensor_tensor(out=xs[:, t0:t0 + m], in0=bank(3 * i + j, m),
                                                           scalar=mod[:, bass.ds(n * 2 + (40 + i), 1), s],
                                                           in1=xs[:, t0:t0 + m], op0=ALU.mult, op1=ALU.add).then_inc(added[i], 1)

                    for g, size in groups:
                        with dve.Fori(0, size) as n:
                            hidden(g, n)
                        with dve.Fori(0, DC // 2) as n:
                            for i in range(2):
                                add(i, g, n)

    def leave(xT):
        st = ExitStack()
        with st:
            xo = [sb(f"xo{i}", [P, D], st) for i in range(4)]
            turned = sem("out_turned")
            kept = sem("out_kept")
            stored = [sem(f"out_stored{i}") for i in range(4)]
            back = [sem(f"out_x_back{i}") for i in range(LT // 2)]
            with nc.Block() as block:
                @block.scalar
                def _(act):
                    for i in range(LT // 2):
                        act.dma_start(xT[:, :, 2 * i * P:(2 * i + 2) * P], x_home[:, :, 2 * i * P:(2 * i + 2) * P]).then_inc(back[i], 16)

                @block.tensor
                def _(pe):
                    n = 0
                    for t in range(LT):
                        pe.wait_ge(back[t // 2], 16)
                        for g in range(2):
                            if n >= 8:
                                pe.wait_ge(kept, n - 7)
                            for c in range(4):
                                mm = nc.tensor.transpose(bank(n % 8, P, c * P), xT[:, 4 * g + c, t * P:(t + 1) * P], ident)
                            mm.then_inc(turned, 1)
                            n += 1

                @block.vector
                def _(dve):
                    for n in range(2 * LT):
                        dve.wait_ge(turned, n + 1)
                        if n >= 8 and n % 2 == 0:
                            dve.wait_ge(stored[(n // 2) % 4], 16 * (n // 8))
                        nc.vector.tensor_copy(xo[(n // 2) % 4][:, (n % 2) * 512:(n % 2) * 512 + 512], bank(n % 8)).then_inc(kept, 1)

                @block.sync
                def _(sp):
                    for t in range(LT):
                        sp.wait_ge(kept, 2 * t + 2)
                        sp.dma_start(out[0, t * P:(t + 1) * P, :], xo[t % 4][:, :]).then_inc(stored[t % 4], 16)
                    for i in range(4):
                        sp.wait_ge(stored[i], 32)

    def attention(tag, nh, maps, parts, keys, vs, yT, y0, out_gain=None, table=None, need=True, meanwhile=None):
        st = ExitStack()
        pairs = list(range(NT // 2 if need else LT // 2))
        with st:
            width = max(len(keys(p)) for p in pairs) * P
            units = [(p, h, s) for p in pairs for h in range(nh) for s in range(2)]
            nu, nv = len(units), len(units) // 2
            e = [[sb(f"e{m}{i}_{tag}", [P, width], st) for i in range(2)] for m in range(maps)]
            hi = sbr(f"hi_{tag}", [P, width // P, 2 * P], st)
            lo = sbr(f"lo_{tag}", [P, width // P, 2 * P], st)
            mx, nm, zs = (sb(f"{n}_{tag}", [P, 4], st) for n in ("mx", "nm", "zs"))
            rz, rw = sb(f"rz_{tag}", [P, 8], st), sb(f"rw_{tag}", [P, 8], st)
            oT = sb(f"oT_{tag}", [P, 2 * P], st)
            o = [sb(f"o{i}_{tag}", [P, 2, nh * HD], st) for i in range(2)]
            if out_gain is not None:
                osq, oss = sb(f"osq_{tag}", [P, 2 * nh * HD], st), sb(f"oss_{tag}", [P, 2, 2 * nh], st)
            scored, maxed, expd, probs = (sem(f"{n}_{tag}") for n in ("scored", "maxed", "expd", "probs"))
            turned, moved, split, summed = (sem(f"{n}_{tag}") for n in ("turned", "moved", "split", "summed"))
            okept, added, taken = (sem(f"{n}_{tag}") for n in ("o_kept", "added", "taken"))
            finished, oturned, ykept = (sem(f"{n}_{tag}") for n in ("finished", "o_turned", "y_kept"))
            osums, oinv, step_s, pstep, biased = (sem(f"{n}_{tag}") for n in ("o_sums", "o_inv", "dve_step", "pool_step", "biased"))
            bb = [sb(f"bb{i}_{tag}", [P, width], st) for i in range(2)] if table else None

            def nkeys(u):
                return len(keys(units[u][0]))

            def segments(p):
                out, col = [], 0
                for kt in keys(p):
                    if out and out[-1][0] + out[-1][1] == kt * P and col % BANK:
                        out[-1][1] += P
                    else:
                        out.append([kt * P, P, col])
                    col += P
                return out

            def batches(u):
                return [(k, min(4, nkeys(u) - k)) for k in range(0, nkeys(u), 4)]

            nb = [0]
            for u in range(nu):
                nb.append(nb[-1] + len(batches(u)))
            AHEAD = 3 - maps
            STEPS = nu + 5

            def sum_at(n):
                v = (n - 2) // 2
                return v if n % 2 == 0 and 0 <= v < nv else None

            def out_at(n):
                g = (n - 4) // (2 * nh) - 1
                return g if (n - 4) % (2 * nh) == 0 and 0 <= g < len(pairs) else None
            turns, where = [], {}
            for n in range(STEPS):
                bs = range(len(batches(n))) if n < nu else []
                for b in bs[:2]:
                    where["turn", n, b] = len(turns)
                    turns.append((split, nb[n] + b + 1))
                if sum_at(n) is not None:
                    where["sum", sum_at(n)] = len(turns)
                    turns.append((taken, sum_at(n) + 1))
                for b in bs[2:]:
                    where["turn", n, b] = len(turns)
                    turns.append((split, nb[n] + b + 1))
                if n < nu:
                    if n % 2:
                        where["values", n // 2] = len(turns)
                        turns.append((okept, n // 2 + 1))
                if out_at(n) is not None:
                    where["out", out_at(n)] = len(turns)
                    turns.append((ykept, out_at(n) + 1))

            def turn_bank(*key):
                return 6 + where[key] % 2

            def score_bank(u, m):
                return 3 * (m if maps == 2 else u % 2)

            with nc.Block() as block:
                @block.sync
                def _(sp):
                    if meanwhile:
                        meanwhile(sp)

                @block.tensor
                def _(pe):
                    def my_turn(*key):
                        if where[key] >= 2:
                            pe.wait_ge(*turns[where[key] - 2])
                        return turn_bank(*key)

                    def scores(u):
                        p, h, s = units[u]
                        if maps == 2 and u >= 1:
                            pe.wait_ge(expd, 2 * u)
                        if maps == 1 and u >= 2:
                            pe.wait_ge(expd, u - 1)
                        q0 = (2 * p + s) * P
                        for m in range(maps):
                            pr = parts(h, m)
                            for k0, n, col in segments(p):
                                for i, (q, k) in enumerate(pr):
                                    mm = nc.tensor.matmul(bank(score_bank(u, m), n, col), q[:, q0:q0 + P], k[:, k0:k0 + n],
                                                          start=(i == 0), stop=(i == len(pr) - 1))
                            mm.then_inc(scored, 1)

                    def turn(u, part):
                        pe.wait_ge(probs, u + 1)
                        for b, (k0, n) in list(enumerate(batches(u)))[part]:
                            tb = my_turn("turn", u, b)
                            for k in range(n):
                                mm = nc.tensor.transpose(bank(tb, P, k * P), e[0][u % 2][:, (k0 + k) * P:(k0 + k + 1) * P], ident)
                            mm.then_inc(turned, 1)

                    def values(v):
                        p, h, s = units[2 * v]
                        tb = my_turn("values", v)
                        kts = keys(p)
                        for i, part in enumerate((hi, lo)):
                            pe.wait_ge(*((moved, nb[2 * v + 2]), (split, nb[2 * v + 2]))[i])
                            for k, kt in enumerate(kts):
                                mm = nc.tensor.matmul(bank(tb, 2 * P), vs[:, kt, h, :], part[:, k, :],
                                                      start=(i == 0 and k == 0), stop=(i == 1 and k == len(kts) - 1))
                        mm.then_inc(summed, 1)

                    def add_parts(v):
                        tb = my_turn("sum", v)
                        pe.wait_ge(okept, v + 1)
                        for s in range(2):
                            mm = nc.tensor.matmul(bank(tb, HD, s * HD), oT[:, s * P:(s + 1) * P], cst[:, C_PAIR:C_PAIR + HD], start=True, stop=True)
                        mm.then_inc(added, 1)

                    def turn_out(g):
                        tb = my_turn("out", g)
                        pe.wait_ge(*((finished, g + 1) if out_gain is not None else (taken, (g + 1) * nh)))
                        n = nh * HD // P
                        for s in range(2):
                            for c in range(n):
                                mm = nc.tensor.transpose(bank(tb, P, (c * 2 + s) * P), o[g % 2][:, s, c * P:(c + 1) * P], ident)
                        mm.then_inc(oturned, 1)

                    for u in range(AHEAD):
                        scores(u)
                    for n in range(STEPS):
                        if maps == 2 and n + 1 < nu:
                            scores(n + 1)
                        if n < nu:
                            turn(n, slice(0, 2))
                        if maps == 1 and n + 2 < nu:
                            scores(n + 2)
                        if sum_at(n) is not None:
                            add_parts(sum_at(n))
                        if n < nu:
                            turn(n, slice(2, None))
                            if n % 2:
                                values(n // 2)
                        if out_at(n) is not None:
                            turn_out(out_at(n))

                @block.scalar
                def _(act):
                    def exps(u, m):
                        p, h, s = units[u]
                        n = nkeys(u) * P
                        i = 2 * (u % 2) + m
                        act.wait_ge(maxed, maps * u + m + 1)
                        if u >= 2:
                            act.wait_ge(probs, u - 1)
                            act.wait_ge(turned, nb[u - 1])
                        src = e[0][u % 2][:, 0:n] if (table and p < LT // 2) else bank(score_bank(u, m), n)
                        nc.scalar.activation(e[m][u % 2][:, 0:n], src, ACT.Exp, bias=nm[:, i:i + 1], accum_out=zs[:, i:i + 1]).then_inc(expd, 1)

                    def moves(u, part):
                        s = u % 2
                        for b, (k0, n) in list(enumerate(batches(u)))[part]:
                            act.wait_ge(turned, nb[u] + b + 1)
                            if b == 0 and s == 0 and u >= 2:
                                act.wait_ge(summed, u // 2)
                            nc.scalar.activation(hi[:, k0:k0 + n, s * P:(s + 1) * P],
                                                 bank(turn_bank("turn", u, b), n * P).rearrange("p (k q) -> p k q", k=n), ACT.Copy).then_inc(moved, 1)

                    def keep_sum(v):
                        act.wait_ge(summed, v + 1)
                        if v >= 1:
                            act.wait_ge(added, v)
                        nc.scalar.activation(oT[:, :], bank(turn_bank("values", v), 2 * P), ACT.Copy).then_inc(okept, 1)

                    def keep_out(g):
                        act.wait_ge(oturned, g + 1)
                        n = nh * HD // P
                        nc.scalar.activation(yT[:, y0:y0 + n, 2 * g * P:(2 * g + 2) * P],
                                             bank(turn_bank("out", g), n * 2 * P).rearrange("p (c t) -> p c t", c=n), ACT.Copy).then_inc(ykept, 1)

                    for u in range(AHEAD):
                        for m in range(maps):
                            exps(u, m)
                    for n in range(STEPS):
                        if n < nu:
                            moves(n, slice(0, 1))
                        if maps == 2 and n + 1 < nu:
                            exps(n + 1, 0)
                        if n < nu:
                            moves(n, slice(1, 2))
                        if maps == 2 and n + 1 < nu:
                            exps(n + 1, 1)
                        if n < nu:
                            moves(n, slice(2, None))
                        if maps == 1 and n + 2 < nu:
                            exps(n + 2, 0)
                        if n < nu and n % 2:
                            keep_sum(n // 2)
                        if out_at(n) is not None:
                            keep_out(out_at(n))

                @block.vector
                def _(dve):
                    step = Chain(dve, step_s)

                    def top(u, m):
                        p, h, s = units[u]
                        n = nkeys(u) * P
                        i = 2 * (u % 2) + m
                        dve.wait_ge(scored, maps * u + m + 1)
                        if u >= 2:
                            dve.wait_ge(expd, maps * (u - 2) + m + 1)
                        if table and p < LT // 2:
                            if u >= 2:
                                dve.wait_ge(turned, nb[u - 1])
                            dve.wait_ge(biased, u + 1)
                            step.then(nc.vector.tensor_tensor_reduce(e[0][u % 2][:, 0:n], bank(score_bank(u, m), n), bb[u % 2][:, 0:n],
                                                                     1.0, 3.0 * NEG, ALU.add, ALU.max, mx[:, i:i + 1]))
                            step.wait()
                            nc.vector.tensor_scalar(nm[:, i:i + 1], mx[:, i:i + 1], -1.0, None, ALU.mult).then_inc(maxed, 1)
                        else:
                            nc.vector.tensor_reduce(nm[:, i:i + 1], bank(score_bank(u, m), n), AX, ALU.max, negate=True).then_inc(maxed, 1)

                    def weigh(u):
                        i, j = 2 * (u % 2), u % 8
                        dve.wait_ge(expd, maps * (u + 1))
                        if u >= 8:
                            dve.wait_ge(taken, (u - 8) // 2 + 1)
                        if maps == 1:
                            nc.vector.reciprocal(rz[:, j:j + 1], zs[:, i:i + 1]).then_inc(probs, 1)
                            return
                        n = nkeys(u) * P
                        step.then(nc.vector.reciprocal(rw[:, j:j + 1], zs[:, i + 1:i + 2]))
                        step.then(nc.vector.reciprocal(rz[:, j:j + 1], zs[:, i:i + 1]))
                        step.wait()
                        step.then(nc.vector.tensor_scalar(rw[:, j:j + 1], rw[:, j:j + 1], zs[:, i:i + 1], neglam[:, 0:1], ALU.mult, ALU.mult))
                        step.wait()
                        nc.vector.scalar_tensor_tensor(out=e[0][u % 2][:, 0:n], in0=e[1][u % 2][:, 0:n], scalar=rw[:, j:j + 1],
                                                       in1=e[0][u % 2][:, 0:n], op0=ALU.mult, op1=ALU.add).then_inc(probs, 1)

                    def splits(u, part):
                        s = u % 2
                        for b, (k0, n) in list(enumerate(batches(u)))[part]:
                            dve.wait_ge(moved, nb[u] + b + 1)
                            nc.vector.tensor_tensor(lo[:, k0:k0 + n, s * P:(s + 1) * P],
                                                    bank(turn_bank("turn", u, b), n * P).rearrange("p (k q) -> p k q", k=n),
                                                    hi[:, k0:k0 + n, s * P:(s + 1) * P].bitcast(F32), ALU.subtract).then_inc(split, 1)

                    def take(v):
                        g, h = divmod(v, nh)
                        dve.wait_ge(added, v + 1)
                        if maps == 1:
                            dve.wait_ge(probs, 2 * v + 2)
                        if h == 0 and g >= 2:
                            dve.wait_ge(oturned, g - 1)
                        for s in range(2):
                            j = (2 * v + s) % 8
                            ins = nc.vector.tensor_scalar(o[g % 2][:, s, h * HD:(h + 1) * HD], bank(turn_bank("sum", v), HD, s * HD), rz[:, j:j + 1], None, ALU.mult)
                        ins.then_inc(taken, 1)
                        if h == nh - 1 and out_gain is not None:
                            ov = o[g % 2][:, :, :].rearrange("p s d -> p (s d)")
                            dve.wait_ge(taken, v + 1)
                            step.then(nc.vector.tensor_tensor(osq[:, :], ov, ov, ALU.mult))
                            step.wait()
                            nc.vector.tensor_reduce(oss[:, g % 2, :], osq[:, :].rearrange("p (h d) -> p h d", d=HD), AX, ALU.add).then_inc(osums, 1)

                    def finish(g):
                        ov = o[g % 2][:, :, :].rearrange("p s (h d) -> p (s h) d", d=HD)
                        dve.wait_ge(oinv, g + 1)
                        step.then(nc.vector.tensor_tensor(ov, ov, oss[:, g % 2, :].unsqueeze(2).broadcast_to([P, 2 * nh, HD]), ALU.mult))
                        step.wait()
                        nc.vector.tensor_tensor(ov, ov, out_gain.unsqueeze(1).broadcast_to([P, 2 * nh, HD]), ALU.mult).then_inc(finished, 1)

                    for u in range(AHEAD):
                        for m in range(maps):
                            top(u, m)
                    if maps == 1:
                        weigh(0)
                    for n in range(STEPS):
                        if maps == 2 and n < nu:
                            weigh(n)
                        if maps == 2 and n + 1 < nu:
                            top(n + 1, 0)
                            top(n + 1, 1)
                        if n < nu:
                            splits(n, slice(0, 1))
                        if n < nu:
                            splits(n, slice(1, 2))
                        if maps == 1 and n + 1 < nu:
                            weigh(n + 1)
                        if maps == 1 and n + 2 < nu:
                            top(n + 2, 0)
                        if sum_at(n) is not None:
                            take(sum_at(n))
                        if n < nu:
                            splits(n, slice(2, None))
                        if out_gain is not None and n >= 1 and out_at(n + 1) is not None:
                            finish(out_at(n + 1))

                @block.gpsimd
                def _(pool):
                    step = Chain(pool, pstep)
                    if table:
                        tb, rowmask = table
                        for i in range(2):
                            step.then(nc.gpsimd.memset(bb[i][:, :], 0.0))
                        step.wait()
                        for u, (p, h, s) in enumerate(units):
                            if p >= LT // 2:
                                continue
                            if u >= 2:
                                pool.wait_ge(maxed, u - 1)
                            kts = keys(p)
                            rows_n = 2 * (len(kts) - 2)
                            qt = 2 * p + s
                            s0 = 2 * kts[0] - 2 * qt + 8
                            if u >= 2 and len(keys(units[u - 2][0])) != len(kts):
                                step.then(nc.gpsimd.memset(bb[u % 2][:, rows_n * GRID_W:], 0.0))
                                step.wait()
                            nc.gpsimd.tensor_tensor(bb[u % 2][:, 0:rows_n * GRID_W].rearrange("p (r c) -> p r c", c=GRID_W), tb[:, h, s0:s0 + rows_n, :],
                                                    rowmask(qt, rows_n).unsqueeze(2).broadcast_to([P, rows_n, GRID_W]), ALU.add).then_inc(biased, 1)
                    if out_gain is not None:
                        for g in range(len(pairs)):
                            pool.wait_ge(osums, g + 1)
                            step.then(nc.gpsimd.tensor_scalar(oss[:, g % 2, :], oss[:, g % 2, :], 1.0 / HD, EPS, ALU.mult, ALU.add))
                            step.wait()
                            nc.gpsimd.tensor_tensor(oss[:, g % 2, :], oss[:, g % 2, :], half[:, 0:2 * nh], ALU.pow).then_inc(oinv, 1)

    def all_keys(p):
        return list(range(NT)) if p < LT // 2 else list(range(LT, NT))

    def window_keys(p):
        if p >= LT // 2:
            return [LT, LT + 1]
        a, b = pair_window(p)
        return list(range(a, b)) + [LT, LT + 1]

    def columns(l, off, n):
        return a["w_in"][l].rearrange("(c p) n -> p c n", p=P)[:, :, off:off + n]

    def fetch_qkv(l, name, i, w):
        def go(eng):
            for j in range(3):
                fetch(eng, w[:, :, j, :], columns(l, OFF[name] + j * GW + i * P, P))
        return go

    def project_qkv(l, name, half_i, w, hd, gq, gk, stack, vs, rope):
        tag = f"{name}p{l}{half_i}"
        st = ExitStack()
        nh = P // hd
        four = hd == 32
        ns = 8 if four else 6
        with st:
            w_there = fetched[0]
            sq = [sb(f"sq{i}_{tag}", [P, 256], st) for i in range(2)]
            n_ = [sb(f"n{i}_{tag}", [P, 256], st) for i in range(2)]
            r_, u_ = sb(f"r_{tag}", [P, 256], st), sb(f"u_{tag}", [P, 256], st)
            so = [sb(f"so{i}_{tag}", [P, ns * P], st) for i in range(2)]
            ss = [sb(f"ss{i}_{tag}", [P, 2 * nh], st) for i in range(2)]
            projected, squared, sums = (sem(f"{n}_{tag}") for n in ("projected", "squared", "sums"))
            inv, normed, vhigh, vlow, turned = (sem(f"{n}_{tag}") for n in ("inv", "normed", "v_high", "v_low", "turned"))
            kept, ready, high, step_s, pstep = (sem(f"{n}_{tag}") for n in ("kept", "ready", "high", "dve_step", "pool_step"))
            lows = sem(f"lows_{tag}")
            def high_q(s):
                v = s[:, 0:nh * (4 if four else 2) * hd].rearrange("p (h c d) -> p h c d", h=nh, d=hd)
                return v[:, :, 0:4:2, :] if four else v[:, :, 0:1, :]

            def low_q(s):
                v = s[:, 0:nh * (4 if four else 2) * hd].rearrange("p (h c d) -> p h c d", h=nh, d=hd)
                return v[:, :, 1:4:2, :] if four else v[:, :, 1:2, :]

            def high_k(s):
                if four:
                    return s[:, 512:1024].rearrange("p (h c d) -> p h c d", h=nh, d=hd)[:, :, 0:2, :]
                return s[:, 256:512].rearrange("p (h c d) -> p h c d", h=nh, d=hd)

            def low_k(s):
                if four:
                    return s[:, 512:1024].rearrange("p (h c d) -> p h c d", h=nh, d=hd)[:, :, 2:4, :]
                return s[:, 512:768].rearrange("p (h c d) -> p h c d", h=nh, d=hd)

            with nc.Block() as block:
                @block.tensor
                def _(pe):
                    pe.wait_ge(ahead, w_there)
                    for t in range(NT + 2):
                        if t < NT:
                            if t >= 2:
                                pe.wait_ge(vlow, t - 1)
                                pe.wait_ge(normed, t - 1)
                            for c in range(DC):
                                mm = nc.tensor.matmul(bank(t % 2, 384), hT[:, c, t * P:(t + 1) * P], w[:, c, :, :].rearrange("p j n -> p (j n)"),
                                                      start=(c == 0), stop=(c == DC - 1))
                            mm.then_inc(projected, 1)
                        if t >= 2:
                            i = t - 2
                            pe.wait_ge(lows, 2 * (i + 1))
                            if i >= 2:
                                pe.wait_ge(kept, i - 1)
                            for c in range(ns):
                                mm = nc.tensor.transpose(bank(2 + 2 * (i % 2), P, c * P), so[i % 2][:, c * P:(c + 1) * P], ident)
                            mm.then_inc(turned, 1)

                @block.scalar
                def _(act):
                    def stacked(t):
                        act.wait_ge(ready, t + 1)
                        if t >= 2:
                            act.wait_ge(turned, t - 1)
                        q, k = n_[t % 2][:, 0:P], n_[t % 2][:, P:2 * P]
                        for x, dst in ((q, high_q(so[t % 2])), (k, high_k(so[t % 2]))):
                            c = dst.shape[2]
                            nc.scalar.activation(dst.bitcast(F32R), x.rearrange("p (h d) -> p h d", d=hd).unsqueeze(2).broadcast_to([P, nh, c, hd]), ACT.Copy).then_inc(high, 1)

                    for t in range(NT + 2):
                        if t < NT:
                            act.wait_ge(projected, t + 1)
                            if t >= 2:
                                act.wait_ge(sums, t - 1)
                            nc.scalar.activation(sq[t % 2][:, :], bank(t % 2, 256), ACT.Square).then_inc(squared, 1)
                            nc.scalar.activation(vs[:, t, :, 0:HD], bank(t % 2, P, 256).rearrange("p (h d) -> p h d", d=HD), ACT.Copy).then_inc(vhigh, 1)
                        if 1 <= t <= NT:
                            stacked(t - 1)
                        if t >= 2:
                            i = t - 2
                            act.wait_ge(turned, i + 1)
                            nc.scalar.activation(stack[:, :, i * P:(i + 1) * P], bank(2 + 2 * (i % 2), ns * P).rearrange("p (c t) -> p c t", c=ns), ACT.Copy).then_inc(kept, 1)

                @block.gpsimd
                def _(pool):
                    step = Chain(pool, pstep)
                    for t in range(NT):
                        pool.wait_ge(sums, t + 1)
                        step.then(nc.gpsimd.tensor_scalar(ss[t % 2][:, :], ss[t % 2][:, :], 1.0 / hd, EPS, ALU.mult, ALU.add))
                        step.wait()
                        nc.gpsimd.tensor_tensor(ss[t % 2][:, :], ss[t % 2][:, :], half[:, 0:2 * nh], ALU.pow).then_inc(inv, 1)

                @block.vector
                def _(dve):
                    step = Chain(dve, step_s)

                    def heads_of(x):
                        return x.rearrange("p (h d) -> p h d", d=hd)

                    def sum_squares(t):
                        dve.wait_ge(squared, t + 1)
                        if t >= 2:
                            dve.wait_ge(normed, t - 1)
                        nc.vector.tensor_reduce(ss[t % 2][:, :], heads_of(sq[t % 2][:, :]), AX, ALU.add).then_inc(sums, 1)
                        dve.wait_ge(vhigh, t + 1)
                        nc.vector.tensor_tensor(vs[:, t, :, HD:2 * HD], bank(t % 2, P, 256).rearrange("p (h d) -> p h d", d=HD),
                                                vs[:, t, :, 0:HD].bitcast(F32), ALU.subtract).then_inc(vlow, 1)

                    def low_parts(t):
                        dve.wait_ge(high, 2 * (t + 1))
                        for x, hp, lp in ((n_[t % 2][:, 0:P], high_q, low_q), (n_[t % 2][:, P:2 * P], high_k, low_k)):
                            dst = lp(so[t % 2])
                            c = dst.shape[2]
                            nc.vector.tensor_tensor(dst, heads_of(x).unsqueeze(2).broadcast_to([P, nh, c, hd]),
                                                    hp(so[t % 2])[:, :, 0:1, :].broadcast_to([P, nh, c, hd]), ALU.subtract).then_inc(lows, 1)

                    sum_squares(0)
                    for t in range(NT):
                        n = n_[t % 2]
                        dve.wait_ge(inv, t + 1)
                        if t >= 2:
                            dve.wait_ge(lows, 2 * (t - 1))
                            dve.wait_ge(high, 2 * (t - 1))
                        nc.vector.tensor_tensor(heads_of(n[:, :]), heads_of(bank(t % 2, 256)), ss[t % 2][:, :].unsqueeze(2).broadcast_to([P, 2 * nh, hd]), ALU.mult).then_inc(normed, 1)
                        dve.wait_ge(normed, t + 1)
                        roped = rope and t < LT
                        for k, g in enumerate((gq, gk)):
                            part = heads_of(n[:, :])[:, k * nh:(k + 1) * nh, :]
                            ins = nc.vector.tensor_tensor(part, part, g.unsqueeze(1).broadcast_to([P, nh, hd]), ALU.mult)
                            if roped or k == 0:
                                step.then(ins)
                            else:
                                step.wait()
                                ins.then_inc(ready, 1)
                        if roped:
                            step.wait()
                            cos = cst[:, C_COS + 32 * t:C_COS + 32 * t + 32].unsqueeze(1).broadcast_to([P, 2 * nh, 32])
                            sin = cst[:, C_SIN + 32 * t:C_SIN + 32 * t + 32].rearrange("p (a b e) -> p a b e", a=2, b=2)
                            nv = n[:, :].rearrange("p (h a b e) -> p h a b e", a=2, b=2, e=8)
                            rv = r_[:, :].rearrange("p (h a b e) -> p h a b e", a=2, b=2, e=8)
                            for x in range(2):
                                for y in range(2):
                                    step.then(nc.vector.tensor_tensor(rv[:, :, x, y, :], nv[:, :, x, 1 - y, :],
                                                                      sin[:, x, y, :].unsqueeze(1).broadcast_to([P, 2 * nh, 8]), ALU.mult))
                            step.then(nc.vector.tensor_tensor(heads_of(u_[:, :]), heads_of(n[:, :]), cos, ALU.mult))
                            step.wait()
                            nc.vector.tensor_tensor(n[:, :], u_[:, :], r_[:, :], ALU.add).then_inc(ready, 1)
                        if t + 1 < NT:
                            sum_squares(t + 1)
                        low_parts(t)

    def mixers(l, yT, w_ahead, need):
        R = {k: rows[:, l, o:o + w] for k, (o, w) in ROWS.items()}

        def two_heads(name, i, hd, maps, y0, rope, keys, meanwhile, out_gain=None):
            st = ExitStack()
            with st:
                tag = f"{name}{l}{i}"
                four = hd == 32
                stack = sbr(f"stack_{tag}", [P, 8 if four else 6, T], st)
                vs = sbr(f"vs_{tag}", [P, NT, 2, 2 * HD], st)
                project_qkv(l, name, i, w_ahead, hd, R[f"{name}_g_q"], R[f"{name}_g_k"], stack, vs, rope)
                if four:
                    def parts(h, m):
                        return [(stack[:, 2 * h + m, :], stack[:, 4 + 2 * h + m, :])]
                else:
                    def parts(h, m):
                        return [(stack[:, h, :], stack[:, 2 + h, :]), (stack[:, h, :], stack[:, 4 + h, :])]
                table = None
                if name == "na":
                    tb = sb(f"tb_{tag}", [P, 2, NSLOT, GRID_W], st)
                    position_table(l, i, tb, yT)
                    table = (tb, lambda qt, n: cst[:, C_ROW + 12 * qt:C_ROW + 12 * qt + n])
                attention(tag, 2, maps, parts, keys, vs, yT, y0 + i, out_gain=out_gain, table=table, need=need, meanwhile=meanwhile)
            clear_semaphores()

        def fetch_mla(eng):
            w, wq, wkv = mla_weights(yT)
            fetch(eng, w, columns(l, OFF["mla"], 416))
            fetch(eng, wq, a["mla_w_uq"][l].rearrange("(c p) n -> p c n", p=P))
            fetch(eng, wkv, a["mla_w_ukv"][l])

        two_heads("diff", 0, DQK, 2, 0, True, all_keys, fetch_qkv(l, "diff", 1, w_ahead), R["diff_g_out"])
        two_heads("diff", 1, DQK, 2, 0, True, all_keys, fetch_mla, R["diff_g_out"])

        def mla():
            st = ExitStack()
            with st:
                qkT = sb(f"mqkT{l}", [P, 2 * H, T], st)
                vs = sbr(f"mvs{l}", [P, NT, H, 2 * HD], st)
                mla_project(l, R, qkT, vs, yT)
                attention(f"mla{l}", H, 1, lambda h, m: [(qkT[0:MD, h, :], qkT[0:MD, H + h, :])],
                          all_keys, vs, yT, 2, need=need, meanwhile=fetch_qkv(l, "na", 0, w_ahead))
        mla()
        clear_semaphores()

        st = ExitStack()
        with st:
            w_ml = sb(f"w_ml{l}", [P, DC, 512], st)
            two_heads("na", 0, HD, 1, 6, False, window_keys, fetch_qkv(l, "na", 1, w_ahead))
            two_heads("na", 1, HD, 1, 6, False, window_keys, lambda eng: fetch(eng, w_ml[:, :, :], columns(l, OFF["mlqk"], 512)))

            mlstm(l, R, yT, w_ml, w_ahead, need)
        clear_semaphores()

    def position_table(l, i, tb, yT):
        read, turned, masked = (sem(f"{n}{l}{i}") for n in ("rpb_read", "rpb_turned", "rpb_masked"))
        n, step = 2 * NSLOT * GRID_W, 6 * GRID_W
        raw = yT[:, 4:6, :].rearrange("p c t -> p (c t)")[:, 0:n]
        flat = tb[:, :, :, :].rearrange("p h s k -> p (h s) k")
        with nc.Block() as block:
            @block.sync
            def _(sp):
                for h in range(2):
                    for x in range(2):
                        off = ((l * H + 2 * i + h) * (NSLOT + 1) + x) * 127
                        sp.dma_start(raw[x * GRID_W:(x + 1) * GRID_W, :].rearrange("p (h s k) -> p h s k", h=2, s=NSLOT)[:, h, :, :],
                                     bass.AP(rpb_pad.tensor, off, [[1, GRID_W], [127, NSLOT], [1, GRID_W]])).then_inc(read, 16)

            @block.tensor
            def _(pe):
                pe.wait_ge(read, 16 * 4)
                for j in range(n // step):
                    nc.tensor.matmul(bank(j, step), cst[:, C_REV:C_REV + P], raw[:, j * step:(j + 1) * step], start=True, stop=True).then_inc(turned, 1)

            @block.vector
            def _(dve):
                for j in range(n // step):
                    dve.wait_ge(turned, j + 1)
                    nc.vector.tensor_tensor(flat[:, 6 * j:6 * j + 6, :], bank(j, step).rearrange("p (s k) -> p s k", k=GRID_W),
                                            cst[:, C_COL:C_COL + 64].unsqueeze(1).broadcast_to([P, 6, GRID_W]), ALU.add).then_inc(masked, 1)

    def mla_weights(yT):
        flat = yT[:, 4:8, :].rearrange("p c t -> p (c t)")
        n, n1 = DC * 416, DC * 416 + 2 * H * MD
        return (flat[:, 0:n].rearrange("p (c n) -> p c n", c=DC), flat[:, n:n1].rearrange("p (c n) -> p c n", c=2),
                flat[:, n1:n1 + 2 * GW])

    def mla_project(l, R, qkT, vs, yT):
        st = ExitStack()
        with st:
            tag = f"mlap{l}"
            w, wq, wkv = mla_weights(yT)
            w_there = fetched[0]
            sq = sb(f"sq_{tag}", [P, 256], st)
            sq2 = sb(f"sq2_{tag}", [P, 2 * H * MD], st)
            cn = [sb(f"cn{i}_{tag}", [P, 384], st) for i in range(2)]
            kr = [sb(f"kr{i}_{tag}", [P, ROPE], st) for i in range(2)]
            cT = sb(f"cT_{tag}", [P, 3, P], st)
            qks = [sb(f"qk{i}_{tag}", [P, 2 * H, MD], st) for i in range(2)]
            rt = sb(f"rt_{tag}", [P, 2 * H, ROPE], st)
            ss = sb(f"ss_{tag}", [P, 2, 2], st)
            s8 = sb(f"s8_{tag}", [P, 2, 2 * H], st)
            projected, sums, inv = (sem(f"{n}_{tag}") for n in ("projected", "sums", "inv"))
            normed, cturned, ckept, up = (sem(f"{n}_{tag}") for n in ("normed", "c_turned", "c_kept", "up"))
            gathered, qsq, qsums, qinv = (sem(f"{n}_{tag}") for n in ("gathered", "q_squared", "q_sums", "q_inv"))
            ready, turned, kept, vkept = (sem(f"{n}_{tag}") for n in ("ready", "turned", "kept", "v_kept"))
            step_s, pstep, vlow = sem(f"dve_step_{tag}"), sem(f"pool_step_{tag}"), sem(f"v_low_{tag}")
            with nc.Block() as block:
                @block.tensor
                def _(pe):
                    pe.wait_ge(ahead, w_there)

                    def down(t):
                        if t >= 2:
                            pe.wait_ge(normed, t - 1)
                        for c in range(DC):
                            mm = nc.tensor.matmul(bank(t % 2, 416), hT[:, c, t * P:(t + 1) * P], w[:, c, :], start=(c == 0), stop=(c == DC - 1))
                        mm.then_inc(projected, 1)

                    def turn_back(t):
                        pe.wait_ge(ready, t + 1)
                        for s in range(2):
                            if t >= 1:
                                pe.wait_ge(kept, 2 * (t - 1) + s + 1)
                            for h in range(H):
                                mm = nc.tensor.transpose(bank(5 + s, P, h * P)[0:MD, :], qks[t % 2][:, s * H + h, :], ident)
                            mm.then_inc(turned, 1)

                    down(0)
                    for t in range(NT):
                        if t + 1 < NT:
                            down(t + 1)
                        pe.wait_ge(normed, t + 1)
                        if t >= 1:
                            pe.wait_ge(ckept, t)
                        for c in range(3):
                            mm = nc.tensor.transpose(bank(2, P, c * P), cn[t % 2][:, c * P:(c + 1) * P], ident)
                        mm.then_inc(cturned, 1)
                        if t >= 2:
                            turn_back(t - 2)
                        pe.wait_ge(ckept, t + 1)
                        if t >= 1:
                            pe.wait_ge(gathered, t)
                            pe.wait_ge(vlow, t)
                        for c in range(2):
                            nc.tensor.matmul(bank(3, H * MD), cT[:, c, :], wq[:, c, :], start=(c == 0), stop=(c == 1))
                        nc.tensor.matmul(bank(4), cT[:, 2, :], wkv[:, :], start=True, stop=True).then_inc(up, 1)
                    turn_back(NT - 2)
                    turn_back(NT - 1)

                @block.scalar
                def _(act):
                    def first(t):
                        act.wait_ge(projected, t + 1)
                        if t >= 2:
                            act.wait_ge(normed, t - 1)
                        nc.scalar.activation(sq[:, :], bank(t % 2, MQ), ACT.Square, scale=MQ ** -0.5, accum_out=ss[:, t % 2, 0:1]).then_inc(sums, 1)
                        act.wait_ge(sums, 2 * t + 1)
                        nc.scalar.activation(sq[:, 0:MKV], bank(t % 2, MKV, MQ), ACT.Square, scale=MKV ** -0.5, accum_out=ss[:, t % 2, 1:2]).then_inc(sums, 1)
                        act.wait_ge(sums, 2 * t + 2)

                    def move(t):
                        act.wait_ge(turned, 2 * t + 2)
                        for s in range(2):
                            nc.scalar.activation(qkT[0:MD, s * H:(s + 1) * H, t * P:(t + 1) * P],
                                                 bank(5 + s)[0:MD, :].rearrange("p (h t) -> p h t", h=H), ACT.Copy).then_inc(kept, 1)

                    first(0)
                    for t in range(NT):
                        if t + 1 < NT:
                            first(t + 1)
                        act.wait_ge(cturned, t + 1)
                        if t >= 1:
                            act.wait_ge(up, t)
                        nc.scalar.activation(cT[:, 0, :], bank(2, P), ACT.Copy, scale=vec[:, l, V_GCQ:V_GCQ + 1])
                        nc.scalar.activation(cT[:, 1, :], bank(2, P, P), ACT.Copy, scale=vec[:, l, V_GCQ + 1:V_GCQ + 2])
                        nc.scalar.activation(cT[:, 2, :], bank(2, P, 2 * P), ACT.Copy, scale=vec[:, l, V_GCKV:V_GCKV + 1]).then_inc(ckept, 1)
                        if t >= 2:
                            move(t - 2)
                        act.wait_ge(up, t + 1)
                        act.wait_ge(gathered, t + 1)
                        nc.scalar.activation(vs[:, t, :, 0:HD],
                                             bank(4).rearrange("p (h d) -> p h d", h=H)[:, :, HD:2 * HD], ACT.Copy).then_inc(vkept, 1)
                        if t >= 1:
                            act.wait_ge(qsums, t)
                        nc.scalar.activation(sq2[:, :], qks[t % 2][:, :, :].rearrange("p h d -> p (h d)"), ACT.Square).then_inc(qsq, 1)
                    move(NT - 2)
                    move(NT - 1)

                @block.gpsimd
                def _(pool):
                    step = Chain(pool, pstep)
                    for t in range(NT + 1):
                        if t < NT:
                            pool.wait_ge(sums, 2 * t + 2)
                            step.then(nc.gpsimd.tensor_scalar(ss[:, t % 2, :], ss[:, t % 2, :], EPS, 1.0, ALU.add, ALU.mult))
                            step.wait()
                            nc.gpsimd.tensor_tensor(ss[:, t % 2, :], ss[:, t % 2, :], half[:, 0:2], ALU.pow).then_inc(inv, 1)
                        if t >= 1:
                            i = t - 1
                            pool.wait_ge(qsums, i + 1)
                            step.then(nc.gpsimd.tensor_scalar(s8[:, i % 2, :], s8[:, i % 2, :], 1.0 / MD, EPS, ALU.mult, ALU.add))
                            step.wait()
                            nc.gpsimd.tensor_tensor(s8[:, i % 2, :], s8[:, i % 2, :], half[:, 0:2 * H], ALU.pow).then_inc(qinv, 1)

                @block.vector
                def _(dve):
                    step = Chain(dve, step_s)

                    def norm_latents(t):
                        dve.wait_ge(inv, t + 1)
                        if t >= 2:
                            dve.wait_ge(cturned, t - 1)
                            dve.wait_ge(gathered, t - 1)
                        nc.vector.tensor_copy(kr[t % 2][:, :], bank(t % 2, ROPE, MQ + MKV))
                        nc.vector.tensor_scalar(cn[t % 2][:, 0:MQ], bank(t % 2, MQ), ss[:, t % 2, 0:1], None, ALU.mult)
                        nc.vector.tensor_scalar(cn[t % 2][:, MQ:MQ + MKV], bank(t % 2, MKV, MQ), ss[:, t % 2, 1:2], None, ALU.mult).then_inc(normed, 1)

                    norm_latents(0)
                    for t in range(NT):
                        if t + 1 < NT:
                            norm_latents(t + 1)
                        dve.wait_ge(up, t + 1)
                        qk = qks[t % 2]
                        if t >= 2:
                            dve.wait_ge(turned, 2 * (t - 1))
                        nc.vector.tensor_copy(qk[:, 0:H, :], bank(3, H * MD).rearrange("p (h d) -> p h d", h=H))
                        nc.vector.tensor_copy(qk[:, H:2 * H, 0:HD], bank(4).rearrange("p (h d) -> p h d", h=H)[:, :, 0:HD])
                        dve.wait_ge(normed, t + 1)
                        nc.vector.tensor_copy(qk[:, H:2 * H, HD:MD], kr[t % 2][:, :].unsqueeze(1).broadcast_to([P, H, ROPE])).then_inc(gathered, 1)
                        dve.wait_ge(vkept, t + 1)
                        nc.vector.tensor_tensor(vs[:, t, :, HD:2 * HD], bank(4).rearrange("p (h d) -> p h d", h=H)[:, :, HD:2 * HD],
                                                vs[:, t, :, 0:HD].bitcast(F32), ALU.subtract).then_inc(vlow, 1)
                        dve.wait_ge(qsq, t + 1)
                        if t >= 2:
                            dve.wait_ge(step_s, n2)
                        nc.vector.tensor_reduce(s8[:, t % 2, :], sq2[:, :].rearrange("p (h d) -> p h d", h=2 * H), AX, ALU.add).then_inc(qsums, 1)
                        dve.wait_ge(qinv, t + 1)
                        n2 = step.then(nc.vector.tensor_tensor(qk[:, :, :], qk[:, :, :], s8[:, t % 2, :].unsqueeze(2).broadcast_to([P, 2 * H, MD]), ALU.mult))
                        step.wait()
                        step.then(nc.vector.tensor_tensor(qk[:, 0:H, :], qk[:, 0:H, :], R["mla_g_q"].unsqueeze(1).broadcast_to([P, H, MD]), ALU.mult))
                        ins = nc.vector.tensor_tensor(qk[:, H:2 * H, :], qk[:, H:2 * H, :], R["mla_g_k"].unsqueeze(1).broadcast_to([P, H, MD]), ALU.mult)
                        if t >= LT:
                            step.wait()
                            ins.then_inc(ready, 1)
                        else:
                            step.then(ins)
                            step.wait()
                            cos = cst[:, C_COS + 32 * t:C_COS + 32 * t + 32].unsqueeze(1).broadcast_to([P, 2 * H, ROPE])
                            sin = cst[:, C_SIN + 32 * t:C_SIN + 32 * t + 32].rearrange("p (a b e) -> p a b e", a=2, b=2)
                            rq = qk[:, :, HD:MD]
                            for x in range(2):
                                for y in range(2):
                                    o0 = HD + 16 * x + 8 * (1 - y)
                                    step.then(nc.vector.tensor_tensor(rt[:, :, 16 * x + 8 * y:16 * x + 8 * y + 8], qk[:, :, o0:o0 + 8],
                                                                      sin[:, x, y, :].unsqueeze(1).broadcast_to([P, 2 * H, 8]), ALU.mult))
                            step.wait()
                            step.then(nc.vector.tensor_tensor(rq, rq, cos, ALU.mult))
                            step.wait()
                            nc.vector.tensor_tensor(rq, rq, rt[:, :, :], ALU.add).then_inc(ready, 1)

    def mlstm(l, R, yT, w_ml, w_ahead, need):
        st = ExitStack()
        nq = NT if need else LT
        order = [[8, 9] + list(range(LT)), [9, 8] + list(range(LT))[::-1]]
        with st:
            qkT = sb(f"lqkT{l}", [P, 4, T], st)
            v = sb(f"lv1_{l}", [P, NT, H, HD + 1], st)
            def so(t):
                return yT[:, 4:6, t * P:(t + 1) * P]
            gt = sb(f"gt{l}", [P, NT, 16], st)
            A, M, EM = (sb(f"{n}{l}", [P, 2, NT, H], st) for n in ("gA", "gM", "gEM"))
            mlstm_project(l, w_ml, qkT, v, so, gt)
            kz = [w_ml[:, :, :].rearrange("p c n -> p (c n)")[:, h * T:(h + 1) * T] for h in range(3)]
            kz.append(w_ahead[:, :, :, :].rearrange("p c j n -> p (c j n)")[:, 0:T])
            mlstm_gates(l, R, gt, A, M, EM, order, qkT, kz)
            clear_semaphores()
            mlstm_mix(l, R, qkT, kz, v, so, A, M, EM, yT, nq)

    def mlstm_project(l, wqk, qkT, v, so, gt):
        st = ExitStack()
        width = T + 4
        span = T + 2
        with st:
            tag = f"mlp{l}"
            wvo = sb(f"wvo_{tag}", [P, DC, 512], st)
            w_there = fetched[0]
            wg = sb(f"wg_{tag}", [P, DC, 16], st)
            u = [sb(f"u{i}_{tag}", [P, width], st) for i in range(2)]
            cv = sb(f"cv_{tag}", [P, width], st)
            loaded_vo, loaded_g, up, copied = (sem(f"{n}_{tag}") for n in ("loaded_vo", "loaded_g", "up", "copied"))
            zeroed, step_s, conv, silu = (sem(f"{n}_{tag}") for n in ("zeroed", "dve_step", "conv", "silu"))
            projected, vkept, okept, gkept = (sem(f"{n}_{tag}") for n in ("projected", "v_kept", "o_kept", "g_kept"))
            with nc.Block() as block:
                @block.sync
                def _(sp):
                    sp.dma_start(wvo[:, :, :], columns(l, OFF["mlvo"], 512)).then_inc(loaded_vo, 16)
                    sp.dma_start(wg[:, :, :], columns(l, OFF["mlg"], 16)).then_inc(loaded_g, 16)

                @block.tensor
                def _(pe):
                    pe.wait_ge(ahead, w_there)
                    for f in range(4):
                        if f >= 2:
                            pe.wait_ge(copied, 2 * (f - 1))
                        for j, (t0, m, s) in enumerate(BLOCKS):
                            for c in range(DC):
                                mm = nc.tensor.matmul(bank(3 * (f % 2) + j, m), wqk[:, c, f * P:(f + 1) * P], hT[:, c, t0:t0 + m], start=(c == 0), stop=(c == DC - 1))
                        mm.then_inc(up, 1)
                    pe.wait_ge(loaded_vo, 16)
                    pe.wait_ge(loaded_g, 16)
                    pe.wait_ge(copied, 8)
                    for t in range(NT):
                        if t >= 2:
                            pe.wait_ge(vkept, t - 1)
                            pe.wait_ge(okept, t - 1)
                            pe.wait_ge(gkept, t - 1)
                        for c in range(DC):
                            nc.tensor.matmul(bank(t % 2), hT[:, c, t * P:(t + 1) * P], wvo[:, c, :], start=(c == 0), stop=(c == DC - 1))
                        for c in range(DC):
                            mm = nc.tensor.matmul(bank(2 + t % 2, 16), hT[:, c, t * P:(t + 1) * P], wg[:, c, :], start=(c == 0), stop=(c == DC - 1))
                        mm.then_inc(projected, 1)

                @block.scalar
                def _(act):
                    act.wait_ge(zeroed, 2)
                    for f in range(4):
                        act.wait_ge(up, f + 1)
                        if f >= 2:
                            act.wait_ge(conv, f - 1)
                        nc.scalar.activation(u[f % 2][:, 1:1 + SEQ], bank(3 * (f % 2), SEQ), ACT.Copy).then_inc(copied, 1)
                        nc.scalar.activation(u[f % 2][:, SEQ + 3:SEQ + 3 + CTX], bank(3 * (f % 2) + 2, CTX), ACT.Copy).then_inc(copied, 1)
                        act.wait_ge(conv, f + 1)
                        nc.scalar.activation(qkT[:, f, 0:SEQ], cv[:, 0:SEQ], ACT.Silu)
                        nc.scalar.activation(qkT[:, f, SEQ:T], cv[:, SEQ + 2:T + 2], ACT.Silu).then_inc(silu, 1)
                    for t in range(NT):
                        act.wait_ge(projected, t + 1)
                        nc.scalar.activation(so(t), bank(t % 2, GW, GW).rearrange("p (c d) -> p c d", c=2), ACT.Sigmoid).then_inc(okept, 1)

                @block.gpsimd
                def _(pool):
                    for i in range(2):
                        nc.gpsimd.memset(u[i][:, :], 0.0).then_inc(zeroed, 1)
                    nc.gpsimd.memset(v[:, :, :, HD:HD + 1], 1.0).then_inc(zeroed, 1)

                @block.vector
                def _(dve):
                    step = Chain(dve, step_s)
                    for f in range(4):
                        def w(k):
                            c = V_MCONV + 4 * k + f
                            return vec[:, l, c:c + 1]
                        dve.wait_ge(copied, 2 * f + 2)
                        if f >= 1:
                            dve.wait_ge(silu, f)
                        x = u[f % 2]
                        step.then(nc.vector.tensor_scalar(cv[:, 0:span], x[:, 0:span], w(0), None, ALU.mult))
                        step.wait()
                        step.then(nc.vector.scalar_tensor_tensor(out=cv[:, 0:span], in0=x[:, 1:1 + span], scalar=w(1), in1=cv[:, 0:span], op0=ALU.mult, op1=ALU.add))
                        step.wait()
                        nc.vector.scalar_tensor_tensor(out=cv[:, 0:span], in0=x[:, 2:2 + span], scalar=w(2), in1=cv[:, 0:span], op0=ALU.mult, op1=ALU.add).then_inc(conv, 1)
                    for t in range(NT):
                        dve.wait_ge(projected, t + 1)
                        dve.wait_ge(okept, t + 1)
                        nc.vector.tensor_copy(v[:, t, :, 0:HD], bank(t % 2, GW).rearrange("p (h d) -> p h d", h=H)).then_inc(vkept, 1)
                        nc.vector.tensor_copy(gt[:, t, :], bank(2 + t % 2, 16)).then_inc(gkept, 1)

    def mlstm_gates(l, R, gt, A, M, EM, order, qkT, kz):
        st = ExitStack()
        G4 = NT * H
        PAD = 64
        with st:
            tag = f"mlg{l}"
            F, E1, B, TOT, TM = (sb(f"{n}_{tag}", [P, 2, NT, H], st) for n in ("F", "E1", "B", "TOT", "TM"))
            off = sb(f"off_{tag}", [P, 2, NT, H], st)
            run = sb(f"run_{tag}", [P, 2, NT, H], st)
            sc = [sb(f"sc{i}_{tag}", [G4, 2, PAD + P], st) for i in range(2)]
            back = sb(f"back_{tag}", [P, 2, G4], st)
            step_s, astep, pstep = sem(f"dve_step_{tag}"), sem(f"act_step_{tag}"), sem(f"pe_step_{tag}")
            padded = sem(f"padded_{tag}")
            flat = "p a t h -> p (a t h)"

            def d(x, i):
                return x[:, i, :, :].rearrange("p t h -> p (t h)")

            def both(x):
                return x[:, :, :, :].rearrange(flat)
            cum = (cst[:, C_CUM:C_CUM + P], cst[:, C_CUMR:C_CUMR + P])
            rev = cst[:, C_REV:C_REV + P]
            e127 = cst[:, C_E127:C_E127 + P]
            marks = {}
            with nc.Block() as block:
                @block.gpsimd
                def _(pool):
                    for i in range(2):
                        nc.gpsimd.memset(sc[i][:, :, :], 3.0 * NEG).then_inc(padded, 1)
                    for h in range(H):
                        own, other = HD * (h % 2), HD * (1 - h % 2)
                        nc.gpsimd.memset(kz[h][other:other + HD, :], 0.0).then_inc(padded, 1)
                        nc.gpsimd.tensor_copy(kz[h][own:own + HD, :], qkT[own:own + HD, 2 + h // 2, :]).then_inc(padded, 1)

                @block.vector
                def _(dve):
                    step = Chain(dve, step_s)

                    def go(ins):
                        step.then(ins)
                        step.wait()
                    for i in range(2):
                        for x, o, b in ((F, 8 + 4 * i, "mlstm_b_f"), (A, 4 * i, "mlstm_b_i")):
                            go(nc.vector.tensor_tensor(x[:, i, :, :], gt[:, :, o:o + 4],
                                                       R[b][:, 4 * i:4 * i + 4].unsqueeze(1).broadcast_to([P, NT, H]), ALU.add))
                    go(nc.vector.scalar_tensor_tensor(out=both(E1), in0=both(F), scalar=-1.0, in1=both(F), op0=ALU.mult, op1=ALU.max))
                    marks["abs"] = step.n
                    dve.wait_ge(astep, 2)
                    go(nc.vector.scalar_tensor_tensor(out=both(F), in0=both(F), scalar=0.0, in1=both(E1), op0=ALU.min, op1=ALU.subtract))
                    marks["lf"] = step.n
                    dve.wait_ge(pstep, 3)
                    go(nc.vector.tensor_copy(both(TOT), bank(2, 2 * G4)))
                    for i in range(2):
                        step.then(nc.vector.memset(off[:, i, order[i][0], :], 0.0))
                    step.wait()
                    for n in range(1, NT):
                        for i in range(2):
                            x, y = order[i][n], order[i][n - 1]
                            step.then(nc.vector.tensor_tensor(off[:, i, x, :], off[:, i, y, :], TOT[:, i, y, :], ALU.add))
                        step.wait()
                    for i in range(2):
                        go(nc.vector.tensor_tensor(d(B, i), bank(i, G4), d(off, i), ALU.add))
                    go(nc.vector.tensor_tensor(both(A), both(A), both(B), ALU.subtract))
                    marks["a"] = step.n
                    dve.wait_ge(pstep, 5)
                    dve.wait_ge(padded, 2)
                    for i in range(2):
                        go(nc.vector.tensor_copy(sc[0][:, i, PAD:PAD + P], bank(3 + i, P)[0:G4, :]))
                    for n in range(7):
                        x, y, k = sc[n % 2], sc[(n + 1) % 2], 1 << n
                        go(nc.vector.tensor_tensor(y[:, :, PAD:PAD + P], x[:, :, PAD:PAD + P], x[:, :, PAD - k:PAD + P - k], ALU.max))
                    marks["scan"] = step.n
                    dve.wait_ge(pstep, 6)
                    go(nc.vector.tensor_copy(back[:, :, :], bank(5, 2 * G4).rearrange("p (a n) -> p a n", a=2)))
                    marks["back"] = step.n
                    dve.wait_ge(pstep, 8)
                    go(nc.vector.tensor_copy(both(TM), bank(6, 2 * G4)))
                    for i in range(2):
                        step.then(nc.vector.memset(run[:, i, order[i][0], :], 3.0 * NEG))
                    step.wait()
                    for n in range(1, NT):
                        for i in range(2):
                            x, y = order[i][n], order[i][n - 1]
                            step.then(nc.vector.tensor_tensor(run[:, i, x, :], run[:, i, y, :], TM[:, i, y, :], ALU.max))
                        step.wait()
                    go(nc.vector.tensor_tensor(d(M, 0), back[:, 0, :], d(run, 0), ALU.max))
                    go(nc.vector.tensor_tensor(d(M, 1), bank(7, G4), d(run, 1), ALU.max))
                    go(nc.vector.tensor_tensor(both(B), both(B), both(M), ALU.add))
                    marks["bm"] = step.n

                @block.scalar
                def _(act):
                    act.wait_ge(step_s, marks["abs"])
                    nc.scalar.activation(both(E1), both(E1), ACT.Exp, scale=-1.0).then_inc(astep, 1)
                    act.wait_ge(astep, 1)
                    nc.scalar.activation(both(E1), both(E1), ACT.Ln, bias=1.0).then_inc(astep, 1)
                    act.wait_ge(step_s, marks["bm"])
                    nc.scalar.activation(both(EM), both(B), ACT.Exp, scale=-1.0).then_inc(astep, 1)

                @block.tensor
                def _(pe):
                    pe.wait_ge(step_s, marks["lf"])
                    for i in range(2):
                        nc.tensor.matmul(bank(i, G4), cum[i], d(F, i), start=True, stop=True).then_inc(pstep, 1)
                    nc.tensor.matmul(bank(2, 2 * G4), ones[:, :], both(F), start=True, stop=True).then_inc(pstep, 1)
                    pe.wait_ge(step_s, marks["a"])
                    nc.tensor.matmul(bank(3, P)[0:G4, :], d(A, 0), ident, start=True, stop=True).then_inc(pstep, 1)
                    nc.tensor.matmul(bank(4, P)[0:G4, :], d(A, 1), rev, start=True, stop=True).then_inc(pstep, 1)
                    pe.wait_ge(step_s, marks["scan"])
                    for i in range(2):
                        mm = nc.tensor.matmul(bank(5, G4, G4 * i), sc[1][:, i, PAD:PAD + P], ident[0:G4, 0:G4], start=True, stop=True)
                    mm.then_inc(pstep, 1)
                    pe.wait_ge(step_s, marks["back"])
                    nc.tensor.matmul(bank(6, 2 * G4), e127, back[:, :, :].rearrange("p a n -> p (a n)"), start=True, stop=True).then_inc(pstep, 1)
                    nc.tensor.matmul(bank(7, G4), rev, back[:, 1, :], start=True, stop=True).then_inc(pstep, 1)

    def mlstm_mix(l, R, qkT, kz, v, so, A, M, EM, yT, nq):
        st = ExitStack()
        nblk = 3 if nq == NT else 2
        RING = 10
        with st:
            tag = f"mlm{l}"
            hs = sb(f"hs_{tag}", [P, NT, GW], st)
            dg = [sb(f"dg{i}_{tag}", [P, 512], st) for i in range(2)]
            nms = [sb(f"nms{i}_{tag}", [P, 2, 512], st) for i in range(2)]
            nmd = [sb(f"nmd{i}_{tag}", [P, 2, 512], st) for i in range(2)]
            WRING = 4
            wt = [sb(f"wt{i}_{tag}", [P, 512], st) for i in range(WRING)]
            pr = [hT[:, :, :].rearrange("p c t -> p (c t)")[:, i * 512:(i + 1) * 512] for i in range(RING)]
            den = sb(f"den_{tag}", [P, 2, 4], st)
            ob = sb(f"ob_{tag}", [P, 2, 4, HD], st)
            ss = sb(f"ss_{tag}", [P, NT, H], st)
            hsq = sb(f"hsq_{tag}", [P, 4 * GW], st)
            step_s, diag, neg, masked, scored = (sem(f"{n}_{tag}") for n in ("dve_step", "diag", "neg_max", "masked", "scored"))
            weighed, product, taken = (sem(f"{n}_{tag}") for n in ("weighed", "product", "taken"))
            sums, inv, ready, turned, kept, pstep = (sem(f"{n}_{tag}") for n in ("sums", "inv", "ready", "turned", "kept", "pool_step"))
            used, nkept = sem(f"used_{tag}"), sem(f"nm_kept_{tag}")
            units = []
            for blk in range(nblk):
                t0, m, s = BLOCKS[blk]
                q0, q1 = t0 // P, (t0 + m) // P
                for h in range(H):
                    jobs = []
                    for kt in ([8, 9] + list(range(LT)) if s == 0 else [8, 9]):
                        for i in range(2):
                            if s == 0 and kt >= LT:
                                lo, hi = q0, q1
                            elif i == 0:
                                lo, hi = max(q0, kt), q1
                            else:
                                lo, hi = q0, min(q1, kt + 1)
                            if lo < hi:
                                jobs.append((i, kt, lo, hi))
                    units.append((blk, h, q0, q1, s, jobs))
            tiles = []
            for n, (blk, h, q0, q1, s, jobs) in enumerate(units):
                for kt in dict.fromkeys(j[1] for j in jobs):
                    tiles.append((n, kt, [j for j in jobs if j[1] == kt]))
            jobs_all = [(n, j) for n, kt, js in tiles for j in js]
            jobs_end = [sum(1 for n, _ in jobs_all if n <= u) for u in range(len(units))]
            first_tile = [min(x for x, t in enumerate(tiles) if t[0] == u) for u in range(len(units))]

            def diag_in(j, q0, q1):
                return q0 <= j[1] < q1

            def pieces(n, j):
                q0, q1 = units[n][2], units[n][3]
                d = diag_in(j, q0, q1)
                return int(d) + int(j[3] - j[2] > int(d))
            wjob, wcount, pcount, jfirst = [], {}, [], []
            w = 0
            for n, j in jobs_all:
                w += pieces(n, j)
                wjob.append(w)
                wcount[n] = w
            done = 0
            for n, kt, js in tiles:
                jfirst.append(done)
                done += len(js)
                pcount.append(done)

            def second(x):
                return x == first_tile[tiles[x][0]] + 1
            last_job = [[[j for j in unit[5] if j[0] == i][-1] for i in range(2)] for unit in units]

            with nc.Block() as block:
                @block.tensor
                def _(pe):
                    def maxima(u):
                        blk, h, q0, q1, s, jobs = units[u]
                        w = (q1 - q0) * P
                        for i in range(2):
                            pe.wait_ge(diag, 2 * u + i + 1)
                            if u >= 1 and i == 0:
                                pe.wait_ge(nkept, 2 * u)
                                pe.wait_ge(masked, 2 * u)
                            nc.tensor.matmul(bank(i, w), ones[:, :], dg[i][:, 0:w], start=True, stop=True).then_inc(neg, 1)

                    def scores(x):
                        u, kt, js = tiles[x]
                        blk, h, q0, q1, s, jobs = units[u]
                        if x >= 4:
                            pe.wait_ge(product, pcount[x - 4])
                        lo, hi = min(j[2] for j in js), max(j[3] for j in js)
                        nc.tensor.matmul(bank(2 + x % 4, (hi - lo) * P, (lo - q0) * P), kz[h][:, kt * P:(kt + 1) * P],
                                         qkT[:, h // 2, lo * P:hi * P], start=True, stop=True).then_inc(scored, 1)

                    def values(x):
                        u, kt, js = tiles[x]
                        blk, h, q0, q1, s, jobs = units[u]
                        for y, j in enumerate(js):
                            n = jfirst[x] + y
                            pe.wait_ge(product, n + 1)
                            if x == first_tile[u] and u >= 1 and y == 0:
                                pe.wait_ge(taken, u)
                            i = j[0]
                            first_job = jobs.index(j) == min(jobs.index(k) for k in jobs if k[0] == i)
                            for q in range(j[2], j[3]):
                                mm = nc.tensor.matmul(bank(6 + i, HD + 1, (q - q0) * (HD + 1)), pr[n % RING][:, (q - q0) * P:(q - q0 + 1) * P],
                                                      v[:, kt, h, :], start=(first_job and q == j[2]), stop=(j is last_job[u][i] and q == j[3] - 1),
                                                      skip_group_check=True)
                            mm.then_inc(used, 1)

                    LEAD = 2
                    maxima(0)
                    for x in range(len(tiles) + LEAD):
                        if x < len(tiles):
                            scores(x)
                            if second(x) and tiles[x][0] + 1 < len(units):
                                maxima(tiles[x][0] + 1)
                        if x >= LEAD:
                            values(x - LEAD)
                    for t in range(nq):
                        pe.wait_ge(ready, t // 4 + 1)
                        if t >= 2:
                            pe.wait_ge(kept, t - 1)
                        else:
                            pe.wait_ge(product, len(jobs_all))
                        for c in range(2):
                            mm = nc.tensor.transpose(bank(2 + t % 2, P, c * P), hs[:, t, c * P:(c + 1) * P], ident)
                        mm.then_inc(turned, 1)

                @block.scalar
                def _(act):
                    def keep_maxima(u):
                        w = (units[u][3] - units[u][2]) * P
                        for i in range(2):
                            act.wait_ge(masked, 2 * u + i + 1)
                            if u >= 2:
                                act.wait_ge(weighed, wcount[u - 2])
                            nc.scalar.activation(nms[u % 2][:, i, 0:w], bank(i, w), ACT.Copy).then_inc(nkept, 1)

                    keep_maxima(0)
                    n = 0
                    for x, (u, kt, js) in enumerate(tiles):
                        blk, h, q0, q1, s, jobs = units[u]
                        for j in js:
                            i = j[0]
                            act.wait_ge(nkept, 2 * u + i + 1)
                            if n >= WRING:
                                act.wait_ge(product, n - WRING + 1)
                            ak = A[:, i, kt, h:h + 1]
                            lo, hi = (j[2] - q0) * P, (j[3] - q0) * P
                            if diag_in(j, q0, q1):
                                dlo = (kt - q0) * P
                                nc.scalar.activation(wt[n % WRING][:, dlo:dlo + P], nmd[u % 2][:, i, dlo:dlo + P], ACT.Exp, bias=ak).then_inc(weighed, 1)
                                if i == 0:
                                    lo = dlo + P
                                else:
                                    hi = dlo
                            if lo < hi:
                                nc.scalar.activation(wt[n % WRING][:, lo:hi], nms[u % 2][:, i, lo:hi], ACT.Exp, bias=ak).then_inc(weighed, 1)
                            n += 1
                        if second(x) and u + 1 < len(units):
                            keep_maxima(u + 1)
                    for t in range(nq):
                        act.wait_ge(turned, t + 1)
                        nc.scalar.activation(yT[:, 4:6, t * P:(t + 1) * P], bank(2 + t % 2, 2 * P).rearrange("p (c t) -> p c t", c=2), ACT.Copy).then_inc(kept, 1)

                @block.vector
                def _(dve):
                    step = Chain(dve, step_s)

                    def diagonals(u):
                        blk, h, q0, q1, s, jobs = units[u]
                        nt = q1 - q0
                        for i in range(2):
                            if u >= 1:
                                dve.wait_ge(neg, 2 * u)
                            nc.vector.scalar_tensor_tensor(out=dg[i][:, 0:nt * P].rearrange("p (t m) -> p t m", t=nt),
                                                           in0=ident.unsqueeze(1).broadcast_to([P, nt, P]), scalar=-1.0,
                                                           in1=M[:, i, q0:q1, h:h + 1].broadcast_to([P, nt, P]),
                                                           op0=ALU.mult, op1=ALU.mult).then_inc(diag, 1)

                    def mask(u):
                        blk, h, q0, q1, s, jobs = units[u]
                        nt = q1 - q0
                        for i in range(2):
                            dve.wait_ge(neg, 2 * u + i + 1)
                            if u >= 2:
                                dve.wait_ge(weighed, wcount[u - 2])
                            m = cst[:, (C_MASK0, C_MASK1)[i]:(C_MASK0, C_MASK1)[i] + P].unsqueeze(1).broadcast_to([P, nt, P])
                            nc.vector.tensor_tensor(nmd[u % 2][:, i, 0:nt * P].rearrange("p (t m) -> p t m", t=nt),
                                                    bank(i, nt * P).rearrange("p (t m) -> p t m", t=nt), m, ALU.add).then_inc(masked, 1)

                    def take(u):
                        blk, h, q0, q1, s, jobs = units[u]
                        nt = q1 - q0
                        dve.wait_ge(used, jobs_end[u])
                        pv = [bank(6 + i, nt * (HD + 1)).rearrange("p (t d) -> p t d", t=nt) for i in range(2)]
                        for i in range(2):
                            step.then(nc.vector.tensor_tensor(den[:, i, 0:nt].unsqueeze(2), pv[i][:, :, HD:HD + 1], EM[:, i, q0:q1, h:h + 1], ALU.max))
                        step.wait()
                        for i in range(2):
                            step.then(nc.vector.scalar_tensor_tensor(out=den[:, i, 0:nt].unsqueeze(2), in0=pv[i][:, :, HD:HD + 1], scalar=-1.0,
                                                                     in1=den[:, i, 0:nt].unsqueeze(2), op0=ALU.mult, op1=ALU.max))
                        step.wait()
                        step.then(nc.vector.reciprocal(den[:, :, 0:nt], den[:, :, 0:nt]))
                        step.wait()
                        for i in range(2):
                            step.then(nc.vector.tensor_tensor(ob[:, i, 0:nt, :], pv[i][:, :, 0:HD],
                                                              den[:, i, 0:nt].unsqueeze(2).broadcast_to([P, nt, HD]), ALU.mult))
                        step.wait()
                        nc.vector.tensor_tensor(hs[:, q0:q1, h * HD:(h + 1) * HD], ob[:, 0, 0:nt, :], ob[:, 1, 0:nt, :], ALU.add).then_inc(taken, 1)

                    def finish(blk):
                        q0, nt = BLOCKS[blk][0] // P, BLOCKS[blk][1] // P
                        hb = hs[:, q0:q0 + nt, :]
                        hv = hb.rearrange("p t (h d) -> p (t h) d", d=HD)
                        sv = ss[:, q0:q0 + nt, :].rearrange("p t h -> p (t h)")
                        dve.wait_ge(taken, H * (blk + 1))
                        step.then(nc.vector.tensor_tensor(hsq[:, 0:nt * GW], hb.rearrange("p t n -> p (t n)"), hb.rearrange("p t n -> p (t n)"), ALU.mult))
                        step.wait()
                        nc.vector.tensor_reduce(sv, hsq[:, 0:nt * GW].rearrange("p (h d) -> p h d", d=HD), AX, ALU.add).then_inc(sums, 1)
                        dve.wait_ge(inv, blk + 1)
                        step.then(nc.vector.tensor_tensor(hv, hv, sv.unsqueeze(2).broadcast_to([P, nt * H, HD]), ALU.mult))
                        step.wait()
                        step.then(nc.vector.tensor_tensor(hv, hv, R["mlstm_g_out"].unsqueeze(1).broadcast_to([P, nt * H, HD]), ALU.mult))
                        step.wait()
                        for t in range(q0, q0 + nt):
                            h2 = hs[:, t, :].rearrange("p (c d) -> p c d", c=2)
                            ins = nc.vector.tensor_tensor(h2, h2, so(t), ALU.mult)
                            if t < q0 + nt - 1:
                                step.then(ins)
                            else:
                                step.wait()
                                ins.then_inc(ready, 1)

                    diagonals(0)
                    mask(0)
                    n = 0
                    for x, (u, kt, js) in enumerate(tiles):
                        blk, h, q0, q1, s, jobs = units[u]
                        for j in js:
                            lo, hi = (j[2] - q0) * P, (j[3] - q0) * P
                            dve.wait_ge(scored, x + 1)
                            dve.wait_ge(weighed, wjob[n])
                            if n >= RING:
                                dve.wait_ge(used, n - RING + 1)
                            nc.vector.scalar_tensor_tensor(out=pr[n % RING][:, lo:hi], in0=bank(2 + x % 4, hi - lo, lo), scalar=HD ** -0.5,
                                                           in1=wt[n % WRING][:, lo:hi], op0=ALU.mult, op1=ALU.mult).then_inc(product, 1)
                            n += 1
                        if x == first_tile[u]:
                            if u + 1 < len(units):
                                diagonals(u + 1)
                        if second(x):
                            if u + 1 < len(units):
                                mask(u + 1)
                            if u >= 1:
                                take(u - 1)
                                if u % H == 0:
                                    finish(u // H - 1)
                    take(len(units) - 1)
                    finish(nblk - 1)

                @block.gpsimd
                def _(pool):
                    for blk in range(nblk):
                        q0, nt = BLOCKS[blk][0] // P, BLOCKS[blk][1] // P
                        f = ss[:, q0:q0 + nt, :].rearrange("p t h -> p (t h)")
                        pool.wait_ge(sums, blk + 1)
                        nc.gpsimd.tensor_scalar(f, f, 1.0 / HD, EPS, ALU.mult, ALU.add).then_inc(pstep, 1)
                        pool.wait_ge(pstep, blk + 1)
                        nc.gpsimd.tensor_tensor(f, f, half[:, 0:nt * H], ALU.pow).then_inc(inv, 1)
    for l in range(DEPTH):
        need = l < DEPTH - 1
        mine = BLOCKS if need else BLOCKS[:2]
        modulation(l, xT)
        st = ExitStack()
        with st:
            yT = sb(f"yT{l}", [P, DC, T], st)
            h_stack = ExitStack()
            with h_stack:
                hT = sb(f"hT{l}", [P, DC, T], h_stack)
                w_ahead = sb(f"w_ahead{l}", [P, DC, 3, P], h_stack)
                norm(l, 0, BLOCKS, xT, (hT,), spill=(l == 0), meanwhile=fetch_qkv(l, "diff", 0, w_ahead))
                x_stack.close()
                clear_semaphores()
                mixers(l, yT, w_ahead, need)
            x_stack = ExitStack()
            xT = take_x(x_stack, f"x_mid{l}")
            project_out(l, mine, yT, xT)
        st = ExitStack()
        with st:
            hh, hl = sbr(f"h_high{l}", [P, DC, T], st), sbr(f"h_low{l}", [P, DC, T], st)
            norm(l, 1, mine, xT, (hh, hl), spill=True)
            x_stack.close()
            clear_semaphores()
            ffn(l, mine, hh, hl)
            clear_semaphores()
        x_stack = ExitStack()
        xT = take_x(x_stack, f"x_end{l}")
    leave(xT)
    x_stack.close()


_INS = ['x', 'c', 'ctx', 'c_ctx', 'w_mod', 'b_mod', 'g_norm1', 'g_norm2', 'w_in', 'w_out',
        'diff_g_q', 'diff_g_k', 'diff_lam', 'diff_g_out', 'mla_g_cq', 'mla_g_ckv', 'mla_w_uq', 'mla_w_ukv',
        'mla_g_q', 'mla_g_k', 'mlstm_w_conv', 'mlstm_b_i', 'mlstm_b_f', 'mlstm_g_out',
        'na_g_q', 'na_g_k', 'na_rpb', 'ffn_w_up', 'ffn_w_conv', 'ffn_w_down']


def kernel(**inputs):
    import concourse.bacc as bacc
    from concourse.bass_utils import run_bass_kernel_spmd

    nc = bacc.Bacc("TRN2", target_bir_lowering=False, num_devices=1)
    arrays, args = {}, {}
    for name in _INS:
        v = np.ascontiguousarray(inputs[name])
        arrays[f"in_{name}"] = v
        args[name] = nc.dram_tensor(f"in_{name}", v.shape, F32, kind="ExternalInput").ap()
    arrays["in_consts"] = shape_constants()
    args["consts"] = nc.dram_tensor("in_consts", (P, C_N), F32, kind="ExternalInput").ap()
    out = nc.dram_tensor("out", (1, SEQ, D), F32, kind="ExternalOutput").ap()
    build(nc, args, out)
    r = run_bass_kernel_spmd(nc, [arrays], core_ids=[0])
    return r.results[0]["out"]
```
